# Optimizing a Trainium2 kernel written in Bass

```python
import jax, jax.numpy as jnp
from jax import lax
import numpy as np

D_MODEL = 2048
BATCH = 1
SEQ = 512
DEPTH = 1
DEC_BATCH = 8
DEC_SEQ = 1
PAST_LEN = 4096
PAGE_SIZE = 128

GROUP_WIDTH = D_MODEL // 4
SSD_WIDTH = GROUP_WIDTH
SSD_HEAD_DIM = 64
SSD_HEADS = SSD_WIDTH // SSD_HEAD_DIM
SSD_GROUPS = 2
SSD_STATE = 64
SSD_CONV = 4
SSD_CHUNK = 128
XBC_WIDTH = SSD_WIDTH + 2 * SSD_GROUPS * SSD_STATE
S5_WIDTH = GROUP_WIDTH
S5_CH = 16
S5_GROUPS = S5_WIDTH // S5_CH
S5_STATE = 64
SC_WIDTH = GROUP_WIDTH
SC_CONV = 3
POOL_WIDTH = GROUP_WIDTH
POOL_WINDOWS = (2, 4, 8, 16)
POOL_GROUP = POOL_WIDTH // len(POOL_WINDOWS)
POOL_HIST = max(POOL_WINDOWS) - 1
N_MEM = 256
XA_HEADS = 4
XA_HEAD_DIM = D_MODEL // XA_HEADS
D_FF = 4 * D_MODEL
EPS = 1e-6
IN_SPLIT_SIZES = (SSD_WIDTH, XBC_WIDTH, SSD_HEADS, S5_WIDTH, SC_WIDTH, SC_WIDTH, SC_WIDTH, POOL_WIDTH)
IN_WIDTH = sum(IN_SPLIT_SIZES)

kernel_name = 'hymba_ssd_s5_conv_pool_step'

def rmsnorm(x, g):
    xf = x.astype(jnp.float32)
    y = xf * lax.rsqrt(jnp.mean(xf * xf, axis=-1, keepdims=True) + EPS)
    return (y * g.astype(jnp.float32)).astype(x.dtype)

def split_cols(x, sizes):
    idx = np.cumsum(np.array(sizes))[:-1].tolist()
    return jnp.split(x, idx, axis=-1)

def causal_dwconv(full, w):
    ch = full.shape[-1]
    return lax.conv_general_dilated(full, w[:, None, :].astype(full.dtype), window_strides=(1,), padding='VALID',
                                    dimension_numbers=('NWC', 'WIO', 'NWC'), feature_group_count=ch)

def ssd_scan(xh, dt, a, bm, cm, h0):
    b, t, nh, hd = xh.shape
    ln = SSD_CHUNK if t % SSD_CHUNK == 0 else t
    nc = t // ln

    def chunks(v):
        return v.reshape((b, nc, ln) + v.shape[2:])

    xc, dtc, bc, cc = chunks(xh), chunks(dt), chunks(bm), chunks(cm)
    acum = jnp.cumsum(dtc * a, axis=2)
    causal = jnp.tril(jnp.ones((ln, ln), dtype=bool))[None, None, :, :, None]
    seg = acum[:, :, :, None, :] - acum[:, :, None, :, :]
    decay = jnp.exp(jnp.where(causal, seg, -jnp.inf))
    xdt = xc * dtc[..., None]
    scores = jnp.einsum('bclhn,bcshn->bclsh', cc, bc) * decay
    y_diag = jnp.einsum('bclsh,bcshp->bclhp', scores, xdt)
    to_end = jnp.exp(acum[:, :, -1:, :] - acum)
    chunk_states = jnp.einsum('bclhn,bclh,bclhp->bchpn', bc, to_end, xdt)
    chunk_decay = jnp.exp(acum[:, :, -1, :])

    def step(hc, inp):
        s_c, d_c = inp
        return hc * d_c[:, :, None, None] + s_c, hc

    h_last, h_prev = lax.scan(step, h0, (jnp.swapaxes(chunk_states, 0, 1), jnp.swapaxes(chunk_decay, 0, 1)))
    h_prev = jnp.swapaxes(h_prev, 0, 1)
    y_off = jnp.einsum('bclhn,bchpn,bclh->bclhp', cc, h_prev, jnp.exp(acum))
    return (y_diag + y_off).reshape(b, t, nh, hd), h_last

def _lin_combine(left, right):
    a_l, b_l = left
    a_r, b_r = right
    return a_r * a_l, a_r * b_l + b_r

def s5_mixer(u, h0_re, h0_im, p):
    f32 = jnp.float32
    b, t, _ = u.shape
    lam = lax.complex(p['s5_lam_re'].astype(f32), p['s5_lam_im'].astype(f32))
    delta = jnp.exp(p['s5_log_dt'].astype(f32))[:, None]
    abar = jnp.exp(lam * delta)
    bbar = ((abar - 1.0) / lam)[..., None] * lax.complex(p['s5_b_re'].astype(f32), p['s5_b_im'].astype(f32))
    cmat = lax.complex(p['s5_c_re'].astype(f32), p['s5_c_im'].astype(f32))
    ug = u.reshape(b, t, S5_GROUPS, S5_CH).astype(jnp.complex64)
    bu = jnp.einsum('gnk,btgk->btgn', bbar, ug)
    a_pow, hs = lax.associative_scan(_lin_combine, (jnp.broadcast_to(abar, bu.shape), bu), axis=1)
    hs = hs + a_pow * lax.complex(h0_re.astype(f32), h0_im.astype(f32))[:, None]
    y = jnp.real(jnp.einsum('gkn,btgn->btgk', cmat, hs)).reshape(b, t, S5_WIDTH) + p['s5_d'].astype(f32) * u
    y = jax.nn.gelu(y)
    y = y * jax.nn.sigmoid(y @ p['s5_w_glu'].astype(f32) + p['s5_b_glu'].astype(f32))
    h_end = hs[:, -1]
    return y, jnp.real(h_end), jnp.imag(h_end)

def pool_mixer(u, prev, start_pos, p):
    f32 = jnp.float32
    b, t, _ = u.shape
    full = jnp.concatenate([prev.astype(f32), u], axis=1)
    csum = jnp.concatenate([jnp.zeros((b, 1, POOL_WIDTH), f32), jnp.cumsum(full, axis=1)], axis=1)
    upto = csum[:, POOL_HIST + 1:]
    pos = start_pos + jnp.arange(t, dtype=jnp.int32)
    parts = []
    for g, w in enumerate(POOL_WINDOWS):
        cs = slice(g * POOL_GROUP, (g + 1) * POOL_GROUP)
        lo = csum[:, POOL_HIST + 1 - w: POOL_HIST + 1 - w + t, cs]
        cnt = jnp.minimum(w, pos + 1).astype(f32)[None, :, None]
        parts.append((upto[..., cs] - lo) / cnt - u[..., cs])
    pooled = jnp.stack(parts, axis=2)
    y = jnp.einsum('btgc,gcd->btgd', pooled, p['pool_w'].astype(f32)).reshape(b, t, POOL_WIDTH)
    return y * p['pool_scale'].astype(f32), full[:, -POOL_HIST:]

def memory_kv(mem, p):
    b, m, _ = mem.shape
    mn = rmsnorm(mem, p['norm_mem_g'])
    k = (mn @ p['w_k']).reshape(b, m, XA_HEADS, XA_HEAD_DIM)
    v = (mn @ p['w_v']).reshape(b, m, XA_HEADS, XA_HEAD_DIM)
    return k, v

def trunk_layer(h, mem_k, mem_v, st, start_pos, p):
    f32 = jnp.float32
    conv_prev, ssd_h0, s5_re0, s5_im0, sc_prev, pool_prev = st
    b, t, _ = h.shape
    xn = rmsnorm(h, p['norm_mix_g'])
    proj = (xn @ p['w_in']).astype(f32)
    z, xbc, dt_raw, u5, gate_b, gate_c, hv, upool = split_cols(proj, IN_SPLIT_SIZES)

    xbc_full = jnp.concatenate([conv_prev.astype(f32), xbc], axis=1)
    xbc_c = jax.nn.silu(causal_dwconv(xbc_full, p['ssd_conv_w'].astype(f32)) + p['ssd_conv_b'].astype(f32))
    xs, bm, cm = split_cols(xbc_c, (SSD_WIDTH, SSD_GROUPS * SSD_STATE, SSD_GROUPS * SSD_STATE))
    xs = xs.reshape(b, t, SSD_HEADS, SSD_HEAD_DIM)
    rep = SSD_HEADS // SSD_GROUPS
    bm = jnp.repeat(bm.reshape(b, t, SSD_GROUPS, SSD_STATE), rep, axis=2)
    cm = jnp.repeat(cm.reshape(b, t, SSD_GROUPS, SSD_STATE), rep, axis=2)
    dt = jax.nn.softplus(dt_raw + p['ssd_dt_bias'].astype(f32))
    a = -jnp.exp(p['ssd_a_log'].astype(f32))
    y_ssd, ssd_new = ssd_scan(xs, dt, a, bm, cm, ssd_h0.astype(f32))
    y_ssd = (y_ssd + p['ssd_d'].astype(f32)[:, None] * xs).reshape(b, t, SSD_WIDTH) * jax.nn.silu(z)

    y_s5, s5_re, s5_im = s5_mixer(u5, s5_re0, s5_im0, p)

    sc_full = jnp.concatenate([sc_prev.astype(f32), gate_c * hv], axis=1)
    y_sc = gate_b * causal_dwconv(sc_full, p['sc_conv_w'].astype(f32))

    y_pool, pool_new = pool_mixer(upool, pool_prev, start_pos, p)

    mix = jnp.concatenate([y_ssd, y_s5, y_sc, y_pool], axis=-1).reshape(b, t, 4, GROUP_WIDTH)
    mix = mix * lax.rsqrt(jnp.mean(mix * mix, axis=-1, keepdims=True) + EPS)
    mix = (mix * p['mix_out_g'].astype(f32).reshape(4, GROUP_WIDTH)).reshape(b, t, D_MODEL)
    h = h + mix.astype(h.dtype) @ p['w_out']

    q = (rmsnorm(h, p['norm_xa_g']) @ p['w_q']).reshape(b, t, XA_HEADS, XA_HEAD_DIM)
    s = jnp.einsum('bthd,bmhd->bhtm', q.astype(f32), mem_k.astype(f32)) * (XA_HEAD_DIM ** -0.5)
    prob = jax.nn.softmax(s, axis=-1)
    o = jnp.einsum('bhtm,bmhd->bthd', prob, mem_v.astype(f32)).reshape(b, t, D_MODEL)
    h = h + o.astype(h.dtype) @ p['w_o']

    xm = rmsnorm(h, p['norm_mlp_g'])
    h = h + jnp.square(jax.nn.relu(xm @ p['w_up'])) @ p['w_down']

    new_st = (xbc_full[:, -(SSD_CONV - 1):], ssd_new, s5_re, s5_im, sc_full[:, -(SC_CONV - 1):], pool_new)
    return h, new_st

def setup_inputs(seed: int = 0) -> dict:
    key = jax.random.key(seed)
    ks = iter(jax.random.split(key, 64))
    f32 = jnp.float32

    def nrm(shape, scale):
        return scale * jax.random.normal(next(ks), shape, f32)

    def gain(shape):
        return 1.0 + 0.02 * jax.random.normal(next(ks), shape, f32)

    def unif(shape, lo, hi):
        return jax.random.uniform(next(ks), shape, f32, minval=lo, maxval=hi)

    dt0 = jnp.exp(unif((DEPTH, SSD_HEADS), np.log(1e-3), np.log(1e-1)))
    lam_im0 = jnp.pi * jnp.arange(S5_STATE, dtype=f32)
    return {
        'x_prompt': nrm((BATCH, SEQ, D_MODEL), 1.0),
        'x_sample': nrm((DEC_BATCH, DEC_SEQ, D_MODEL), 1.0),
        'mem_prompt': nrm((BATCH, N_MEM, D_MODEL), 1.0),
        'state_ssd_conv': nrm((DEPTH, DEC_BATCH, SSD_CONV - 1, XBC_WIDTH), 1.0),
        'state_ssd': nrm((DEPTH, DEC_BATCH, SSD_HEADS, SSD_HEAD_DIM, SSD_STATE), 0.5),
        'state_s5_re': nrm((DEPTH, DEC_BATCH, S5_GROUPS, S5_STATE), 0.3),
        'state_s5_im': nrm((DEPTH, DEC_BATCH, S5_GROUPS, S5_STATE), 0.3),
        'state_sconv': nrm((DEPTH, DEC_BATCH, SC_CONV - 1, SC_WIDTH), 1.0),
        'state_pool': nrm((DEPTH, DEC_BATCH, POOL_HIST, POOL_WIDTH), 1.0),
        'cache_mem_k': nrm((DEPTH, DEC_BATCH, N_MEM, XA_HEADS, XA_HEAD_DIM), 1.0),
        'cache_mem_v': nrm((DEPTH, DEC_BATCH, N_MEM, XA_HEADS, XA_HEAD_DIM), 1.0),
        'norm_mix_g': gain((DEPTH, D_MODEL)),
        'w_in': nrm((DEPTH, D_MODEL, IN_WIDTH), D_MODEL ** -0.5),
        'ssd_conv_w': nrm((DEPTH, SSD_CONV, XBC_WIDTH), SSD_CONV ** -0.5),
        'ssd_conv_b': nrm((DEPTH, XBC_WIDTH), 0.02),
        'ssd_dt_bias': dt0 + jnp.log(-jnp.expm1(-dt0)),
        'ssd_a_log': jnp.log(unif((DEPTH, SSD_HEADS), 1.0, 16.0)),
        'ssd_d': gain((DEPTH, SSD_HEADS)),
        's5_lam_re': -0.5 + nrm((DEPTH, S5_GROUPS, S5_STATE), 0.01),
        's5_lam_im': lam_im0 + nrm((DEPTH, S5_GROUPS, S5_STATE), 0.01),
        's5_log_dt': unif((DEPTH, S5_GROUPS), np.log(1e-3), np.log(1e-1)),
        's5_b_re': nrm((DEPTH, S5_GROUPS, S5_STATE, S5_CH), (2 * S5_CH) ** -0.5),
        's5_b_im': nrm((DEPTH, S5_GROUPS, S5_STATE, S5_CH), (2 * S5_CH) ** -0.5),
        's5_c_re': nrm((DEPTH, S5_GROUPS, S5_CH, S5_STATE), S5_STATE ** -0.5),
        's5_c_im': nrm((DEPTH, S5_GROUPS, S5_CH, S5_STATE), S5_STATE ** -0.5),
        's5_d': nrm((DEPTH, S5_WIDTH), 1.0),
        's5_w_glu': nrm((DEPTH, S5_WIDTH, S5_WIDTH), S5_WIDTH ** -0.5),
        's5_b_glu': nrm((DEPTH, S5_WIDTH), 0.02),
        'sc_conv_w': nrm((DEPTH, SC_CONV, SC_WIDTH), SC_CONV ** -0.5),
        'pool_w': nrm((DEPTH, len(POOL_WINDOWS), POOL_GROUP, POOL_GROUP), POOL_GROUP ** -0.5),
        'pool_scale': 1.0 + nrm((DEPTH, POOL_WIDTH), 0.1),
        'mix_out_g': gain((DEPTH, D_MODEL)),
        'w_out': nrm((DEPTH, D_MODEL, D_MODEL), D_MODEL ** -0.5),
        'norm_xa_g': gain((DEPTH, D_MODEL)),
        'norm_mem_g': gain((DEPTH, D_MODEL)),
        'w_q': nrm((DEPTH, D_MODEL, D_MODEL), D_MODEL ** -0.5),
        'w_k': nrm((DEPTH, D_MODEL, D_MODEL), D_MODEL ** -0.5),
        'w_v': nrm((DEPTH, D_MODEL, D_MODEL), D_MODEL ** -0.5),
        'w_o': nrm((DEPTH, D_MODEL, D_MODEL), D_MODEL ** -0.5),
        'norm_mlp_g': gain((DEPTH, D_MODEL)),
        'w_up': nrm((DEPTH, D_MODEL, D_FF), D_MODEL ** -0.5),
        'w_down': nrm((DEPTH, D_FF, D_MODEL), D_FF ** -0.5),
        'final_norm_g': gain((D_MODEL,)),
    }

def reference(x_prompt, x_sample, mem_prompt, state_ssd_conv, state_ssd, state_s5_re, state_s5_im,
              state_sconv, state_pool, cache_mem_k, cache_mem_v, norm_mix_g, w_in, ssd_conv_w, ssd_conv_b,
              ssd_dt_bias, ssd_a_log, ssd_d, s5_lam_re, s5_lam_im, s5_log_dt, s5_b_re, s5_b_im, s5_c_re,
              s5_c_im, s5_d, s5_w_glu, s5_b_glu, sc_conv_w, pool_w, pool_scale, mix_out_g, w_out, norm_xa_g,
              norm_mem_g, w_q, w_k, w_v, w_o, norm_mlp_g, w_up, w_down, final_norm_g):
    f32 = jnp.float32
    stacked = dict(norm_mix_g=norm_mix_g, w_in=w_in, ssd_conv_w=ssd_conv_w, ssd_conv_b=ssd_conv_b,
                   ssd_dt_bias=ssd_dt_bias, ssd_a_log=ssd_a_log, ssd_d=ssd_d, s5_lam_re=s5_lam_re,
                   s5_lam_im=s5_lam_im, s5_log_dt=s5_log_dt, s5_b_re=s5_b_re, s5_b_im=s5_b_im,
                   s5_c_re=s5_c_re, s5_c_im=s5_c_im, s5_d=s5_d, s5_w_glu=s5_w_glu, s5_b_glu=s5_b_glu,
                   sc_conv_w=sc_conv_w, pool_w=pool_w, pool_scale=pool_scale, mix_out_g=mix_out_g,
                   w_out=w_out, norm_xa_g=norm_xa_g, norm_mem_g=norm_mem_g, w_q=w_q, w_k=w_k, w_v=w_v,
                   w_o=w_o, norm_mlp_g=norm_mlp_g, w_up=w_up, w_down=w_down)
    bp = x_prompt.shape[0]
    st_prompt = (jnp.zeros((bp, SSD_CONV - 1, XBC_WIDTH), f32),
                 jnp.zeros((bp, SSD_HEADS, SSD_HEAD_DIM, SSD_STATE), f32),
                 jnp.zeros((bp, S5_GROUPS, S5_STATE), f32),
                 jnp.zeros((bp, S5_GROUPS, S5_STATE), f32),
                 jnp.zeros((bp, SC_CONV - 1, SC_WIDTH), f32),
                 jnp.zeros((bp, POOL_HIST, POOL_WIDTH), f32))
    hp, hs = x_prompt, x_sample
    p_new, s_new, p_mk, p_mv = [], [], [], []
    for l in range(DEPTH):
        p = {name: arr[l] for name, arr in stacked.items()}
        mk, mv = memory_kv(mem_prompt, p)
        hp, st_p = trunk_layer(hp, mk, mv, st_prompt, 0, p)
        st_s_in = (state_ssd_conv[l], state_ssd[l], state_s5_re[l], state_s5_im[l], state_sconv[l], state_pool[l])
        hs, st_s = trunk_layer(hs, cache_mem_k[l], cache_mem_v[l], st_s_in, PAST_LEN, p)
        p_new.append(st_p)
        s_new.append(st_s)
        p_mk.append(mk)
        p_mv.append(mv)
    y_prompt = rmsnorm(hp, final_norm_g)
    y_sample = rmsnorm(hs, final_norm_g)
    p_ssd_conv, p_ssd, p_s5_re, p_s5_im, p_sconv, p_pool = [jnp.stack(c) for c in zip(*p_new)]
    s_ssd_conv, s_ssd, s_s5_re, s_s5_im, s_sconv, s_pool = [jnp.stack(c) for c in zip(*s_new)]
    p_mem_k = jnp.stack(p_mk)
    p_mem_v = jnp.stack(p_mv)
    return (y_prompt, y_sample, p_ssd_conv, p_ssd, p_s5_re, p_s5_im, p_sconv, p_pool, p_mem_k, p_mem_v,
            s_ssd_conv, s_ssd, s_s5_re, s_s5_im, s_sconv, s_pool)


_drawn_inputs = setup_inputs


def setup_inputs(seed=0):
    import zlib

    import numpy as np

    out = dict(_drawn_inputs(seed))
    spreads = {}
    factors = {'ssd_d': 8.0,
     's5_lam_re': 3.904,
     's5_b_glu': 8.0,
     'mix_out_g': 3.805,
     'norm_xa_g': 8.0,
     'norm_mem_g': 2.86,
     'norm_mlp_g': 3.692,
     'final_norm_g': 2.859}
    for name, (base, spread) in spreads.items():
        noise = np.random.default_rng([zlib.crc32(name.encode()), seed]).standard_normal(out[name].shape)
        drawn = base * np.exp(spread * noise) if base else spread * noise
        out[name] = __import__('jax').numpy.asarray(drawn.astype(out[name].dtype))
    for name, factor in factors.items():
        out[name] = (out[name] * factor).astype(out[name].dtype)
    return out
```

```python
from contextlib import ExitStack

import numpy as np

import concourse.bass as bass
from concourse import mybir
from concourse.alu_op_type import AluOpType as ALU

F32 = mybir.dt.float32
F32R = mybir.dt.float32r
ACT = mybir.ActivationFunctionType
AX = mybir.AxisListType

P = 128
D = 2048
KT = D // P
SEQ = 512
NS = 8
TOK = SEQ + NS
HALF = TOK // 2
NMEM = 256
GW = 512
GT = GW // P
DFF = 4 * D
EPS = 1e-6
NH = 8
HD = 64
CH = 128
NC = SEQ // CH
NST = 16
XAH = 4
XAD = D // XAH
SCALE = float(XAD) ** -0.5
POOL_W = (2, 4, 8, 16)
PH = 15

C_Z, C_XBC, C_DT, C_U5, C_B, C_C, C_HV, C_POOL = 0, 512, 1280, 1288, 1800, 2312, 2824, 3336
IN_W = 3848

T_IN, T_KV, T_OUT, T_Q, T_O, T_MLP = 0, 15, 31, 39, 47, 55
N_CHUNK = DFF // D
T_END = T_MLP + 16 * N_CHUNK
O_IN, O_KV, O_OUT, O_Q, O_O, O_MLP = 0, 30, 38, 54, 70, 86

PI2_A = 6.28125
PI2_B = float((np.float32(2 * np.pi - PI2_A).view(np.uint32) & np.uint32(0xFFFFE000)).view(np.float32))
PI2_C = float(2 * np.pi - PI2_A - PI2_B)
ROUND = 12582912.0
PI_IN = 3.1415925


S5_AT = [13 * st // 4 for st in range(16)]
NORM_ORDER = (1, 2, 3, 0)
OUT_ORDER = (*range(8, 16), *range(4, 8), *range(0, 4))


def constants():
    c = np.zeros((P, 1264), np.float32)
    c[:, 0:128] = np.eye(P)
    c[:, 128:256] = 1.0
    p = np.arange(P)
    c[:, 256:384] = p[:, None] <= p[None, :]
    c[:, 384] = (p // 16) % 2 == 0
    c[:, 385] = (p // 16) % 2 == 1
    c[:, 386] = p < 64
    c[:, 387] = p >= 64
    for g, w in enumerate(POOL_W):
        for b in range(NS):
            c[b * PH + PH - (w - 1):(b + 1) * PH, 400 + 8 * g + b] = 1.0
        c[:, 432 + 16 * g:448 + 16 * g] = 1.0 / np.minimum(w, np.arange(16) + 1.0)
    for j in range(4):
        for k in range(8):
            c[k, 512 + 128 * j:640 + 128 * j] = (k % 4 == j) & (p // 64 == k // 4)
    return c


class Steps:

    def __init__(self, eng, own):
        self.eng, self.own, self.n, self.loop_i, self.per = eng, own, {}, [], {}

    def __call__(self, ins, sem=None):
        sem = sem or self.own
        k = sem
        ins.then_inc(sem, 1)
        self.n[k] = self.n.get(k, 0) + 1
        at = self.n[k]
        for i, per in self.loop_i:
            at = i * per.get(k, 0) + at
        self.eng.wait_ge(sem, at)

    def enter(self, i, per):
        self.loop_i.append((i, {s: c for s, c in per}))

    def leave(self, turns):
        _, per = self.loop_i.pop()
        for k, c in per.items():
            self.n[k] = self.n.get(k, 0) + c * (turns - 1)


class Signals:
    pass


def build(nc, io, consts_ap, outs):
    xscr = nc.dram_tensor("xscr", [P, KT, TOK], F32, kind="Internal").ap()
    uscr = nc.dram_tensor("uscr", [IN_W, TOK], F32, kind="Internal").ap()
    zscr = nc.dram_tensor("zscr", [NS, 768], F32, kind="Internal").ap()
    dscr = nc.dram_tensor("dscr", [128], F32, kind="Internal").ap()
    yscr = nc.dram_tensor("yscr", [NH, NS, 64], F32, kind="Internal").ap()
    base = 1152
    R_H = base
    R_A = R_H + KT * TOK * 4
    R_B = R_A + 2 * KT * TOK * 4
    R_W = R_B + 2 * KT * TOK * 4
    R_S = R_W + 10 * 4096
    here = {"at": R_S}

    def at(name, shape, off, dt=F32):
        return nc.alloc_sbuf_tensor_at(name, shape, dt, offset=off)

    def small(name, shape, dt=F32):
        n = 4
        for s in shape[1:]:
            n *= s
        t = at(name, shape, here["at"], dt)
        here["at"] += (n + 31) // 32 * 32
        assert here["at"] <= 229344, here["at"]
        return t

    ctx = ExitStack()
    with ctx:
        def sem(name):
            return ctx.enter_context(nc.semaphore(name))

        h = at("h", [P, KT, TOK], R_H)
        xT = at("xT", [P, KT, TOK], R_H)
        y = at("y", [P, KT, TOK], R_H)
        LO = KT * TOK * 4
        xh = at("xh", [P, KT, TOK], R_A, F32R)
        xl = at("xl", [P, KT, TOK], R_A + LO, F32R)
        mixh = at("mixh", [P, KT, TOK], R_A, F32R)
        mixl = at("mixl", [P, KT, TOK], R_A + LO, F32R)
        ah = at("ah", [P, KT, TOK], R_B, F32R)
        al = at("al", [P, KT, TOK], R_B + LO, F32R)
        q = at("q", [P, KT, TOK], R_A)
        oh = at("oh", [P, KT, TOK], R_B, F32R)
        ol = at("ol", [P, KT, TOK], R_B + LO, F32R)
        mh = at("mh", [P, KT, TOK], R_A, F32R)
        ml = at("ml", [P, KT, TOK], R_A + LO, F32R)
        fh = at("fh", [P, KT, TOK], R_B, F32R)
        fl = at("fl", [P, KT, TOK], R_B + LO, F32R)
        raw = at("raw", [P, 2, 1024], R_W)
        whi = at("whi", [P, 4, 1024], R_W + 8192, F32R)
        wlo = at("wlo", [P, 4, 1024], R_W + 8192 + 16384, F32R)

        xnat = at("xnat", [P, 5, D], R_B)
        mnat = at("mnat", [P, 2, D], R_B + 40960)
        s5nat = at("s5nat", [NS, 2, D], R_H)
        cvnat = at("cvnat", [24, 768], R_H + 16640)
        scnat = at("scnat", [16, GW], R_H + 16640 + 3072)
        plnat = at("plnat", [NS * PH, GW], R_H + 16640 + 5120)
        memh = at("memh", [P, KT, NMEM], R_B, F32R)
        meml = at("meml", [P, KT, NMEM], R_B + 16384, F32R)

        bnat = at("bnat", [P, 2, NST, 16], R_B)
        cnat = at("cnat", [P, 2, 4, 64], R_B + 2048)
        bexp = at("bexp", [P, 2, NST, 2, 16], R_B + 4096)
        cexp = at("cexp", [P, 2, 4, 2, 64], R_B + 8192)
        sm = at("sm", [P, 24, NST], R_B + 12288)
        ang = at("ang", [P, 4, 9, NST], R_B + 12288 + 1536)
        btmp = at("btmp", [P, 2, NST, 16], R_B + 12288 + 4096)
        bT = at("bT", [P, 2, 4, P], R_H)
        cT = at("cT", [P, 2, 4, P], R_H + 4096)
        elo = at("elo", [P, 2, NST, 32], R_H + 23808)
        ehi = at("ehi", [P, 2, NST, 16], R_H + 27904)
        etmp = at("etmp", [P, 2, NST, 16], R_H + 29952)
        BU = R_B + 32768
        rot = [at(f"rot{i}", [P, 5, SEQ], BU) for i in range(1)][0]
        tab = at("tab", [P, 2, 2, SEQ], BU + 10240)
        stg = at("stg", [P, 2, TOK], BU + 18432)
        u5 = at("u5", [P, GT, TOK], BU + 24704)
        ptmp = at("ptmp", [P, SEQ], BU + 22592)

        kvst = at("kvst", [P, 2, 2, 512], R_A)
        xc = at("xc", [P, 6, TOK], R_A + 8192)
        dtw = at("dtw", [NH, 6, TOK], R_A + 20672)
        xb = at("xb", [P, 2, 528], R_A + 33152)
        tb = at("tb", [P, NC, P], R_A + 33152)
        smk = at("smk", [P, 2, NC, CH], R_A + 35200)
        scb = at("scb", [P, 2, 4, 524], R_A + 39296)
        xdt = at("xdt", [P, NC, GW], R_A + 39296)
        xde = at("xde", [P, GW], R_A + 47488)
        cj = at("cj", [P, 4, SEQ], R_A + 49536)
        sig = at("sig", [P, GT, TOK], R_A + 57728)
        ht = at("ht", [P, 32, 64], R_A + 57728)
        gm = at("gm", [P, 2, SEQ], BU)
        tm = at("tm", [P, 3, NC, NH], BU + 4096)
        decs = at("decs", [P, 4, NC], BU + 4480)
        r64 = at("r64", [P, 160], BU + 4544)
        s64 = at("s64", [P, 2], BU + 5184)
        y64 = at("y64", [P, 32], BU + 5216)
        sdt = at("sdt", [8, 16], BU + 5344)
        zs = at("zs", [P, 4, NS], BU + 5408)
        selG = at("selG", [8, 4, P], BU + 6080)
        pu = at("pu", [P, 2, PH + TOK + 1], BU + 8128)
        pt = at("pt", [P, 2, PH + TOK + 1], BU + 12416)
        pt2 = at("pt2", [P, 2, PH + TOK + 1], BU + 16704)
        plw = at("plw", [P, GT, P], BU + 20992)
        hst = at("hst", [P, NC + 1, GW], BU + 8128)
        pst = at("pst", [P, 4, 64], BU + 18368)
        zt = at("zt", [P, 2, TOK], BU + 21440)
        wglu = at("wglu", [P, GT, GW], BU + 25600)
        hs = at("hs", [P, 32, 64], BU + 25600)

        AT = R_A + LO
        kNh = at("kNh", [P, 2, XAD], AT)
        kTh = at("kTh", [P, 4, NMEM], AT + 4096)
        vNh = at("vNh", [P, 2, XAD], AT + 8192)
        pT = at("pT", [P, 2, SEQ], AT + 12288)
        piece = at("piece", [P, 4, 2, XAD], AT + 16384)
        ynat = at("ynat", [P, 5, D], R_A)

        idn = small("idn", [P, P])
        ones = small("ones", [P, P])
        causal = small("causal", [P, P])
        mks = small("mks", [P, 112])
        gains = small("gains", [P, 6, KT])
        cvw = small("cvw", [P, 6, 4])
        cvb = small("cvb", [P, 6])
        scw = small("scw", [P, 4, 3])
        c4 = small("c4", [P, 4, 4])
        dtb = small("dtb", [NH, 4])
        rB = small("rB", [P, TOK])
        ssq = small("ssq", [P, TOK])
        sqt = small("sqt", [P, TOK])
        upr = at("upr", [P, TOK], here["at"])
        dtr = small("dtr", [NH, TOK])
        dwt = small("dwt", [P, KT, NH])
        dwh = small("dwh", [P, KT, NH], F32R)
        dwl = small("dwl", [P, KT, NH], F32R)
        convS = small("convS", [P, 6, 24])
        scS = small("scS", [P, 4, 16])
        plS = small("plS", [P, 4, NS])
        h0 = small("h0", [P, 2, NST, NS])
        scn = small("scn", [P, 4, 10])
        s5o = small("s5o", [P, 2, NST, NS + 1])
        rmem = small("rmem", [P, 8])
        s5p = small("s5p", [P, 8, NST])
        smx = small("smx", [P, 16])
        hsq = at("hsq", [P, TOK], here["at"])
        pr = small("pr", [P, NMEM])
        prs = small("prs", [NS, NMEM])
        pTs = small("pTs", [P, 2, NS])
        ssc = small("ssc", [P, 2, NS])
        lin = ctx.enter_context(nc.psum_tensor("lin", [P, 4, 512], F32))
        aux = ctx.enter_context(nc.psum_tensor("aux", [P, 4, 512], F32))

        s = Signals()
        s.cst_in = sem("cst_in")
        s.gain_in = sem("gain_in")
        s.par_in = sem("par_in")
        s.x_in0 = sem("x_in0")
        s.x_in1 = sem("x_in1")
        s.x_in2 = sem("x_in2")
        s.x_in3 = sem("x_in3")
        s.x_in4 = sem("x_in4")
        s.mem_in = sem("mem_in")
        s.st_in = sem("st_in")
        s.s5_in = sem("s5_in")
        s.xs_st = sem("xs_st")
        s.raw0 = sem("raw0")
        s.raw1 = sem("raw1")
        s.w_hi = sem("w_hi")
        s.w_lo = sem("w_lo")
        s.pe_unit = sem("pe_unit")
        s.tile_free = sem("tile_free")
        s.x_tr = sem("x_tr")
        s.x_ev = sem("x_ev")
        s.split_hi = sem("split_hi")
        s.split_lo = sem("split_lo")
        s.sq_done = sem("sq_done")
        s.ss_done = sem("ss_done")
        s.stat_mm = sem("stat_mm")
        s.inv_done = sem("inv_done")
        s.r_ready = sem("r_ready")
        s.dt_hi = sem("dt_hi")
        s.dt_lo = sem("dt_lo")
        s.dt_mm = sem("dt_mm")
        s.dt_ev = sem("dt_ev")
        s.st_tr = sem("st_tr")
        s.st_ev = sem("st_ev")
        s.s5_tr = sem("s5_tr")
        s.s5_ev = sem("s5_ev")
        s.mem_tr = sem("mem_tr")
        s.mem_hi = sem("mem_hi")
        s.mem_lo = sem("mem_lo")
        s.mem_sq = sem("mem_sq")
        s.mem_inv = sem("mem_inv")
        s.mem_r = sem("mem_r")
        s.s5_act = sem("s5_act")
        s.s5_ask = sem("s5_ask")
        s.tab_rdy = sem("tab_rdy")
        s.s5_bu = sem("s5_bu")
        s.s5_rot = sem("s5_rot")
        s.s5_h = sem("s5_h")
        s.s5_c = sem("s5_c")
        s.s5_y = sem("s5_y")
        s.s5_fin = sem("s5_fin")
        s.pj0 = sem("pj0")
        s.pj1 = sem("pj1")
        s.kv0 = sem("kv0")
        s.kv1 = sem("kv1")
        s.glu_in = sem("glu_in")
        s.glu_act = sem("glu_act")
        s.glu_mm = sem("glu_mm")
        s.glu_sig = sem("glu_sig")
        s.glu_y = sem("glu_y")
        s.sc_done = sem("sc_done")
        s.pl_in = sem("pl_in")
        s.pl_mm = sem("pl_mm")
        s.pl_ev = sem("pl_ev")
        s.cv_in0 = sem("cv_in0")
        s.sc_in0 = sem("sc_in0")
        s.sc_in1 = sem("sc_in1")
        s.pu0 = sem("pu0")
        s.pu1 = sem("pu1")
        s.z_in0 = sem("z_in0")
        s.z_in1 = sem("z_in1")
        s.sel_in = sem("sel_in")
        s.cv_in1 = sem("cv_in1")
        s.cv_acc = sem("cv_acc")
        s.cv_act = sem("cv_act")
        s.dt_ask = sem("dt_ask")
        s.dt_act = sem("dt_act")
        s.dt_done = sem("dt_done")
        s.tm_tr = sem("tm_tr")
        s.tm_ev = sem("tm_ev")
        s.tb_tr = sem("tb_tr")
        s.tb_ev = sem("tb_ev")
        s.xt_tr = sem("xt_tr")
        s.xt_ev = sem("xt_ev")
        s.sc_mm = sem("sc_mm")
        s.sm_ev = sem("sm_ev")
        s.ea_mm = sem("ea_mm")
        s.ea_act = sem("ea_act")
        s.cj_ev = sem("cj_ev")
        s.cs_mm = sem("cs_mm")
        s.h_ev = sem("h_ev")
        s.z_use = sem("z_use")
        s.y_fin = sem("y_fin")
        s.mx_pool = sem("mx_pool")
        s.ss_out = sem("ss_out")
        s.mixn = sem("mixn")
        s.oh_hi = sem("oh_hi")
        s.oh_lo = sem("oh_lo")
        s.ac_mm = sem("ac_mm")
        s.g_pre = sem("g_pre")
        s.g_exp = sem("g_exp")
        s.g_ev = sem("g_ev")
        s.y_mm = sem("y_mm")
        s.y_ev = sem("y_ev")
        s.z_act = sem("z_act")
        s.ps_tr = sem("ps_tr")
        s.ps_ev = sem("ps_ev")
        s.ss_st = sem("ss_st")
        s.ss_in = sem("ss_in")
        s.ss_s = sem("ss_s")
        s.ss_y = sem("ss_y")
        s.ss_yst = sem("ss_yst")
        s.ss_yin = sem("ss_yin")
        s.out_st = sem("out_st")
        s.h_in = sem("h_in")
        s.kh_in = sem("kh_in")
        s.vh_in = sem("vh_in")
        s.kt_tr = sem("kt_tr")
        s.kt_ev = sem("kt_ev")
        s.sc2 = sem("sc2")
        s.p_ask = sem("p_ask")
        s.p_exp = sem("p_exp")
        s.p_ev = sem("p_ev")
        s.p_tr = sem("p_tr")
        s.pt_ev = sem("pt_ev")
        s.pv = sem("pv")
        s.o_ev = sem("o_ev")
        s.qb = sem("qb")
        s.ss_ev = sem("ss_ev")
        s.pc0 = sem("pc0")
        s.pc1 = sem("pc1")
        s.pc2 = sem("pc2")
        s.pc3 = sem("pc3")
        s.sp_tr = sem("sp_tr")
        s.sp_ask = sem("sp_ask")
        s.sp_exp = sem("sp_exp")
        s.sp_ev = sem("sp_ev")
        s.sp_tb = sem("sp_tb")
        s.sp_tev = sem("sp_tev")
        s.spv = sem("spv")
        s.so_ev = sem("so_ev")
        s.up_sq = sem("up_sq")
        s.hid_hi = sem("hid_hi")
        s.hid_lo = sem("hid_lo")
        s.f_ev = sem("f_ev")
        s.f_tr = sem("f_tr")
        s.f_nat = sem("f_nat")
        s.pe_own = sem("pe_own")
        s.act_own = sem("act_own")
        s.dve_own = sem("dve_own")
        s.pool_own = sem("pool_own")

        raw_rdy = (s.raw0, s.raw1)
        x_in = (s.x_in0, s.x_in1, s.x_in2, s.x_in3, s.x_in4)
        pj = (s.pj0, s.pj1)
        kv_out = (s.kv0, s.kv1)
        cv_in = (s.cv_in0, s.cv_in1)
        sc_in = (s.sc_in0, s.sc_in1)
        pu_in = (s.pu0, s.pu1)
        z_in = (s.z_in0, s.z_in1)
        pc_in = (s.pc0, s.pc1, s.pc2, s.pc3)

        def halves(t):
            return t.rearrange("p (a b) -> p a b", a=2)

        def flat(t):
            return t[:].rearrange("p k n -> p (k n)")

        def lin_tile(b):
            return lin[:, 2 * b:2 * b + 2, 0:HALF]

        def kp(w):
            return w.rearrange("(k p) n -> p k n", p=P)

        def in_row(t):
            return C_U5 + P * t if t < 20 else P * (t - 20)

        block = ctx.enter_context(nc.Block())

        @block.sync
        def _(sp):
            for i in range(4):
                sp.dma_start(xnat[:, i, :], io["x_prompt"][P * i:P * i + P, :]).then_inc(x_in[i], 16)
            sp.dma_start(xnat[0:NS, 4, :], io["x_sample"]).then_inc(x_in[4], 16)

            def load(T, slot, src, shape):
                if not (isinstance(T, int) and T == 0 and slot < 2):
                    sp.wait_ge(s.w_hi, 4 * T + (slot - 1))
                    sp.wait_ge(s.w_lo, 4 * T + (slot - 1))
                dst = raw[:, slot % 2, :].rearrange("p (k n) -> p k n", n=shape)
                sp.dma_start(dst, src).then_inc(raw_rdy[slot % 2], 16)

            def load_pair(T, w, col, k0=0, turned=0):
                for slot in range(4):
                    load(T, slot, kp(w)[:, bass.ds(k0 + 8 * ((slot + turned) % 2), 8), bass.ds(col + P * (slot // 2), P)], P)

            load_pair(0, io["w_in"], C_U5)
            for i in range(2):
                sp.dma_start(mnat[:, i, :], io["mem"][P * i:P * i + P, :]).then_inc(s.mem_in, 16)
            with sp.Fori(1, 10) as p:
                load_pair(p, io["w_in"], 256 * p + C_U5)
            with sp.Fori(0, 5) as p:
                load_pair(p + 10, io["w_in"], 256 * p)
            for m, w in enumerate(("w_v", "w_k")):
                with sp.Fori(0, 4) as b:
                    for u in range(8):
                        load(2 * b + (T_KV + 8 * m + u // 4), u % 4,
                             kp(io[w])[:, 2 * u:2 * u + 2, bass.ds(512 * b, 512)], 512)
            for p in range(8):
                load_pair(p + T_OUT, io["w_out"], 256 * p, 0, 1)

            def load_piece(hd, i):
                n = 16 * hd + i
                kv, b = i // NS, i % NS
                if n >= 4:
                    j = n - 4
                    if (j % 16) < NS:
                        sp.wait_ge(s.ss_ev, NS * (j // 16) + j % 16 + 1)
                    else:
                        sp.wait_ge(s.spv, NS * (j // 16) + j % 16 - NS + 1)
                else:
                    sp.wait_ge(s.split_lo, 32 + 16)
                src = io["cache_k" if kv == 0 else "cache_v"][b].rearrange("(m p) n -> p m n", p=P)
                sp.dma_start(piece[:, n % 4, :, :], src[:, :, XAD * hd:XAD * hd + XAD]).then_inc(pc_in[n % 4], 16)

            load_pair(T_Q, io["w_q"], 0)
            load_pair(T_Q + 1, io["w_q"], 256)
            for hd in range(XAH):
                for i in range(4):
                    load_piece(hd, i)
                if hd < XAH - 1:
                    load_pair(T_Q + 2 * hd + 2, io["w_q"], 512 * hd + 512)
                else:
                    load_pair(T_O, io["w_o"], 0)
                for i in range(4, 16):
                    load_piece(hd, i)
                if hd < XAH - 1:
                    load_pair(T_Q + 2 * hd + 3, io["w_q"], 512 * hd + 768)
            with sp.Fori(1, 8) as p:
                load_pair(p + T_O, io["w_o"], 256 * p)
            with sp.Fori(0, N_CHUNK) as c:
                with sp.Fori(0, 8) as p:
                    load_pair(16 * c + p + T_MLP, io["w_up"], 2048 * c + 256 * p)
                with sp.Fori(0, 8) as p:
                    load_pair(16 * c + p + (T_MLP + 8), io["w_down"], 256 * p, 16 * c)
            sp.wait_ge(s.out_st, 16 * N_OUT)

        @block.gpsimd
        def _(pool):
            step = Steps(pool, s.pool_own)

            def lo_unit(T, slot):
                pool.wait_ge(s.w_hi, 4 * T + slot + 1)
                pool.tensor_tensor(wlo[:, slot, :], raw[:, slot % 2, :], whi[:, slot, :].bitcast(F32),
                                   ALU.subtract).then_inc(s.w_lo, 1)

            def lo_turn(T):
                for slot in range(4):
                    lo_unit(T, slot)

            def table(st):
                if st == 0:
                    pool.wait_ge(s.s5_ev, 1)
                    pool.wait_ge(s.mem_lo, KT)
                if st >= 2:
                    pool.wait_ge(s.s5_h, st - 1)
                c, sn = (tab[:, st % 2, i, :].rearrange("p (m r) -> p m r", r=32) for i in range(2))
                t = ptmp[:, :].rearrange("p (m r) -> p m r", r=32)
                hc, hs = (ehi[:, i, st, :].unsqueeze(2).to_broadcast([P, 16, 32]) for i in range(2))
                lc, ls = (elo[:, i, st, :].unsqueeze(1).to_broadcast([P, 16, 32]) for i in range(2))
                step(pool.tensor_tensor(c, hc, lc, ALU.mult))
                step(pool.tensor_tensor(t, hs, ls, ALU.mult))
                step(pool.tensor_tensor(c, c, t, ALU.subtract))
                step(pool.tensor_tensor(sn, hs, lc, ALU.mult))
                step(pool.tensor_tensor(t, hc, ls, ALU.mult))
                step(pool.tensor_tensor(sn, sn, t, ALU.add), s.tab_rdy)

            for T in range(2):
                lo_turn(T)
            table(0)
            table(1)
            for n in range(52):
                lo_unit(2 + n // 4, n % 4)
                if n - 2 in S5_AT and S5_AT.index(n - 2) + 2 < NST:
                    table(S5_AT.index(n - 2) + 2)
            with pool.Fori(T_KV, T_END) as T:
                lo_turn(T)

        @block.scalar
        def _(act):
            ctx.enter_context(nc.allow_non_contiguous_dma(reason="small parameters and states"))
            step = Steps(act, s.act_own)

            def hi_units(first, last):
                for g in range(first, last):
                    slot, n = g % 4, 4 * T_KV + g
                    act.wait_ge(raw_rdy[slot % 2], 16 * (n // 2 + 1))
                    act.wait_ge(s.pe_unit, n - 3)
                    act.activation(whi[:, slot, :], raw[:, slot % 2, :], ACT.Copy).then_inc(s.w_hi, 1)

            def hi_turn(T):
                for slot in range(4):
                    act.wait_ge(raw_rdy[slot % 2], 32 * T + 16 * (slot // 2 + 1))
                    if not (isinstance(T, int) and T == 0):
                        act.wait_ge(s.pe_unit, 4 * T + (slot - 3))
                    act.activation(whi[:, slot, :], raw[:, slot % 2, :], ACT.Copy).then_inc(s.w_hi, 1)

            def dma(out, in_, sm):
                act.dma_start(out, in_).then_inc(sm, 16)

            dma(idn[:], consts_ap[:, 0:128], s.cst_in)
            dma(ones[:], consts_ap[:, 128:256], s.cst_in)
            dma(causal[:], consts_ap[:, 256:384], s.cst_in)
            dma(mks[:], consts_ap[:, 384:496], s.cst_in)
            for i, g in enumerate(("norm_mix_g", "mix_out_g", "norm_xa_g", "norm_mem_g", "norm_mlp_g", "final_norm_g")):
                dma(gains[:, i, :], io[g].rearrange("(k p) -> p k", p=P), s.gain_in)
            dma(dwt[:], kp(io["w_in"])[:, :, C_DT:C_DT + NH], s.par_in)
            for j in range(4):
                dma(cvw[:, :, j], io["ssd_conv_w"][j].rearrange("(k p) -> p k", p=P), s.par_in)
            dma(cvb[:], io["ssd_conv_b"].rearrange("(k p) -> p k", p=P), s.par_in)
            for j in range(3):
                dma(scw[:, :, j], io["sc_conv_w"][j].rearrange("(k p) -> p k", p=P), s.par_in)
            for i, g in enumerate(("s5_d", "s5_b_glu", "pool_scale")):
                dma(c4[:, i + 1, :], io[g].rearrange("(k p) -> p k", p=P), s.par_in)
            for hh in range(2):
                dma(c4[64 * hh:64 * hh + 64, 0, :],
                    io["ssd_d"].rearrange("(a i h) -> a h i", a=1, h=2)[:, hh, :].to_broadcast([64, 4]), s.par_in)
            dma(dtb[:, 0:1], io["ssd_dt_bias"].rearrange("(h a) -> h a", a=1), s.par_in)
            dma(dtb[:, 1:2], io["ssd_a_log"].rearrange("(h a) -> h a", a=1), s.par_in)
            for i, g in enumerate(("s5_lam_re", "s5_lam_im")):
                for hh in range(2):
                    dma(s5p[64 * hh:64 * hh + 64, 3 + i, :], io[g].rearrange("(i h) n -> h n i", h=2)[hh], s.par_in)
            for hh in range(2):
                dma(s5p[64 * hh:64 * hh + 64, 5, :],
                    io["s5_log_dt"].rearrange("(a i h) -> a h i", a=1, h=2)[:, hh, :].to_broadcast([64, NST]), s.par_in)

            def split_tile(n, k, src, g):
                act.activation(mov[n // KT][:, k, :], src, ACT.Copy, scale=gains[:, g, k:k + 1]).then_inc(s.split_hi, 1)
                if n >= 1:
                    act.wait_ge(s.ss_done, n)
                act.activation(sqt[:], src, ACT.Square).then_inc(s.sq_done, 1)

            mov = {0: xh}
            act.wait_ge(s.gain_in, 16 * 6)
            for k in range(KT):
                act.wait_ge(s.x_ev, k + 1)
                split_tile(k, k, xT[:, k, :], 0)
                if k == 7:
                    hi_turn(0)
            act.wait_ge(s.x_ev, KT)
            dma(xscr, xT[:], s.xs_st)

            def root(n):
                act.wait_ge(s.inv_done, n + 1)
                act.activation(rB[:], rB[:], ACT.Sqrt).then_inc(s.r_ready, 1)

            act.wait_ge(s.par_in, 16 * N_PAR)
            act.activation(dwh[:], dwt[:], ACT.Copy).then_inc(s.dt_hi, 1)
            root(0)
            act.wait_ge(s.x_tr, KT)
            for i, g in enumerate(("s5_b_re", "s5_b_im")):
                dma(bnat[:, i, :, :], io[g].rearrange("(i h) n k -> (h n) i k", h=2), s.s5_in)
            for i, g in enumerate(("s5_c_re", "s5_c_im")):
                dma(cnat[:, i, :, :], io[g].rearrange("(f g) k n -> (g k) f n", f=4), s.s5_in)
            act.wait_ge(s.xs_st, 16)
            act.wait_ge(s.ss_done, KT)
            act.wait_ge(s.split_lo, KT)
            for i, g in enumerate(("state_s5_re", "state_s5_im")):
                dma(s5nat[:, i, :], io[g], s.st_in)
            dma(cvnat[:], io["state_ssd_conv"], s.st_in)
            dma(scnat[:], io["state_sconv"], s.st_in)
            dma(plnat[:], io["state_pool"], s.st_in)
            hi_turn(1)
            act.wait_ge(s.s5_ask, 1)
            act.activation(s5p[:, 5, :], s5p[:, 5, :], ACT.Exp).then_inc(s.s5_act, 1)
            act.wait_ge(s.s5_ask, 2)
            act.activation(s5p[:, 0, :], sm[:, 0, :], ACT.Exp).then_inc(s.s5_act, 1)
            act.wait_ge(s.s5_ask, 3)
            act.activation(ang[:, 1, :, :], ang[:, 0, :, :], ACT.Sin).then_inc(s.s5_act, 1)
            act.activation(ang[:, 2, :, :], ang[:, 0, :, :], ACT.Sin, scale=0.5).then_inc(s.s5_act, 1)
            act.wait_ge(s.mem_in, 32)
            for i in range(2):
                step(act.activation(xnat[:, 4, :], mnat[:, i, :], ACT.Square, accum_out=rmem[:, i:i + 1]), s.mem_sq)
            act.wait_ge(s.mem_inv, 1)
            act.activation(rmem[:, 2:4], rmem[:, 2:4], ACT.Sqrt).then_inc(s.mem_r, 1)
            act.wait_ge(s.s5_ev, 1)
            for k in range(KT):
                act.wait_ge(s.mem_tr, k + 1)
                act.activation(memh[:, k, :], aux[:, k % 2, 0:NMEM], ACT.Copy,
                               scale=gains[:, 3, k:k + 1]).then_inc(s.mem_hi, 1)
            hi_turn(2)

            def store_u(T):
                for t in (2 * T, 2 * T + 1):
                    act.wait_ge(s.tile_free, t + 1)
                    dma(uscr[in_row(t):in_row(t) + P, :], stg[:, t % 2, :], pj[t % 2])

            def kv_store(b):
                act.wait_ge(s.tile_free, O_KV + b + 1)
                dst = outs["p_mem_v" if b < 4 else "p_mem_k"].rearrange("(m p) n -> p m n", p=P)
                dma(dst[:, :, 512 * (b % 4):512 * (b % 4) + 512], kvst[:, b % 2, :, :], kv_out[b % 2])

            for T in range(3, T_KV + 1):
                hi_turn(T)
                store_u(T - 1)
            for i in range(2):
                act.wait_ge(pj[i], 16 * 13)

            def load_conv(i):
                dma(xb[:, i % 2, 3:3 + TOK], uscr[C_XBC + P * i:C_XBC + P * i + P, :], cv_in[i % 2])

            def load_short(i):
                for j, c0 in enumerate((C_C, C_HV, C_B)):
                    o = 2 if j == 0 else 0
                    dma(scb[:, i % 2, j, o:o + TOK], uscr[c0 + P * i:c0 + P * i + P, :], sc_in[i % 2])

            def load_pool(i):
                dma(pu[:, i % 2, PH:PH + TOK], uscr[C_POOL + P * i:C_POOL + P * i + P, :], pu_in[i % 2])

            def load_z(i):
                dma(zt[:, i % 2, :], uscr[C_Z + P * i:C_Z + P * i + P, :], z_in[i % 2])

            load_conv(0)
            load_conv(1)
            load_short(0)
            load_short(1)
            act.wait_ge(s.s5_y, 4)
            for i in range(4):
                act.activation(y[:, 4 + i, :], y[:, 4 + i, :], ACT.Gelu_apprx_tanh).then_inc(s.glu_act, 1)
            act.wait_ge(s.s5_fin, 1)
            dma(wglu[:], kp(io["s5_w_glu"]), s.glu_in)
            dma(selG[:], consts_ap[0:8, 512:1024].rearrange("k (j m) -> k j m", j=4), s.sel_in)
            dma(plw[:], io["pool_w"].rearrange("g c d -> c g d"), s.pl_in)
            load_pool(0)
            load_pool(1)
            hi_units(4, 7)
            for i in range(6):
                act.wait_ge(s.cv_acc, i + 1)
                if i + 2 < 6:
                    load_conv(i + 2)
                act.activation(xc[:, i, :], xc[:, i, :], ACT.Silu).then_inc(s.cv_act, 1)
                if 1 <= i <= 4:
                    act.wait_ge(s.glu_mm, i)
                    act.activation(halves(sig[:, i - 1, :]), aux[:, 2 * ((i - 1) % 2):2 * ((i - 1) % 2) + 2, 0:HALF],
                                   ACT.Sigmoid, bias=c4[:, 2, i - 1:i]).then_inc(s.glu_sig, 1)
                hi_units(7 + i, 8 + i)
            act.wait_ge(s.cv_act, 6)
            for k in range(6):
                dma(zscr[:, P * k:P * k + P].rearrange("b p -> p b"), xc[:, k, SEQ:TOK], s.ss_st)
            act.wait_ge(s.dt_ask, 1)
            act.activation(dtw[:, 1, :], dtw[:, 1, :], ACT.Exp).then_inc(s.dt_act, 1)
            act.activation(dtb[:, 2:3], dtb[:, 1:2], ACT.Exp).then_inc(s.dt_act, 1)
            hi_units(13, 17)
            act.wait_ge(s.sc_done, 1)
            load_short(2)
            act.wait_ge(s.dt_ask, 2)
            for c in range(NC):
                act.activation(dtw[:, 4, CH * c:CH * c + CH], dtw[:, 3, CH * c:CH * c + CH], ACT.Exp, scale=-1.0,
                               bias=dtw[:, 3, CH * c + CH - 1:CH * c + CH]).then_inc(s.dt_act, 1)
            act.activation(sdt[:, 0:8], sdt[:, 0:8], ACT.Exp).then_inc(s.dt_act, 1)
            act.wait_ge(s.dt_act, 7)
            dma(dscr[0:64].rearrange("(h b) -> h b", h=8), sdt[:, 0:8], s.ss_st)
            act.wait_ge(s.sc_done, 2)
            load_short(3)
            act.wait_ge(s.dt_done, 1)
            dma(dscr[64:128].rearrange("(h b) -> h b", h=8), dtw[:, 2, SEQ:TOK], s.ss_st)
            kv_store(0)
            act.wait_ge(s.ss_st, 16 * 8)
            for f in range(2):
                rows = slice(64 * f, 64 * f + 64)
                for hd in range(NH):
                    dma(r64[64 * f + 8 * hd:64 * f + 8 * hd + 8, 0:32], zscr[:, 64 * hd + 32 * f:64 * hd + 32 * f + 32], s.ss_in)
                    for j in range(2):
                        b0 = 512 + 128 * j + 64 * (hd // 4)
                        dma(r64[64 * f + 8 * hd:64 * f + 8 * hd + 8, 32 + 64 * j:96 + 64 * j], zscr[:, b0:b0 + 64], s.ss_in)
                for j in range(2):
                    dma(s64[rows, j:j + 1], dscr[64 * j:64 * j + 64].rearrange("(p a) -> p a", a=1), s.ss_in)
                for hd in range(NH):
                    dma(hs[64 * f + 8 * hd:64 * f + 8 * hd + 8, :, :],
                        io["state_ssd"][:, hd, 2048 * f:2048 * f + 2048].rearrange("b (p n) -> b p n", n=64), s.ss_s)
            hi_units(17, 18)
            for j in range(4):
                act.wait_ge(s.ea_mm, j + 1)
                if j >= 2:
                    act.wait_ge(s.cj_ev, j - 1)
                act.activation(gm[:, j % 2, :], aux[:, 2 + j % 2, :], ACT.Exp).then_inc(s.ea_act, 1)
                if j >= 1:
                    hi_units(17 + j, 18 + j)
            hi_units(21, 23)
            kv_store(1)
            for i in (2, 3):
                act.wait_ge(s.mx_pool, i - 1)
                load_pool(i)
                hi_units(19 + 2 * i, 21 + 2 * i)
            hi_units(27, 30)
            act.wait_ge(s.pl_ev, 4)
            load_z(0)
            load_z(1)
            kv_store(2)

            def norm_squares(j, ready, count):
                act.wait_ge(ready, count)
                for i in range(4):
                    act.wait_ge(s.ss_done, KT + 4 * j + i)
                    act.activation(sqt[:], y[:, 4 * NORM_ORDER[j] + i, :], ACT.Square).then_inc(s.sq_done, 1)

            hi_units(30, 31)
            norm_squares(0, s.glu_y, 1)
            hi_units(31, 33)
            root(1)
            hi_units(33, 34)
            norm_squares(1, s.sc_done, 4)
            hi_units(34, 36)
            root(2)
            kv_store(3)
            hi_units(36, 47)
            norm_squares(2, s.pl_ev, 4)
            hi_units(47, 48)
            root(3)
            kv_store(4)
            hi_units(48, 49)
            act.wait_ge(s.ss_y, 1)
            for f in range(2):
                dma(yscr.rearrange("h b p -> (h b) p")[:, 32 * f:32 * f + 32], y64[64 * f:64 * f + 64, :], s.ss_yst)
            for f in range(2):
                for hd in range(NH):
                    dma(outs["s_ssd"][:, hd, 2048 * f:2048 * f + 2048].rearrange("b (p n) -> b p n", n=64),
                        hs[64 * f + 8 * hd:64 * f + 8 * hd + 8, :, :], s.ss_out)
            act.wait_ge(s.ss_yst, 32)
            for k in range(4):
                for hh in range(2):
                    dma(y[64 * hh:64 * hh + 64, k, SEQ:TOK], yscr[2 * k + hh].rearrange("b p -> p b"), s.ss_yin)
            for hd in range(NH):
                act.wait_ge(s.g_pre, hd + 1)
                act.activation(gm[:, hd % 2, :], gm[:, hd % 2, :], ACT.Exp).then_inc(s.g_exp, 1)
                if hd % 2 == 0:
                    i = hd // 2
                    if i >= 2:
                        act.wait_ge(s.z_use, i - 1)
                        load_z(i)
                    act.wait_ge(z_in[i % 2], 16 * (i // 2 + 1))
                    act.activation(zt[:, i % 2, :], zt[:, i % 2, :], ACT.Silu).then_inc(s.z_act, 1)
                hi_units(49 + 2 * hd, 51 + 2 * hd)
                if hd == 3:
                    kv_store(5)
            norm_squares(3, s.y_fin, 1)

            def mix_hi(k):
                act.activation(mixh[:, k, :], y[:, k, :], ACT.Copy).then_inc(s.split_hi, 1)

            for k in OUT_ORDER[0:4]:
                mix_hi(k)
            hi_units(65, 67)
            root(4)
            for k in OUT_ORDER[4:12]:
                mix_hi(k)
            hi_units(67, 68)
            kv_store(6)
            kv_store(7)
            for i in range(2):
                act.wait_ge(kv_out[i], 16 * 4)
            for i in range(4):
                act.wait_ge(s.mixn, 12 + i + 1)
                mix_hi(i)
            act.wait_ge(s.ps_ev, 1)
            dma(outs["p_ssd"].rearrange("(i q) n -> q i n", q=P), pst[:], s.ss_out)
            act.wait_ge(s.split_lo, 2 * KT)
            dma(h[:], xscr, s.h_in)
            act.wait_ge(s.ss_out, 16 * 17)

            def residual_pair(m, n, t, mo, g):
                for i in range(2):
                    act.wait_ge(s.tile_free, t + (i + 1))
                    act.wait_ge(s.ss_done, n + i)
                    src = flat(h)[:, bass.ds(TOK * (m + i), TOK)]
                    act.activation(flat(mo)[:, bass.ds(TOK * (m + i), TOK)], src, ACT.Copy,
                                   scale=gains[:, g, bass.ds(m + i, 1)]).then_inc(s.split_hi, 1)
                    act.activation(sqt[:], src, ACT.Square).then_inc(s.sq_done, 1)

            with act.Fori(0, 8) as p:
                hi_turn(p + (T_OUT + 1))
                residual_pair(2 * p, 2 * p + 2 * KT, 2 * p + O_OUT, ah, 2)
            root(5)
            hi_turn(T_Q + 1)
            def store_states(part):
                if part == 0:
                    for i in range(3):
                        dma(outs["p_ssd_conv"][i:i + 1, :],
                            uscr[C_XBC:C_XBC + 768, SEQ - 3 + i:SEQ - 2 + i].rearrange("f a -> a f"), s.out_st)
                    for b in range(NS):
                        dma(outs["s_ssd_conv"][3 * b + 2:3 * b + 3, :],
                            uscr[C_XBC:C_XBC + 768, SEQ + b:SEQ + b + 1].rearrange("f a -> a f"), s.out_st)
                        dma(outs["s_ssd_conv"][3 * b:3 * b + 2, :], io["state_ssd_conv"][3 * b + 1:3 * b + 3, :], s.out_st)
                elif part == 1:
                    for b in range(NS):
                        dma(outs["s_pool"][PH * b + PH - 1:PH * b + PH, :],
                            uscr[C_POOL:C_POOL + GW, SEQ + b:SEQ + b + 1].rearrange("f a -> a f"), s.out_st)
                        dma(outs["s_pool"][PH * b:PH * b + PH - 1, :], io["state_pool"][PH * b + 1:PH * b + PH, :], s.out_st)
                    for i in range(PH):
                        dma(outs["p_pool"][i:i + 1, :],
                            uscr[C_POOL:C_POOL + GW, SEQ - PH + i:SEQ - PH + i + 1].rearrange("f a -> a f"), s.out_st)
                elif part == 2:
                    for i, n in enumerate(("s5_re", "s5_im")):
                        for hh in range(2):
                            for j in range(NS + 1):
                                dst = outs["p_" + n][:, :] if j == NS else outs["s_" + n][32 * j:32 * j + 32, :]
                                dma(dst.rearrange("(i h) n -> h n i", h=2)[hh], s5o[64 * hh:64 * hh + 64, i, :, j], s.out_st)
                else:
                    for j in range(10):
                        dst = outs["p_sconv"][j:j + 1, :] if j < 2 else outs["s_sconv"][2 * j - 3:2 * j - 2, :]
                        dma(dst.rearrange("a (k p) -> p k a", p=P), scn[:, :, j:j + 1], s.out_st)
                    for b in range(NS):
                        dma(outs["s_sconv"][2 * b:2 * b + 1, :], io["state_sconv"][2 * b + 1:2 * b + 2, :], s.out_st)

            for hd in range(XAH):
                if hd >= 1:
                    hi_turn(T_Q + 2 * hd + 1)
                    act.wait_ge(s.so_ev, hd)
                if hd == 0:
                    act.wait_ge(s.tile_free, O_Q)
                for k_or_v, (dst, got) in enumerate(((kNh, s.kh_in), (vNh, s.vh_in))):
                    src = outs["p_mem_v" if k_or_v else "p_mem_k"].rearrange("(m p) n -> p m n", p=P)
                    if hd == 0 and k_or_v == 0:
                        for i in range(2):
                            act.wait_ge(kv_out[i], 16 * 4)
                    dma(dst[:], src[:, :, XAD * hd:XAD * hd + XAD], got)
                hi_turn(T_Q + 2 * hd + 2)
                for tt in range(4):
                    n = 4 * hd + tt
                    act.wait_ge(s.p_ask, n + 1)
                    act.activation(pr[:], lin[:, tt, 0:NMEM], ACT.Exp, scale=SCALE,
                                   bias=smx[:, 1:2], accum_out=smx[:, 2:3]).then_inc(s.p_exp, 1)
                act.wait_ge(s.sp_ask, hd + 1)
                act.activation(prs[:], aux[0:NS, 2, 0:NMEM], ACT.Exp, scale=SCALE, bias=smx[0:NS, 5:6],
                               accum_out=smx[0:NS, 6:7]).then_inc(s.sp_exp, 1)
                store_states(hd)
            for k in range(KT):
                act.wait_ge(s.so_ev, XAH)
                act.activation(oh[:, k, :], q[:, k, :], ACT.Copy).then_inc(s.oh_hi, 1)
            with act.Fori(0, 8) as p:
                hi_turn(p + (T_O + 1))
                residual_pair(2 * p, 2 * p + 3 * KT, 2 * p + O_O, mh, 4)
            root(6)

            def up_pair(c, p):
                hi_turn(16 * c + p + (T_MLP + 1))
                for i in range(2):
                    act.wait_ge(s.tile_free, 32 * c + 2 * p + (O_MLP + i + 1))
                    step(act.activation(hsq[:], upr[:], ACT.Square), s.up_sq)
                    act.activation(fh[:, bass.ds(2 * p + i, 1), :], hsq[:], ACT.Copy).then_inc(s.hid_hi, 1)

            with act.Fori(0, N_CHUNK - 1) as c:
                step.enter(c, [(s.up_sq, 16)])
                with act.Fori(0, 8) as p:
                    step.enter(p, [(s.up_sq, 2)])
                    up_pair(c, p)
                step.leave(8)
                with act.Fori(0, 8) as p:
                    hi_turn(16 * c + p + (T_MLP + 9))
            step.leave(N_CHUNK - 1)
            with act.Fori(0, 8) as p:
                step.enter(p, [(s.up_sq, 2)])
                up_pair(N_CHUNK - 1, p)
            step.leave(8)
            L = 16 * (N_CHUNK - 1)

            def last_pair(p):
                for i in range(2):
                    act.wait_ge(s.tile_free, 2 * p + (O_MLP + 32 * (N_CHUNK - 1) + 16 + i + 1))
                    act.wait_ge(s.ss_done, 2 * p + (4 * KT + i))
                    act.activation(sqt[:], flat(h)[:, bass.ds(TOK * (2 * p + i), TOK)], ACT.Square).then_inc(s.sq_done, 1)

            with act.Fori(0, 7) as p:
                hi_turn(p + (T_MLP + L + 9))
                last_pair(p)
            last_pair(7)
            root(7)
            for k in range(KT):
                act.wait_ge(s.f_tr, k + 1)
                step(act.activation(ynat[:, 0:4, P * k:P * k + P],
                                    aux[:, 2 * (k % 2), :].rearrange("p (t n) -> p t n", t=4), ACT.Copy), s.f_nat)
                step(act.activation(ynat[0:NS, 4, P * k:P * k + P], aux[0:NS, 2 * (k % 2) + 1, 0:P], ACT.Copy), s.f_nat)
                if k % 4 == 3:
                    c0 = P * (k - 3)
                    dma(outs["y_prompt"].rearrange("(t p) n -> p t n", p=P)[:, :, c0:c0 + 512],
                        ynat[:, 0:4, c0:c0 + 512], s.out_st)
                    dma(outs["y_sample"][:, c0:c0 + 512], ynat[0:NS, 4, c0:c0 + 512], s.out_st)

        @block.tensor
        def _(pe):
            step = Steps(pe, s.pe_own)

            def out_unit(T, i, half, t, hi, lo, ready, order):
                if half == 0 and not (isinstance(t, int) and t < 2):
                    pe.wait_ge(s.tile_free, t - 1)
                slot = 2 * i + half
                pe.wait_ge(s.w_lo, 4 * T + slot + 1)
                for n in range(8 * half, 8 * half + 8):
                    k = order[n]
                    if ready is not None and i == 0:
                        pe.wait_ge(ready[0], ready[1] + (n + 1))
                    wh = whi[:, slot, P * (k % 8):P * (k % 8) + P]
                    wl = wlo[:, slot, P * (k % 8):P * (k % 8) + P]
                    for part, (w, m) in enumerate(((wh, hi), (wh, lo), (wl, hi))):
                        for f in range(2):
                            mm = pe.matmul(lin[:, 2 * i + f, 0:HALF], w, m[:, k, HALF * f:HALF * f + HALF],
                                           start=(n == 0 and part == 0), stop=(n == KT - 1 and part == 2))
                mm.then_inc(s.pe_unit, 1)

            def out_tile(T, i, t, hi, lo, ready, order=range(KT)):
                for half in range(2):
                    out_unit(T, i, half, t, hi, lo, ready, order)

            def pair(T, t, hi, lo, ready=None, order=range(KT)):
                out_tile(T, 0, t, hi, lo, ready, order)
                out_tile(T, 1, t + 1, hi, lo, ready, order)

            def statistics(n, count, bank):
                pe.wait_ge(s.ss_done, count)
                for f in range(2):
                    mm = pe.matmul(aux[:, bank + f, 0:HALF], ones[:], ssq[:, HALF * f:HALF * f + HALF],
                                   start=True, stop=True)
                mm.then_inc(s.stat_mm, 1)

            pe.wait_ge(s.cst_in, 64)
            for x in x_in:
                pe.wait_ge(x, 16)
            for k in range(KT):
                if k >= 2:
                    pe.wait_ge(s.x_ev, k - 1)
                b = 2 * (k % 2)
                for i in range(4):
                    pe.transpose(aux[:, b, P * i:P * i + P], xnat[:, i, P * k:P * k + P], idn[:])
                pe.transpose(aux[:, b + 1, 0:NS], xnat[0:NS, 4, P * k:P * k + P], idn[0:NS, 0:NS]).then_inc(s.x_tr, 1)

            out_tile(0, 0, 0, xh, xl, (s.split_lo, 0))
            pe.wait_ge(s.x_ev, KT)
            statistics(0, KT, 2)
            out_tile(0, 1, 1, xh, xl, None)
            pe.wait_ge(s.dt_lo, 1)
            for kk in range(KT):
                for n, (w, m) in enumerate(((dwh, xh), (dwh, xl), (dwl, xh))):
                    for f in range(2):
                        mm = pe.matmul(aux[0:NH, f, 0:HALF], w[:, kk, :], m[:, kk, HALF * f:HALF * f + HALF],
                                       start=(kk == 0 and n == 0), stop=(kk == KT - 1 and n == 2))
            mm.then_inc(s.dt_mm, 1)
            pair(1, 2, xh, xl)

            pe.wait_ge(s.st_in, 80)
            pe.wait_ge(s.dt_ev, 1)
            for i in range(6):
                pe.transpose(aux[:, 0, 24 * i:24 * i + 24], cvnat[:, P * i:P * i + P], idn[0:24, 0:24])
            for i in range(4):
                pe.transpose(aux[:, 0, 144 + 16 * i:160 + 16 * i], scnat[:, P * i:P * i + P], idn[0:16, 0:16])
            for i in range(4):
                pe.matmul(aux[:, 0, 208 + 8 * i:216 + 8 * i], plnat[:, P * i:P * i + P],
                          mks[0:NS * PH, 16 + 8 * i:24 + 8 * i], start=True, stop=True)
            for c in range(2):
                for st in range(NST):
                    mm = pe.transpose(aux[:, 1, 128 * c + 8 * st:128 * c + 8 * st + 8],
                                      s5nat[:, c, P * st:P * st + P], idn[0:NS, 0:NS])
            mm.then_inc(s.st_tr, 1)
            pe.wait_ge(s.s5_ask, 4)
            pe.wait_ge(s.inv_done, 1)
            pe.wait_ge(s.st_ev, 1)
            for c in range(2):
                for f in range(4):
                    pe.transpose(aux[:, 2 + c, P * f:P * f + P], bexp[:, c, 4 * f:4 * f + 4, :, :].rearrange("p a b c -> p (a b c)"), idn[:])
                    mm = pe.transpose(aux[:, c, P * f:P * f + P], cexp[:, c, f, :, :].rearrange("p a b -> p (a b)"), idn[:])
            mm.then_inc(s.s5_tr, 1)
            pe.wait_ge(s.mem_in, 32)
            pe.wait_ge(s.s5_ev, 1)
            for k in range(KT):
                if k >= 2:
                    pe.wait_ge(s.mem_lo, k - 1)
                for i in range(2):
                    mm = pe.transpose(aux[:, k % 2, P * i:P * i + P], mnat[:, i, P * k:P * k + P], idn[:])
                mm.then_inc(s.mem_tr, 1)

            def s5_in(st):
                f, r = st // 4, 32 * (st % 4)
                if st == 0:
                    pe.wait_ge(s.mem_lo, KT)
                    pe.wait_ge(s.tile_free, 4)
                else:
                    pe.wait_ge(s.s5_rot, st)
                for c in range(2):
                    pe.matmul(aux[:, c, :], bT[r:r + 32, c, f, :], u5[r:r + 32, f, 0:SEQ], start=True, stop=True)
                    mm = pe.matmul(aux[:, 3, 8 * c:8 * c + 8], bT[r:r + 32, c, f, :], u5[r:r + 32, f, SEQ:TOK],
                                   start=True, stop=True)
                mm.then_inc(s.s5_bu, 1)

            def s5_out(st):
                f, r = st // 4, 32 * (st % 4)
                pe.wait_ge(s.s5_h, st + 1)
                for c in range(2):
                    pe.matmul(aux[r:r + 32, 2, :], cT[:, c, f, r:r + 32], rot[:, 3 + c, :], start=(c == 0), stop=(c == 1))
                for c in range(2):
                    mm = pe.matmul(aux[r:r + 32, 3, 32:40], cT[:, c, f, r:r + 32], s5o[:, c, st, 0:NS],
                                   start=(c == 0), stop=(c == 1))
                mm.then_inc(s.s5_c, 1)

            def kv_units(first, last):
                for g in range(first, last):
                    b, u = g // 8, g % 8
                    if u == 0:
                        pe.wait_ge(s.tile_free, O_KV + b - 1)
                    slot = u % 4
                    pe.wait_ge(s.w_lo, 4 * T_KV + g + 1)
                    for j in range(2):
                        kk = 2 * u + j
                        wh, wl = whi[:, slot, 512 * j:512 * j + 512], wlo[:, slot, 512 * j:512 * j + 512]
                        for m in range(2):
                            for n, (a, w) in enumerate(((memh, wh), (meml, wh), (memh, wl))):
                                mm = pe.matmul(lin[:, 2 * (b % 2) + m, :], a[:, kk, P * m:P * m + P], w,
                                               start=(kk == 0 and n == 0), stop=(kk == KT - 1 and n == 2))
                    mm.then_inc(s.pe_unit, 1)

            def attention(hd):
                f0 = 4 * hd
                pe.wait_ge(s.kh_in, 16 * hd + 16)
                if hd == 0:
                    pe.wait_ge(s.inv_done, 6)
                else:
                    pe.wait_ge(s.so_ev, hd)
                for d in range(4):
                    for m in range(2):
                        mm = pe.transpose(aux[:, d // 2, NMEM * (d % 2) + P * m:NMEM * (d % 2) + P * m + P],
                                          kNh[:, m, P * d:P * d + P], idn[:])
                mm.then_inc(s.kt_tr, 1)
                pe.wait_ge(s.kt_ev, hd + 1)
                pe.wait_ge(s.tile_free, O_Q + 4 * hd + 4)

                def prob_t(tt):
                    n = 4 * hd + tt
                    pe.wait_ge(s.p_ev, n + 1)
                    if n >= 1:
                        pe.wait_ge(s.pt_ev, n)
                    for m in range(2):
                        mm = pe.transpose(aux[:, 3, P * m:P * m + P], pr[:, P * m:P * m + P], idn[:])
                    mm.then_inc(s.p_tr, 1)

                for tt in range(4):
                    n = 4 * hd + tt
                    for d in range(4):
                        mm = pe.matmul(lin[:, tt, 0:NMEM], q[:, f0 + d, P * tt:P * tt + P],
                                       kTh[:, d, :], start=(d == 0), stop=(d == 3))
                    mm.then_inc(s.sc2, 1)
                    if tt >= 1:
                        prob_t(tt - 1)
                    for b in (2 * tt, 2 * tt + 1):
                        sample_query(hd, b)
                prob_t(3)
                pe.wait_ge(s.pt_ev, 4 * hd + 4)
                pe.wait_ge(s.vh_in, 16 * hd + 16)
                for d in range(4):
                    k = 4 * hd + d
                    if d < 2:
                        pe.wait_ge(s.ss_ev, 8 * hd + 8)
                    else:
                        pe.wait_ge(s.o_ev, k - 1)
                    for m in range(2):
                        mm = pe.matmul(aux[:, d % 2, :], vNh[:, m, P * d:P * d + P], pT[:, m, :],
                                       start=(m == 0), stop=(m == 1))
                    mm.then_inc(s.pv, 1)
                pe.wait_ge(s.p_exp, 4 * hd + 4)
                for m in range(2):
                    mm = pe.transpose(aux[0:NS, 2, P * m:P * m + P], ssc[:, m, :], idn[:])
                mm.then_inc(s.sp_tr, 1)
                pe.wait_ge(s.sp_ev, hd + 1)
                for m in range(2):
                    mm = pe.transpose(aux[:, 3, 256 + 8 * m:264 + 8 * m], prs[:, P * m:P * m + P], idn[0:NS, 0:NS])
                mm.then_inc(s.sp_tb, 1)
                pe.wait_ge(s.sp_tev, hd + 1)
                for b in range(NS):
                    n = 16 * hd + 8 + b
                    pe.wait_ge(pc_in[n % 4], 16 * (n // 4 + 1))
                    for d in range(4):
                        for m in range(2):
                            mm = pe.matmul(aux[:, 2, 256 + 8 * d + b:257 + 8 * d + b],
                                           piece[:, n % 4, m, P * d:P * d + P], pTs[:, m, b:b + 1],
                                           start=(m == 0), stop=(m == 1))
                    mm.then_inc(s.spv, 1)

            def sample_query(hd, b):
                n = 8 * hd + b
                if b >= 2:
                    pe.wait_ge(s.ss_ev, n - 1)
                elif hd > 0 or b == 0:
                    pass
                for d in range(4):
                    mm = pe.matmul(aux[:, b % 2, P * d:P * d + P],
                                   q[:, 4 * hd + d, SEQ + b:SEQ + b + 1].to_broadcast([P, P]), idn[:],
                                   start=True, stop=True)
                mm.then_inc(s.qb, 1)

            for n in range(52):
                if n in S5_AT:
                    st = S5_AT.index(n)
                    if st > 0:
                        s5_out(st - 1)
                        if st % 4 == 0:
                            pe.wait_ge(s.s5_y, st // 4)
                    s5_in(st)
                out_unit(2 + n // 4, n // 2 % 2, n % 2, 4 + n // 2, xh, xl, None, range(KT))
            s5_out(NST - 1)

            kv_units(0, 4)
            pe.wait_ge(s.glu_act, 4)
            pe.wait_ge(s.glu_in, 16)
            for i in range(4):
                if i == 2:
                    kv_units(4, 6)
                if i >= 2:
                    pe.wait_ge(s.glu_sig, i - 1)
                for f in range(2):
                    for k in range(4):
                        mm = pe.matmul(aux[:, 2 * (i % 2) + f, 0:HALF], wglu[:, k, P * i:P * i + P],
                                       y[:, 4 + k, HALF * f:HALF * f + HALF], start=(k == 0), stop=(k == 3))
                mm.then_inc(s.glu_mm, 1)
            kv_units(6, 14)
            pe.wait_ge(s.glu_sig, 4)
            pe.wait_ge(s.dt_done, 1)
            for c in range(NC):
                for j, row in enumerate((2, 5, 3)):
                    mm = pe.transpose(aux[:, 0, 32 * c + 8 * j:32 * c + 8 * j + 8],
                                      dtw[:, row, CH * c:CH * c + CH], idn[0:NH, 0:NH])
            mm.then_inc(s.tm_tr, 1)
            pe.wait_ge(s.cv_act, 6)
            for c in range(NC):
                mm = pe.transpose(aux[:, 1, P * c:P * c + P], xc[:, 4, CH * c:CH * c + CH], idn[:])
            mm.then_inc(s.tb_tr, 1)
            for g in range(2):
                r = 64 * g
                for c in range(NC):
                    mm = pe.matmul(aux[:, 2 + g, P * c:P * c + P], xc[r:r + 64, 4, CH * c:CH * c + CH],
                                   xc[r:r + 64, 5, CH * c:CH * c + CH], start=True, stop=True)
                mm.then_inc(s.sc_mm, 1)
            kv_units(14, 15)
            pe.wait_ge(s.sel_in, 16)
            for j in range(4):
                if j >= 2:
                    kv_units(13 + j, 14 + j)
                if j < 2:
                    pe.wait_ge(s.sm_ev, j + 1)
                else:
                    pe.wait_ge(s.ea_act, j - 1)
                pe.matmul(aux[:, 2 + j % 2, :], selG[:, j, :], dtw[:, 3, 0:SEQ], start=True, stop=True).then_inc(s.ea_mm, 1)
            kv_units(17, 20)
            pe.wait_ge(s.tm_ev, 1)
            pe.wait_ge(s.tb_ev, 1)
            pe.wait_ge(s.pl_in, 16)
            for i in range(4):
                pe.wait_ge(s.mx_pool, i + 1)
                if i >= 1:
                    pe.wait_ge(s.pl_ev, i)
                for f in range(2):
                    mm = pe.matmul(aux[:, f, 0:HALF], plw[:, i, :], halves(pt[:, i % 2, 0:TOK])[:, f, :],
                                   start=True, stop=True)
                mm.then_inc(s.pl_mm, 1)
                kv_units(20 + 2 * i, 22 + 2 * i)
            kv_units(28, 30)
            pe.wait_ge(s.ea_act, 4)
            statistics(1, KT + 4, 2)
            kv_units(30, 33)
            statistics(2, KT + 8, 2)
            kv_units(33, 36)
            for c in range(NC):
                if c == 0:
                    pe.wait_ge(s.pl_ev, 4)
                for i in range(4):
                    mm = pe.transpose(aux[:, 0, P * i:P * i + P], xc[:, i, CH * c:CH * c + CH], idn[:])
                mm.then_inc(s.xt_tr, 1)
                kv_units(36 + 2 * c, 37 + 2 * c)
                pe.wait_ge(s.xt_ev, c + 1)
                if c > 0:
                    pe.wait_ge(s.h_ev, c)
                pe.matmul(aux[:, 1, :], tb[:, c, :], xde[:], start=True, stop=True).then_inc(s.cs_mm, 1)
                kv_units(37 + 2 * c, 38 + 2 * c)
            statistics(3, KT + 12, 2)
            kv_units(44, 46)

            def running_sums(hd):
                if hd >= 2:
                    pe.wait_ge(s.g_pre, hd - 1)
                pe.matmul(aux[:, hd % 2, :], idn[0:NH, hd:hd + 1].to_broadcast([NH, P]), dtw[:, 3, 0:SEQ],
                          start=True, stop=True).then_inc(s.ac_mm, 1)

            pe.wait_ge(s.h_ev, 4)
            pe.wait_ge(s.cj_ev, 4)
            pe.wait_ge(s.inv_done, 4)
            running_sums(0)
            for hd in range(NH):
                j, i, hh = hd % 4, hd // 2, hd % 2
                if hd + 1 < NH:
                    running_sums(hd + 1)
                kv_units(46 + 2 * hd, 48 + 2 * hd)
                if hh == 0 and i >= 2:
                    pe.wait_ge(s.y_ev, i - 1)
                pe.wait_ge(s.g_ev, hd + 1)
                for c in range(NC):
                    o = aux[64 * hh:64 * hh + 64, 2 + i % 2, CH * c:CH * c + CH]
                    mm = pe.matmul(o, xdt[:, c, HD * hd:HD * hd + HD], gm[:, hd % 2, CH * c:CH * c + CH],
                                   start=True, stop=(c == 0))
                    if c > 0:
                        mm = pe.matmul(o, hst[:, c, HD * hd:HD * hd + HD], cj[:, j, CH * c:CH * c + CH],
                                       start=False, stop=True)
                mm.then_inc(s.y_mm, 1)
            pe.wait_ge(s.g_pre, 8)
            for i in range(4):
                mm = pe.transpose(aux[:, 0, P * i:P * i + P], hst[:, NC, P * i:P * i + P], idn[:])
            mm.then_inc(s.ps_tr, 1)
            kv_units(62, 64)
            pe.wait_ge(s.y_ev, 4)
            statistics(4, KT + 16, 2)

            pair(T_OUT, O_OUT, mixh, mixl, (s.split_lo, KT), OUT_ORDER)
            with pe.Fori(1, 8) as p:
                pair(p + T_OUT, 2 * p + O_OUT, mixh, mixl, None, OUT_ORDER)
            out_tile(T_Q, 0, O_Q, ah, al, (s.split_lo, 2 * KT))
            statistics(5, 3 * KT, 2)
            out_tile(T_Q, 1, O_Q + 1, ah, al, None)
            pair(T_Q + 1, O_Q + 2, ah, al)
            for hd in range(XAH):
                attention(hd)
                if hd < XAH - 1:
                    for j in (2, 3):
                        pair(T_Q + 2 * hd + j, O_Q + 4 * hd + 2 * j, ah, al)
            pair(T_O, O_O, oh, ol, (s.oh_lo, 0))
            with pe.Fori(1, 8) as p:
                pair(p + T_O, 2 * p + O_O, oh, ol)
            out_tile(T_MLP, 0, O_MLP, mh, ml, (s.split_lo, 3 * KT))
            statistics(6, 4 * KT, 2)
            out_tile(T_MLP, 1, O_MLP + 1, mh, ml, None)
            with pe.Fori(1, 8) as p:
                pair(p + T_MLP, 2 * p + O_MLP, mh, ml)
            with pe.Fori(0, 8) as p:
                pair(p + (T_MLP + 8), 2 * p + (O_MLP + 16), fh, fl, (s.hid_lo, 0))
            with pe.Fori(1, N_CHUNK) as c:
                with pe.Fori(0, 8) as p:
                    pair(16 * c + p + T_MLP, 32 * c + 2 * p + O_MLP, mh, ml)
                with pe.Fori(0, 8) as p:
                    pair(16 * c + p + (T_MLP + 8), 32 * c + 2 * p + (O_MLP + 16), fh, fl, (s.hid_lo, 16 * c))
            statistics(7, 5 * KT, 2)
            for k in range(KT):
                pe.wait_ge(s.f_ev, k + 1)
                if k >= 2:
                    pe.wait_ge(s.f_nat, 2 * (k - 1))
                b = 2 * (k % 2)
                for i in range(4):
                    pe.transpose(aux[:, b, P * i:P * i + P], h[:, k, P * i:P * i + P], idn[:])
                pe.transpose(aux[0:NS, b + 1, 0:P], h[:, k, SEQ:TOK], idn[:]).then_inc(s.f_tr, 1)

        @block.vector
        def _(v):
            step = Steps(v, s.dve_own)

            def tt(out, a, b, op, sm=None):
                step(v.tensor_tensor(out, a, b, op), sm)

            def ts(out, a, s1, s2=None, op0=ALU.mult, op1=None, sm=None):
                if op1 is None:
                    step(v.tensor_scalar(out, a, s1, None, op0), sm)
                else:
                    step(v.tensor_scalar(out, a, s1, s2, op0, op1), sm)

            def stt(out, a, sc, b, op0, op1, sm=None):
                step(v.scalar_tensor_tensor(out=out, in0=a, scalar=sc, in1=b, op0=op0, op1=op1), sm)

            def cp(out, a, sm=None):
                step(v.tensor_copy(out, a), sm)

            def add_square(n, first):
                v.wait_ge(s.sq_done, n + 1)
                if first:
                    cp(ssq[:], sqt[:], s.ss_done)
                else:
                    tt(ssq[:], ssq[:], sqt[:], ALU.add, s.ss_done)

            def inverse(n, width, bank):
                v.wait_ge(s.stat_mm, n + 1)
                ts(halves(rB[:]), aux[:, bank:bank + 2, 0:HALF], 1.0 / width, EPS, ALU.mult, ALU.add)
                step(v.reciprocal(rB[:], rB[:]), s.inv_done)

            v.wait_ge(s.gain_in, 16 * 6)
            for k in range(KT + 1):
                if k < KT:
                    v.wait_ge(s.x_tr, k + 1)
                    cp(xT[:, k, 0:SEQ], aux[:, 2 * (k % 2), :])
                    cp(xT[:, k, SEQ:TOK], aux[:, 2 * (k % 2) + 1, 0:NS], s.x_ev)
                if k >= 1:
                    v.wait_ge(s.split_hi, k)
                    stt(xl[:, k - 1, :], xT[:, k - 1, :], gains[:, 0, k - 1:k], xh[:, k - 1, :].bitcast(F32),
                        ALU.mult, ALU.subtract, s.split_lo)
                    add_square(k - 1, k == 1)
            inverse(0, D, 2)
            v.wait_ge(s.dt_hi, 1)
            tt(dwl[:], dwt[:], dwh[:].bitcast(F32), ALU.subtract, s.dt_lo)
            v.wait_ge(s.r_ready, 1)

            def evict_u(t):
                v.wait_ge(s.pe_unit, 2 * t + 2)
                if t < 4:
                    out = u5[:, t, :]
                else:
                    if t >= 6:
                        v.wait_ge(pj[t % 2], 16 * ((t - 4) // 2))
                    out = stg[:, t % 2, :]
                tt(halves(out), lin_tile(t % 2), halves(rB[:]), ALU.mult, s.tile_free)

            evict_u(0)
            evict_u(1)
            v.wait_ge(s.dt_mm, 1)
            tt(halves(dtr[:]), aux[0:NH, 0:2, 0:HALF], halves(rB[0:NH, :]), ALU.mult, s.dt_ev)

            v.wait_ge(s.par_in, 16 * N_PAR)
            v.wait_ge(s.xs_st, 16)
            step(v.tensor_copy(sm[:, 23, :], s5p[:, 5, :]), s.s5_ask)
            v.wait_ge(s.s5_act, 1)
            tt(sm[:, 0, :], s5p[:, 3, :], s5p[:, 5, :], ALU.mult, s.s5_ask)
            tt(sm[:, 1, :], s5p[:, 4, :], s5p[:, 5, :], ALU.mult)
            for k in range(9):
                ts(ang[:, 3, k, :], sm[:, 1, :], float(2 ** k))
            a0, a3 = ang[:, 0, :, :], ang[:, 3, :, :]
            ts(a0, a3, float(1 / (2 * np.pi)), ROUND, ALU.mult, ALU.add)
            ts(a0, a0, -ROUND, None, ALU.add)
            for c in (PI2_A, PI2_B, PI2_C):
                stt(a3, a0, -c, a3, ALU.mult, ALU.add)
            ts(a0, a3, PI_IN, -PI_IN, ALU.min, ALU.max, s.s5_ask)
            v.wait_ge(s.s5_act, 4)
            tt(ang[:, 2, :, :], ang[:, 2, :, :], ang[:, 2, :, :], ALU.mult)
            ts(ang[:, 2, :, :], ang[:, 2, :, :], -2.0, 1.0, ALU.mult, ALU.add)
            tt(s5p[:, 1, :], s5p[:, 0, :], ang[:, 2, 0, :], ALU.mult)
            tt(s5p[:, 2, :], s5p[:, 0, :], ang[:, 1, 0, :], ALU.mult)
            lr, li = s5p[:, 3, :], s5p[:, 4, :]
            tt(sm[:, 2, :], lr, lr, ALU.mult)
            tt(sm[:, 3, :], li, li, ALU.mult)
            tt(sm[:, 2, :], sm[:, 2, :], sm[:, 3, :], ALU.add)
            step(v.reciprocal(sm[:, 2, :], sm[:, 2, :]))
            ts(sm[:, 4, :], s5p[:, 1, :], -1.0, None, ALU.add)
            tt(sm[:, 5, :], sm[:, 4, :], lr, ALU.mult)
            tt(sm[:, 6, :], s5p[:, 2, :], li, ALU.mult)
            tt(sm[:, 5, :], sm[:, 5, :], sm[:, 6, :], ALU.add)
            tt(sm[:, 5, :], sm[:, 5, :], sm[:, 2, :], ALU.mult)
            tt(sm[:, 6, :], s5p[:, 2, :], lr, ALU.mult)
            tt(sm[:, 7, :], sm[:, 4, :], li, ALU.mult)
            tt(sm[:, 6, :], sm[:, 6, :], sm[:, 7, :], ALU.subtract)
            tt(sm[:, 6, :], sm[:, 6, :], sm[:, 2, :], ALU.mult)
            v.wait_ge(s.s5_in, 64)
            fr, fi = (sm[:, i, :].unsqueeze(2).to_broadcast([P, NST, 16]) for i in (5, 6))
            br, bi = bnat[:, 0, :, :], bnat[:, 1, :, :]
            for (x1, x2, op), out in (((fr, fi, ALU.subtract), 0), ((fi, fr, ALU.add), 1)):
                tt(btmp[:, 0, :, :], br, x1, ALU.mult)
                tt(btmp[:, 1, :, :], bi, x2, ALU.mult)
                tt(btmp[:, 0, :, :], btmp[:, 0, :, :], btmp[:, 1, :, :], op)
                for hh in range(2):
                    ts(bexp[:, out, :, hh, :], btmp[:, 0, :, :], mks[:, 2 + hh:3 + hh])
            for c in range(2):
                for hh in range(2):
                    ts(cexp[:, c, :, hh, :], cnat[:, c, :, :], mks[:, hh:hh + 1], -1.0 if c else 1.0,
                       ALU.mult, ALU.mult, s.s5_ask if (c, hh) == (1, 1) else None)

            def doubling(tabl, k0, steps):
                step(v.memset(tabl[:, 0, :, 0:1], 1.0))
                step(v.memset(tabl[:, 1, :, 0:1], 0.0))
                for k in range(steps):
                    n = 1 << k
                    c = ang[:, 2, k0 + k, :].unsqueeze(2).to_broadcast([P, NST, n])
                    sn = ang[:, 1, k0 + k, :].unsqueeze(2).to_broadcast([P, NST, n])
                    r, i = tabl[:, 0, :, 0:n], tabl[:, 1, :, 0:n]
                    t = etmp[:, 0, :, 0:n]
                    tt(tabl[:, 0, :, n:2 * n], r, c, ALU.mult)
                    tt(t, i, sn, ALU.mult)
                    tt(tabl[:, 0, :, n:2 * n], tabl[:, 0, :, n:2 * n], t, ALU.subtract)
                    tt(tabl[:, 1, :, n:2 * n], r, sn, ALU.mult)
                    tt(t, i, c, ALU.mult)
                    tt(tabl[:, 1, :, n:2 * n], tabl[:, 1, :, n:2 * n], t, ALU.add)

            doubling(elo, 0, 5)
            doubling(ehi, 5, 4)
            evict_u(2)
            evict_u(3)
            v.wait_ge(s.st_tr, 1)
            cp(convS[:].rearrange("p a b -> p (a b)"), aux[:, 0, 0:144])
            cp(scS[:].rearrange("p a b -> p (a b)"), aux[:, 0, 144:208])
            cp(plS[:].rearrange("p a b -> p (a b)"), aux[:, 0, 208:240])
            cp(h0[:].rearrange("p c a b -> p (c a b)"), aux[:, 1, 0:256], s.st_ev)
            v.wait_ge(s.s5_tr, 1)
            cp(bT[:].rearrange("p c a b -> p c (a b)"), aux[:, 2:4, :])
            cp(cT[:].rearrange("p c a b -> p c (a b)"), aux[:, 0:2, :], s.s5_ev)
            v.wait_ge(s.mem_sq, 2)
            ts(rmem[:, 2:4], rmem[:, 0:2], 1.0 / D, EPS, ALU.mult, ALU.add)
            step(v.reciprocal(rmem[:, 2:4], rmem[:, 2:4]), s.mem_inv)
            for k in range(KT):
                v.wait_ge(s.mem_hi, k + 1)
                stt(meml[:, k, :], aux[:, k % 2, 0:NMEM], gains[:, 3, k:k + 1], memh[:, k, :].bitcast(F32),
                    ALU.mult, ALU.subtract, s.mem_lo)
            v.wait_ge(s.mem_r, 1)

            def s5_states(st):
                c, sn = tab[:, st % 2, 0, :], tab[:, st % 2, 1, :]
                vr, vi, t, hr, hi = (rot[:, i, :] for i in (0, 1, 2, 3, 4))
                bur, bui = aux[:, 0, :], aux[:, 1, :]
                v.wait_ge(s.s5_bu, st + 1)
                v.wait_ge(s.tab_rdy, st + 1)
                tt(vr, bur, c, ALU.mult)
                tt(t, bui, sn, ALU.mult)
                tt(vr, vr, t, ALU.add)
                tt(vi, bui, c, ALU.mult)
                tt(t, bur, sn, ALU.mult)
                tt(vi, vi, t, ALU.subtract)
                a_r, a_i = s5p[:, 1, st:st + 1], s5p[:, 2, st:st + 1]
                so = s5o[:, :, st, :]
                stt(so[:, 0, 0:NS], h0[:, 0, st, :], a_r, aux[:, 3, 0:NS], ALU.mult, ALU.add)
                stt(so[:, 1, 0:NS], h0[:, 1, st, :], a_r, aux[:, 3, NS:2 * NS], ALU.mult, ALU.add, s.s5_rot)
                ts(t[:, 0:NS], h0[:, 1, st, :], a_i)
                tt(so[:, 0, 0:NS], so[:, 0, 0:NS], t[:, 0:NS], ALU.subtract)
                stt(so[:, 1, 0:NS], h0[:, 0, st, :], a_i, so[:, 1, 0:NS], ALU.mult, ALU.add)
                rho = s5p[:, 0, st:st + 1].to_broadcast([P, SEQ])
                step(v.tensor_tensor_scan(vr, rho, vr, 0.0, ALU.mult, ALU.add))
                step(v.tensor_tensor_scan(vi, rho, vi, 0.0, ALU.mult, ALU.add))
                if st >= 1:
                    v.wait_ge(s.s5_c, st)
                tt(hr, vr, c, ALU.mult)
                tt(t, vi, sn, ALU.mult)
                tt(hr, hr, t, ALU.subtract)
                tt(hi, vr, sn, ALU.mult)
                tt(t, vi, c, ALU.mult)
                tt(hi, hi, t, ALU.add)
                cp(so[:, 0, NS:NS + 1], hr[:, SEQ - 1:SEQ])
                cp(so[:, 1, NS:NS + 1], hi[:, SEQ - 1:SEQ], s.s5_h)

            def s5_y(f):
                v.wait_ge(s.s5_c, 4 * f + 4)
                stt(y[:, 4 + f, 0:SEQ], u5[:, f, 0:SEQ], c4[:, 1, f:f + 1], aux[:, 2, :], ALU.mult, ALU.add)
                stt(y[:, 4 + f, SEQ:TOK], u5[:, f, SEQ:TOK], c4[:, 1, f:f + 1], aux[:, 3, 32:40],
                    ALU.mult, ALU.add, s.s5_y)

            def evict_kv(b):
                v.wait_ge(s.pe_unit, 4 * (T_KV + 2 * b) + 8)
                if b >= 2:
                    v.wait_ge(kv_out[b % 2], 16 * (b // 2))
                ts(kvst[:, b % 2, 0, :], lin[:, 2 * (b % 2), :], rmem[:, 2:3])
                ts(kvst[:, b % 2, 1, :], lin[:, 2 * (b % 2) + 1, :], rmem[:, 3:4], sm=s.tile_free)

            for n in range(52):
                if n in S5_AT:
                    st = S5_AT.index(n)
                    if st > 0 and st % 4 == 0:
                        s5_y(st // 4 - 1)
                    s5_states(st)
                if n % 2 == 1:
                    evict_u(4 + n // 2)
            s5_y(3)
            step(v.memset(smx[:, 15:16], 0.0), s.s5_fin)

            for i in range(6):
                v.wait_ge(cv_in[i % 2], 16 * (i // 2 + 1))
                x, o = xb[:, i % 2, :], xc[:, i, :]
                step(v.memset(x[:, 0:3], 0.0))
                ts(o, x[:, 3:3 + TOK], cvw[:, i, 3:4], cvb[:, i:i + 1], ALU.mult, ALU.add)
                for r in (2, 1, 0):
                    stt(o[:, SEQ:TOK], convS[:, i, r:24:3], cvw[:, i, r:r + 1], o[:, SEQ:TOK], ALU.mult, ALU.add)
                    stt(o[:, 0:SEQ], x[:, r:r + SEQ], cvw[:, i, r:r + 1], o[:, 0:SEQ], ALU.mult, ALU.add,
                        s.cv_acc if r == 0 else None)
            ts(dtw[:, 0, :], dtr[:], dtb[:, 0:1], None, ALU.add)
            stt(dtw[:, 1, :], dtw[:, 0, :], -1.0, dtw[:, 0, :], ALU.mult, ALU.max)
            ts(dtw[:, 1, :], dtw[:, 1, :], -1.0, sm=s.dt_ask)

            def short_conv(i):
                v.wait_ge(sc_in[i % 2], 48 * (i // 2 + 1))
                c, hv, b, pr_ = (scb[:, i % 2, j, :] for j in range(4))
                step(v.memset(pr_[:, 0:2], 0.0))
                tt(pr_[:, 2:2 + TOK], c[:, 2:2 + TOK], hv[:, 0:TOK], ALU.mult)
                cp(scn[:, i, :], pr_[:, SEQ:SEQ + 10])
                o = y[:, 8 + i, :]
                ts(o[:, 0:SEQ], pr_[:, 2:2 + SEQ], scw[:, i, 2:3])
                stt(o[:, 0:SEQ], pr_[:, 1:1 + SEQ], scw[:, i, 1:2], o[:, 0:SEQ], ALU.mult, ALU.add)
                stt(o[:, 0:SEQ], pr_[:, 0:SEQ], scw[:, i, 0:1], o[:, 0:SEQ], ALU.mult, ALU.add)
                ts(o[:, SEQ:TOK], pr_[:, 2 + SEQ:2 + TOK], scw[:, i, 2:3])
                for r in (1, 0):
                    stt(o[:, SEQ:TOK], scS[:, i, r:16:2], scw[:, i, r:r + 1], o[:, SEQ:TOK], ALU.mult, ALU.add)
                tt(o, o, b[:, 0:TOK], ALU.mult, s.sc_done)

            short_conv(0)
            v.wait_ge(s.dt_act, 2)
            e, z, z2, dt = dtw[:, 1, :], dtw[:, 2, :], dtw[:, 3, :], dtw[:, 4, :]
            ts(z, e, 2.0, None, ALU.add)
            step(v.reciprocal(z, z))
            tt(z, z, e, ALU.mult)
            tt(z2, z, z, ALU.mult)
            ts(dt, z2, 1.0 / 17, 1.0 / 15, ALU.mult, ALU.add)
            for k in (13, 11, 9, 7, 5, 3, 1):
                tt(dt, dt, z2, ALU.mult)
                ts(dt, dt, 1.0 / k, None, ALU.add)
            tt(dt, dt, z, ALU.mult)
            ts(dtw[:, 1, :], dtw[:, 0, :], 0.0, None, ALU.max)
            stt(dtw[:, 2, :], dt, 2.0, dtw[:, 1, :], ALU.mult, ALU.add)
            ts(dtb[:, 2:3], dtb[:, 2:3], -1.0)
            ts(dtw[:, 1, :], dtw[:, 2, :], dtb[:, 2:3])
            cp(sdt[:, 0:8], dtw[:, 1, SEQ:TOK])
            one = ones[0:NH, 0:CH]
            for c in range(NC):
                w = slice(CH * c, CH * c + CH)
                step(v.tensor_tensor_scan(dtw[:, 3, w], one, dtw[:, 1, w], 0.0, ALU.mult, ALU.add),
                     s.dt_ask if c == 3 else None)
            for i in range(4):
                v.wait_ge(s.glu_sig, i + 1)
            for i in range(4):
                tt(y[:, 4 + i, :], y[:, 4 + i, :], sig[:, i, :], ALU.mult, s.glu_y if i == 3 else None)
            short_conv(1)
            v.wait_ge(s.dt_act, 7)
            tt(dtw[:, 5, 0:SEQ], dtw[:, 4, 0:SEQ], dtw[:, 2, 0:SEQ], ALU.mult, s.dt_done)
            evict_kv(0)
            short_conv(2)
            short_conv(3)
            v.wait_ge(s.tm_tr, 1)
            src = aux[:, 0, 0:128].rearrange("p (c j h) -> p c j h", c=NC, j=4)
            for j in range(3):
                ts(tm[:, j, :, :], src[:, :, j, :], -1.0 if j == 2 else 1.0, sm=s.tm_ev if j == 2 else None)
            v.wait_ge(s.tb_tr, 1)
            cp(tb[:].rearrange("p a b -> p (a b)"), aux[:, 1, :], s.tb_ev)
            for g in range(2):
                v.wait_ge(s.sc_mm, g + 1)
                tt(smk[:, g, :, :], aux[:, 2 + g, :].rearrange("p (a b) -> p a b", a=NC),
                   causal[:].unsqueeze(1).to_broadcast([P, NC, CH]), ALU.mult, s.sm_ev)
            for j in range(4):
                v.wait_ge(s.ea_act, j + 1)
                cp(decs[:, j, :], gm[:, j % 2, CH - 1:SEQ:CH])
                tt(cj[:, j, :], xc[:, 5, 0:SEQ], gm[:, j % 2, :], ALU.mult, s.cj_ev)
            evict_kv(1)

            def pool_rows(i, w):
                v.wait_ge(pu_in[i % 2], 16 * (i // 2 + 1))
                u = pu[:, i % 2, :]
                step(v.memset(u[:, 0:PH], 0.0))
                a, b = pt2[:, 0, :], pt2[:, 1, :]
                n = PH + SEQ
                src, dst = u, a
                for d in range(i + 1):
                    sh, lo = 1 << d, PH - (w - (2 << d))
                    tt(dst[:, lo:n], src[:, lo:n], src[:, lo - sh:n - sh], ALU.add)
                    src, dst = dst, (b if dst is a else a)
                if i >= 2:
                    v.wait_ge(s.pl_mm, i - 1)
                o = pt[:, i % 2, :]
                stt(o[:, 0:SEQ], src[:, PH:n], 1.0 / w, u[:, PH:n], ALU.mult, ALU.subtract)
                tt(o[:, 0:16], src[:, PH:PH + 16], mks[:, 48 + 16 * i:64 + 16 * i], ALU.mult)
                tt(o[:, 0:16], o[:, 0:16], u[:, PH:PH + 16], ALU.subtract)
                tt(o[:, SEQ:TOK], plS[:, i, :], u[:, n:n + NS], ALU.add)
                stt(o[:, SEQ:TOK], o[:, SEQ:TOK], 1.0 / w, u[:, n:n + NS], ALU.mult, ALU.subtract, s.mx_pool)

            for i in range(5):
                if i < 4:
                    pool_rows(i, POOL_W[i])
                if i >= 1:
                    v.wait_ge(s.pl_mm, i)
                    ts(halves(y[:, 11 + i, :]), aux[:, 0:2, 0:HALF], c4[:, 3, i - 1:i], sm=s.pl_ev)
            step(v.memset(hst[:].rearrange("p a b -> p (a b)"), 0.0))
            evict_kv(2)

            def norm_sum(j):
                for i in range(4):
                    add_square(KT + 4 * j + i, i == 0)

            def norm_apply(j):
                v.wait_ge(s.r_ready, 2 + j)
                for i in range(4):
                    k = 4 * NORM_ORDER[j] + i
                    stt(y[:, k, :], y[:, k, :], gains[:, 1, k:k + 1], rB[:], ALU.mult, ALU.mult, s.mixn)

            norm_sum(0)
            inverse(1, GW, 2)
            norm_apply(0)
            norm_sum(1)
            inverse(2, GW, 2)
            norm_apply(1)
            evict_kv(3)
            for c in range(NC):
                v.wait_ge(s.xt_tr, c + 1)
                xv = aux[:, 0, :].rearrange("p (h n) -> p h n", h=NH)
                if c > 0:
                    v.wait_ge(s.cs_mm, c)
                tt(xde[:].rearrange("p (h n) -> p h n", h=NH), xv,
                   tm[:, 1, c, :].unsqueeze(2).to_broadcast([P, NH, HD]), ALU.mult)
                tt(xdt[:, c, :].rearrange("p (h n) -> p h n", h=NH), xv,
                   tm[:, 0, c, :].unsqueeze(2).to_broadcast([P, NH, HD]), ALU.mult, s.xt_ev)
                v.wait_ge(s.cs_mm, c + 1)
                for g in range(2):
                    r, w = slice(64 * g, 64 * g + 64), slice(256 * g, 256 * g + 256)
                    o = hst[r, c + 1, w]
                    if c > 0:
                        tt(o.rearrange("p (h n) -> p h n", h=4), hst[r, c, w].rearrange("p (h n) -> p h n", h=4),
                           decs[r, :, c:c + 1].to_broadcast([64, 4, HD]), ALU.mult)
                        tt(o, o, aux[r, 1, w], ALU.add, s.h_ev if g else None)
                    else:
                        cp(o, aux[r, 1, w], s.h_ev if g else None)
            norm_sum(2)
            inverse(3, GW, 2)
            norm_apply(2)
            evict_kv(4)
            v.wait_ge(s.ss_in, 16 * 52)
            v.wait_ge(s.ss_s, 16 * 16)
            ts(r64[:, 0:32], r64[:, 0:32], s64[:, 1:2])
            tt(ht[:], r64[:, 0:32].unsqueeze(2).to_broadcast([P, 32, 64]), r64[:, 32:96].unsqueeze(1).to_broadcast([P, 32, 64]), ALU.mult)
            stt(hs[:].rearrange("p a b -> p (a b)"), hs[:].rearrange("p a b -> p (a b)"), s64[:, 0:1],
                ht[:].rearrange("p a b -> p (a b)"), ALU.mult, ALU.add)
            tt(ht[:], hs[:], r64[:, 96:160].unsqueeze(1).to_broadcast([P, 32, 64]), ALU.mult)
            step(v.tensor_reduce(y64[:], ht[:], AX.X, ALU.add), s.ss_y)

            def g_pre(hd):
                v.wait_ge(s.ac_mm, hd + 1)
                if hd >= 2:
                    v.wait_ge(s.y_mm, hd - 1)
                for c in range(NC):
                    w = slice(CH * c, CH * c + CH)
                    ts(gm[:, hd % 2, w], aux[:, hd % 2, w], tm[:, 2, c, hd:hd + 1], 0.0, ALU.add, ALU.min,
                       s.g_pre if c == 3 else None)

            g_pre(0)
            for hd in range(NH):
                if hd + 1 < NH:
                    g_pre(hd + 1)
                v.wait_ge(s.g_exp, hd + 1)
                g_ = gm[:, hd % 2, :].rearrange("p (a b) -> p a b", a=NC)
                tt(g_, g_, smk[:, hd // 4, :, :], ALU.mult, s.g_ev)
                if hd in (2, 6):
                    evict_kv(5 if hd == 2 else 6)
                if hd % 2 == 1:
                    i = hd // 2
                    v.wait_ge(s.y_mm, hd + 1)
                    stt(y[:, i, 0:SEQ], xc[:, i, 0:SEQ], c4[:, 0, i:i + 1], aux[:, 2 + i % 2, :], ALU.mult, ALU.add, s.y_ev)
                    v.wait_ge(s.z_act, i + 1)
                    tt(y[:, i, 0:SEQ], y[:, i, 0:SEQ], zt[:, i % 2, 0:SEQ], ALU.mult)
                    cp(zs[:, i, :], zt[:, i % 2, SEQ:TOK], s.z_use)
            v.wait_ge(s.ss_yin, 16 * 8)
            for i in range(4):
                o = y[:, i, SEQ:TOK]
                stt(o, xc[:, i, SEQ:TOK], c4[:, 0, i:i + 1], o, ALU.mult, ALU.add)
                tt(o, o, zs[:, i, :], ALU.mult, s.y_fin if i == 3 else None)
            norm_sum(3)

            def mix_lo(n):
                k = OUT_ORDER[n]
                v.wait_ge(s.split_hi, KT + n + 1)
                tt(mixl[:, k, :], y[:, k, :], mixh[:, k, :].bitcast(F32), ALU.subtract, s.split_lo)

            for n in range(4):
                mix_lo(n)
            inverse(4, GW, 2)
            for n in range(4, 8):
                mix_lo(n)
            norm_apply(3)
            for n in range(8, 12):
                mix_lo(n)
            evict_kv(7)
            for n in range(12, KT):
                mix_lo(n)
            v.wait_ge(s.ps_tr, 1)
            for g in range(2):
                for i in (2 * g, 2 * g + 1):
                    cp(pst[:, i, :], aux[:, 0, P * i + 64 * g:P * i + 64 * g + 64], s.ps_ev if i == 3 else None)
            v.wait_ge(s.h_in, 16)

            def residual_pair(T, m, n, lo, g):
                for i in range(2):
                    v.wait_ge(s.pe_unit, 4 * T + (2 * i + 2))
                    w = bass.ds(TOK * (m + i), TOK)
                    ht = flat(h)[:, w]
                    tt(halves(ht), lin_tile(i), halves(ht), ALU.add, s.tile_free)
                    if lo is not None:
                        v.wait_ge(s.split_hi, n + (i + 1))
                        stt(flat(lo[0])[:, w], ht, gains[:, g, bass.ds(m + i, 1)], flat(lo[1])[:, w].bitcast(F32),
                            ALU.mult, ALU.subtract, s.split_lo)
                    if n is not None:
                        v.wait_ge(s.sq_done, (4 * KT if lo is None else 0) + n + (i + 1))
                        tt(ssq[:], ssq[:], sqt[:], ALU.add, s.ss_done)

            def residual(T0, n0, lo, g):
                step(v.memset(ssq[:], 0.0))
                with v.Fori(0, 8) as p:
                    step.enter(p, [(s.tile_free, 2), (s.ss_done, 2)] + ([(s.split_lo, 2)] if lo else []))
                    residual_pair(p + T0, 2 * p, 2 * p + n0, lo, g)
                    step.leave(8)

            residual(T_OUT, 2 * KT, (al, ah), 2)
            inverse(5, D, 2)

            def evict_q(t):
                v.wait_ge(s.pe_unit, 4 * T_Q + 2 * t + 2)
                if t == 0:
                    v.wait_ge(s.r_ready, 6)
                tt(halves(q[:, t, :]), lin_tile(t % 2), halves(rB[:]), ALU.mult, s.tile_free)

            for hd in range(XAH):
                for t in range(4 * hd, 4 * hd + 4):
                    evict_q(t)
                v.wait_ge(s.kt_tr, hd + 1)
                cp(kTh[:].rearrange("p (a d) m -> p a (d m)", a=2), aux[:, 0:2, :], s.kt_ev)
                for t4 in range(4):
                    n = 4 * hd + t4
                    v.wait_ge(s.sc2, n + 1)
                    sc = lin[:, t4, 0:NMEM]
                    step(v.tensor_reduce(smx[:, 0:1], sc, AX.X, ALU.max))
                    if n >= 1:
                        v.wait_ge(s.p_tr, n)
                    ts(smx[:, 1:2], smx[:, 0:1], -SCALE, sm=s.p_ask)
                    for b in (2 * t4, 2 * t4 + 1):
                        m = 8 * hd + b
                        i = 16 * hd + b
                        v.wait_ge(s.qb, m + 1)
                        v.wait_ge(pc_in[i % 4], 16 * (i // 4 + 1))
                        for mt in range(2):
                            step(v.tensor_tensor_reduce(piece[:, i % 4, mt, :], piece[:, i % 4, mt, :], aux[:, b % 2, :],
                                                        1.0, 0.0, ALU.mult, ALU.add, ssc[:, mt, b:b + 1]),
                                 s.ss_ev if mt else None)
                    v.wait_ge(s.p_exp, n + 1)
                    step(v.reciprocal(smx[:, 3:4], smx[:, 2:3]))
                    ts(pr[:], pr[:], smx[:, 3:4], sm=s.p_ev)
                    v.wait_ge(s.p_tr, n + 1)
                    if n >= 4:
                        v.wait_ge(s.pv, 4 * hd)
                    cp(pT[:, :, P * t4:P * t4 + P], aux[:, 3, 0:NMEM].rearrange("p (m t) -> p m t", m=2), s.pt_ev)
                for d in range(4):
                    k = 4 * hd + d
                    v.wait_ge(s.pv, k + 1)
                    cp(q[:, k, 0:SEQ], aux[:, d % 2, :], s.o_ev)
                v.wait_ge(s.sp_tr, hd + 1)
                sc = aux[0:NS, 2, 0:NMEM]
                step(v.tensor_reduce(smx[0:NS, 4:5], sc, AX.X, ALU.max))
                ts(smx[0:NS, 5:6], smx[0:NS, 4:5], -SCALE, sm=s.sp_ask)
                v.wait_ge(s.sp_exp, hd + 1)
                step(v.reciprocal(smx[0:NS, 7:8], smx[0:NS, 6:7]))
                ts(prs[:], prs[:], smx[0:NS, 7:8], sm=s.sp_ev)
                v.wait_ge(s.sp_tb, hd + 1)
                cp(pTs[:].rearrange("p a b -> p (a b)"), aux[:, 3, 256:272], s.sp_tev)
                v.wait_ge(s.spv, 8 * hd + 8)
                cp(q[:, 4 * hd:4 * hd + 4, SEQ:TOK], aux[:, 2, 256:288].rearrange("p (d b) -> p d b", d=4), s.so_ev)
            for k in range(KT):
                v.wait_ge(s.oh_hi, k + 1)
                tt(ol[:, k, :], q[:, k, :], oh[:, k, :].bitcast(F32), ALU.subtract, s.oh_lo)
            residual(T_O, 3 * KT, (ml, mh), 4)
            inverse(6, D, 2)
            v.wait_ge(s.r_ready, 7)

            def up_pair(T, c, p):
                for i in range(2):
                    v.wait_ge(s.pe_unit, 4 * T + (2 * i + 2))
                    n = 16 * c + 2 * p
                    stt(halves(upr[:]), lin_tile(i), 0.0, halves(rB[:]), ALU.max, ALU.mult, s.tile_free)
                    v.wait_ge(s.hid_hi, n + (i + 1))
                    w = bass.ds(TOK * (2 * p + i), TOK)
                    tt(flat(fl)[:, w], hsq[:], flat(fh)[:, w].bitcast(F32), ALU.subtract, s.hid_lo)

            per_up = [(s.tile_free, 2), (s.hid_lo, 2)]
            with v.Fori(0, N_CHUNK - 1) as c:
                step.enter(c, [(s.hid_lo, 16), (s.tile_free, 32)])
                with v.Fori(0, 8) as p:
                    step.enter(p, per_up)
                    up_pair(16 * c + p + T_MLP, c, p)
                    step.leave(8)
                with v.Fori(0, 8) as p:
                    step.enter(p, [(s.tile_free, 2)])
                    residual_pair(16 * c + p + (T_MLP + 8), 2 * p, None, None, None)
                    step.leave(8)
                step.leave(N_CHUNK - 1)
            L = N_CHUNK - 1
            with v.Fori(0, 8) as p:
                step.enter(p, per_up)
                up_pair(p + (T_MLP + 16 * L), L, p)
                step.leave(8)
            step(v.memset(ssq[:], 0.0))
            with v.Fori(0, 8) as p:
                step.enter(p, [(s.tile_free, 2), (s.ss_done, 2)])
                residual_pair(p + (T_MLP + 16 * L + 8), 2 * p, 2 * p, None, None)
                step.leave(8)
            inverse(7, D, 2)
            v.wait_ge(s.r_ready, 8)
            for k in range(KT):
                stt(h[:, k, :], h[:, k, :], gains[:, 5, k:k + 1], rB[:], ALU.mult, ALU.mult, s.f_ev)


N_PAR = 22
N_OUT = 112

_IN = {
    "x_prompt": (SEQ, D), "x_sample": (NS, D), "mem_prompt": (NMEM, D), "state_ssd_conv": (24, 768),
    "state_ssd": (NS, NH, 4096), "state_s5_re": (NS, D), "state_s5_im": (NS, D), "state_sconv": (16, GW),
    "state_pool": (NS * PH, GW), "cache_mem_k": (NS, NMEM, D), "cache_mem_v": (NS, NMEM, D),
    "norm_mix_g": (D,), "w_in": (D, IN_W), "ssd_conv_w": (4, 768), "ssd_conv_b": (768,), "ssd_dt_bias": (NH,),
    "ssd_a_log": (NH,), "ssd_d": (NH,), "s5_lam_re": (32, 64), "s5_lam_im": (32, 64), "s5_log_dt": (32,),
    "s5_b_re": (32, 64, 16), "s5_b_im": (32, 64, 16), "s5_c_re": (32, 16, 64), "s5_c_im": (32, 16, 64),
    "s5_d": (GW,), "s5_w_glu": (GW, GW), "s5_b_glu": (GW,), "sc_conv_w": (3, GW), "pool_w": (4, P, P),
    "pool_scale": (GW,), "mix_out_g": (D,), "w_out": (D, D), "norm_xa_g": (D,), "norm_mem_g": (D,),
    "w_q": (D, D), "w_k": (D, D), "w_v": (D, D), "w_o": (D, D), "norm_mlp_g": (D,), "w_up": (D, DFF),
    "w_down": (DFF, D), "final_norm_g": (D,),
}
_SHORT = {"mem_prompt": "mem", "cache_mem_k": "cache_k", "cache_mem_v": "cache_v"}
_OUT = [
    ("y_prompt", (SEQ, D), (1, SEQ, D)), ("y_sample", (NS, D), (NS, 1, D)),
    ("p_ssd_conv", (3, 768), (1, 1, 3, 768)), ("p_ssd", (512, 64), (1, 1, 8, 64, 64)),
    ("p_s5_re", (32, 64), (1, 1, 32, 64)), ("p_s5_im", (32, 64), (1, 1, 32, 64)),
    ("p_sconv", (2, GW), (1, 1, 2, GW)), ("p_pool", (PH, GW), (1, 1, PH, GW)),
    ("p_mem_k", (NMEM, D), (1, 1, NMEM, XAH, XAD)), ("p_mem_v", (NMEM, D), (1, 1, NMEM, XAH, XAD)),
    ("s_ssd_conv", (24, 768), (1, NS, 3, 768)), ("s_ssd", (NS, NH, 4096), (1, NS, 8, 64, 64)),
    ("s_s5_re", (256, 64), (1, NS, 32, 64)), ("s_s5_im", (256, 64), (1, NS, 32, 64)),
    ("s_sconv", (16, GW), (1, NS, 2, GW)), ("s_pool", (NS * PH, GW), (1, NS, PH, GW)),
]


def kernel(**inputs):
    import concourse.bacc as bacc
    from concourse.bass_utils import run_bass_kernel_spmd

    nc = bacc.Bacc("TRN2", target_bir_lowering=False, num_devices=1, dynamic_dma_scratch_size=1024)
    arrays, io = {}, {}
    for name, shape in _IN.items():
        a = np.ascontiguousarray(inputs[name]).reshape(shape)
        arrays["in_" + name] = a
        io[_SHORT.get(name, name)] = nc.dram_tensor("in_" + name, shape, mybir.dt.from_np(a.dtype), kind="ExternalInput").ap()
    arrays["consts"] = constants()
    cst = nc.dram_tensor("consts", arrays["consts"].shape, F32, kind="ExternalInput").ap()
    outs = {n: nc.dram_tensor("out_" + n, shape, F32, kind="ExternalOutput").ap() for n, shape, _ in _OUT}
    build(nc, io, cst, outs)
    r = run_bass_kernel_spmd(nc, [arrays], core_ids=[0])
    return tuple(r.results[0]["out_" + n].reshape(shape) for n, _, shape in _OUT)
```

```python
from contextlib import ExitStack

import numpy as np

import concourse.bass as bass
from concourse import mybir
from concourse.alu_op_type import AluOpType as ALU

F32 = mybir.dt.float32
F32R = mybir.dt.float32r
ACT = mybir.ActivationFunctionType
AX = mybir.AxisListType

P = 128
D = 2048
KT = D // P
SEQ = 512
NS = 8
TOK = SEQ + NS
HALF = TOK // 2
NMEM = 256
GW = 512
GT = GW // P
DFF = 4 * D
EPS = 1e-6
NH = 8
HD = 64
CH = 128
NC = SEQ // CH
NST = 16
XAH = 4
XAD = D // XAH
SCALE = float(XAD) ** -0.5
POOL_W = (2, 4, 8, 16)
PH = 15

C_Z, C_XBC, C_DT, C_U5, C_B, C_C, C_HV, C_POOL = 0, 512, 1280, 1288, 1800, 2312, 2824, 3336
IN_W = 3848

T_KV, T_OUT, T_Q, T_O, T_MLP = 15, 31, 39, 47, 55
N_CHUNK = DFF // D
T_END = T_MLP + 16 * N_CHUNK
O_KV, O_OUT, O_Q, O_O, O_MLP = 30, 38, 54, 70, 86

PI2_A = 6.28125
PI2_B = float((np.float32(2 * np.pi - PI2_A).view(np.uint32) & np.uint32(0xFFFFE000)).view(np.float32))
PI2_C = float(2 * np.pi - PI2_A - PI2_B)
ROUND = 12582912.0
PI_IN = 3.1415925

S5_AT = [4 + 3 * st for st in range(16)]
FIRST = (0, 2, 1, 3)
NORM_ORDER = (1, 2, 3, 0)
OUT_ORDER = (*range(8, 16), *range(4, 8), *range(0, 4))


def constants():
    c = np.zeros((P, 1264), np.float32)
    c[:, 0:128] = np.eye(P)
    c[:, 128:256] = 1.0
    p = np.arange(P)
    c[:, 256:384] = p[:, None] <= p[None, :]
    c[:, 384] = (p // 16) % 2 == 0
    c[:, 385] = (p // 16) % 2 == 1
    c[:, 386] = p < 64
    c[:, 387] = p >= 64
    for g, w in enumerate(POOL_W):
        for b in range(NS):
            c[b * PH + PH - (w - 1):(b + 1) * PH, 400 + 8 * g + b] = 1.0
        c[:, 432 + 16 * g:448 + 16 * g] = 1.0 / np.minimum(w, np.arange(16) + 1.0)
    for j in range(4):
        for k in range(8):
            c[k, 512 + 128 * j:640 + 128 * j] = (k % 4 == j) & (p // 64 == k // 4)
    return c


class Steps:

    def __init__(self, eng, own):
        self.eng, self.own, self.n, self.loop_i, self.per = eng, own, {}, [], {}

    def __call__(self, ins, sem=None):
        sem = sem or self.own
        ins.then_inc(sem, 1)
        self.n[sem] = self.n.get(sem, 0) + 1
        at = self.n[sem]
        for i, per in self.loop_i:
            at = i * per.get(sem, 0) + at
        self.eng.wait_ge(sem, at)

    def enter(self, i, per):
        self.loop_i.append((i, {s: c for s, c in per}))

    def leave(self, turns):
        _, per = self.loop_i.pop()
        for k, c in per.items():
            self.n[k] = self.n.get(k, 0) + c * (turns - 1)


class Signals:
    pass


def build(nc, io, consts_ap, outs):
    xscr = nc.dram_tensor("xscr", [P, KT, TOK], F32, kind="Internal").ap()
    uscr = nc.dram_tensor("uscr", [IN_W, TOK], F32, kind="Internal").ap()
    zscr = nc.dram_tensor("zscr", [NS, GW], F32, kind="Internal").ap()
    bscr = nc.dram_tensor("bscr", [NS, 2, P], F32, kind="Internal").ap()
    dscr = nc.dram_tensor("dscr", [128], F32, kind="Internal").ap()
    yscr = nc.dram_tensor("yscr", [NS, NH, 64], F32, kind="Internal").ap()
    base = 1152
    R_H = base
    R_A = R_H + KT * TOK * 4
    R_B = R_A + 2 * KT * TOK * 4
    R_W = R_B + 2 * KT * TOK * 4
    R_S = R_W + 10 * 4096
    here = {"at": R_S}

    def at(name, shape, off, dt=F32):
        return nc.alloc_sbuf_tensor_at(name, shape, dt, offset=off)

    def small(name, shape, dt=F32):
        n = 4
        for s in shape[1:]:
            n *= s
        t = at(name, shape, here["at"], dt)
        here["at"] += (n + 31) // 32 * 32
        assert here["at"] <= 229344, here["at"]
        return t

    ctx = ExitStack()
    with ctx:
        def sem(name):
            return ctx.enter_context(nc.semaphore(name))

        h = at("h", [P, KT, TOK], R_H)
        xT = at("xT", [P, KT, TOK], R_H)
        y = at("y", [P, KT, TOK], R_H)
        LO = KT * TOK * 4
        xh = at("xh", [P, KT, TOK], R_A, F32R)
        xl = at("xl", [P, KT, TOK], R_A + LO, F32R)
        mixh = at("mixh", [P, KT, TOK], R_A, F32R)
        mixl = at("mixl", [P, KT, TOK], R_A + LO, F32R)
        ah = at("ah", [P, KT, TOK], R_B, F32R)
        al = at("al", [P, KT, TOK], R_B + LO, F32R)
        q = at("q", [P, KT, TOK], R_A)
        oh = at("oh", [P, KT, TOK], R_B, F32R)
        ol = at("ol", [P, KT, TOK], R_B + LO, F32R)
        mh = at("mh", [P, KT, TOK], R_A, F32R)
        ml = at("ml", [P, KT, TOK], R_A + LO, F32R)
        fh = at("fh", [P, KT, TOK], R_B, F32R)
        fl = at("fl", [P, KT, TOK], R_B + LO, F32R)
        raw = at("raw", [P, 2, 1024], R_W)
        whi = at("whi", [P, 4, 1024], R_W + 8192, F32R)
        wlo = at("wlo", [P, 4, 1024], R_W + 8192 + 16384, F32R)

        xnat = at("xnat", [P, 5, D], R_B)
        mnat = at("mnat", [P, 2, D], R_B + 40960)
        s5nat = at("s5nat", [NS, 2, D], R_H)
        cvnat = at("cvnat", [24, 768], R_H + 16640)
        scnat = at("scnat", [16, GW], R_H + 16640 + 3072)
        plnat = at("plnat", [NS * PH, GW], R_H + 16640 + 5120)
        memh = at("memh", [P, KT, NMEM], R_B, F32R)
        meml = at("meml", [P, KT, NMEM], R_B + 16384, F32R)

        dte = at("dte", [NH, 3, TOK], R_H + 16640)
        bnat = at("bnat", [P, 2, NST, 16], R_B)
        cnat = at("cnat", [P, 2, 4, 64], R_B + 2048)
        bexp = at("bexp", [P, 2, NST, 2, 16], R_B + 4096)
        cexp = at("cexp", [P, 2, 4, 2, 64], R_B + 8192)
        sm = at("sm", [P, 24, NST], R_B + 12288)
        ang = at("ang", [P, 4, 9, NST], R_B + 12288 + 1536)
        btmp = at("btmp", [P, 2, NST, 16], R_B + 12288 + 4096)
        bT = at("bT", [P, 2, 4, P], R_H)
        cT = at("cT", [P, 2, 4, P], R_H + 4096)
        elo = at("elo", [P, 2, NST, 32], R_H + 23808)
        ehi = at("ehi", [P, 2, NST, 16], R_H + 27904)
        etmp = at("etmp", [P, 2, NST, 16], R_H + 29952)
        BU = R_B + 32768
        rot = at("rot", [P, 5, SEQ], BU)
        tab = at("tab", [P, 2, 2, SEQ], BU + 10240)
        stg = at("stg", [P, 2, TOK], BU + 18432)
        u5 = at("u5", [P, GT, TOK], BU + 24704)
        ptmp = at("ptmp", [P, SEQ], BU + 22592)

        kvst = at("kvst", [P, 2, 2, 512], R_A)
        xc = at("xc", [P, 6, TOK], R_A + 8192)
        dtw = at("dtw", [NH, 6, TOK], R_A + 20672)
        xb = at("xb", [P, 6, 528], R_A + 33152)
        tb = at("tb", [P, NC, P], R_A + 33152)
        smk = at("smk", [P, 2, NC, CH], R_A + 35200)
        scb = at("scb", [P, 2, 4, 524], R_A + 45824)
        xdt = at("xdt", [P, NC, GW], R_A + 39296)
        xde = at("xde", [P, GW], R_A + 47488)
        cj = at("cj", [P, 4, SEQ], R_A + 49536)
        ht = at("ht", [P, 32, 64], R_A + 58368)
        sig = at("sig", [P, GT, TOK], BU)
        gm = at("gm", [P, 2, SEQ], BU)
        tm = at("tm", [P, 3, NC, NH], BU + 4096)
        decs = at("decs", [P, 4, NC], BU + 4480)
        r64 = at("r64", [P, 160], BU + 4544)
        s64 = at("s64", [P, 2], BU + 5184)
        y64 = at("y64", [P, 32], BU + 5216)
        zs = at("zs", [P, 4, NS], BU + 5408)
        selG = at("selG", [8, 4, P], BU + 23296)
        pu = at("pu", [P, 2, PH + TOK + 1], BU + 8320)
        pt = at("pt", [P, 2, PH + TOK + 1], BU + 12608)
        pt2 = at("pt2", [P, 2, PH + TOK + 1], BU + 16896)
        plw = at("plw", [P, GT, P], BU + 21184)
        hst = at("hst", [P, NC + 1, GW], BU + 8128)
        pst = at("pst", [P, 4, 64], BU + 18368)
        zt = at("zt", [P, 2, TOK], BU + 21440)
        wglu = at("wglu", [P, GT, GW], BU + 25600)
        hs = at("hs", [P, 32, 64], BU + 25600)

        AT = R_A + LO
        kNh = at("kNh", [P, 2, XAD], AT)
        kTh = at("kTh", [P, 4, NMEM], AT + 4096)
        vNh = at("vNh", [P, 2, XAD], AT + 8192)
        po = at("po", [NS, XAD], AT + 4096)
        pT = at("pT", [P, 2, SEQ], AT + 12288)
        piece = at("piece", [P, 4, 2, XAD], AT + 16384)
        ynat = at("ynat", [P, 5, D], R_A)

        idn = small("idn", [P, P])
        ones = small("ones", [P, P])
        causal = small("causal", [P, P])
        mks = small("mks", [P, 112])
        gains = small("gains", [P, 6, KT])
        cvw = small("cvw", [P, 6, 4])
        cvb = small("cvb", [P, 6])
        scw = small("scw", [P, 4, 3])
        c4 = small("c4", [P, 4, 4])
        dtb = small("dtb", [NH, 4])
        rB = small("rB", [P, TOK])
        ssq = small("ssq", [P, TOK])
        sqt = small("sqt", [P, TOK])
        upr = at("upr", [P, TOK], here["at"])
        dtr = small("dtr", [NH, TOK])
        dwt = small("dwt", [P, KT, NH])
        dwh = small("dwh", [P, KT, NH], F32R)
        dwl = small("dwl", [P, KT, NH], F32R)
        convS = small("convS", [P, 6, 24])
        scS = small("scS", [P, 4, 16])
        plS = small("plS", [P, 4, NS])
        h0 = small("h0", [P, 2, NST, NS])
        sde = small("sde", [NH, 8])
        scn = small("scn", [P, 4, 10])
        s5o = small("s5o", [P, 2, NST, NS + 1])
        rmem = small("rmem", [P, 8])
        s5p = small("s5p", [P, 8, NST])
        smx = small("smx", [P, 16])
        hsq = at("hsq", [P, TOK], here["at"])
        pr = small("pr", [P, NMEM])
        prs = small("prs", [NS, NMEM])
        pTd = small("pTd", [P, 2, NS, NS])
        ssc = small("ssc", [P, 2, NS])
        lin = ctx.enter_context(nc.psum_tensor("lin", [P, 4, 512], F32))
        aux = ctx.enter_context(nc.psum_tensor("aux", [P, 4, 512], F32))

        s = Signals()
        s.cst_in = sem("cst_in")
        s.gain_in = sem("gain_in")
        s.gmix_in = sem("gmix_in")
        s.par_in = sem("par_in")
        s.x_in0 = sem("x_in0")
        s.x_in1 = sem("x_in1")
        s.x_in2 = sem("x_in2")
        s.x_in3 = sem("x_in3")
        s.x_in4 = sem("x_in4")
        s.mem_in = sem("mem_in")
        s.st_in = sem("st_in")
        s.s5_in = sem("s5_in")
        s.xs_st = sem("xs_st")
        s.raw0 = sem("raw0")
        s.raw1 = sem("raw1")
        s.w_hi = sem("w_hi")
        s.w_lo = sem("w_lo")
        s.pe_unit = sem("pe_unit")
        s.tile_free = sem("tile_free")
        s.x_tr = sem("x_tr")
        s.x_ev = sem("x_ev")
        s.split_hi = sem("split_hi")
        s.split_lo = sem("split_lo")
        s.sq_done = sem("sq_done")
        s.ss_done = sem("ss_done")
        s.stat_mm = sem("stat_mm")
        s.inv_done = sem("inv_done")
        s.r_ready = sem("r_ready")
        s.dt_hi = sem("dt_hi")
        s.dt_lo = sem("dt_lo")
        s.dt_mm = sem("dt_mm")
        s.dt_ev = sem("dt_ev")
        s.st_tr = sem("st_tr")
        s.st_ev = sem("st_ev")
        s.s5_tr = sem("s5_tr")
        s.s5_ev = sem("s5_ev")
        s.mem_tr = sem("mem_tr")
        s.mem_hi = sem("mem_hi")
        s.mem_lo = sem("mem_lo")
        s.mem_sq = sem("mem_sq")
        s.mem_inv = sem("mem_inv")
        s.mem_r = sem("mem_r")
        s.s5_act = sem("s5_act")
        s.s5_ask = sem("s5_ask")
        s.tab_rdy = sem("tab_rdy")
        s.s5_bu = sem("s5_bu")
        s.s5_rot = sem("s5_rot")
        s.s5_h = sem("s5_h")
        s.s5_c = sem("s5_c")
        s.s5_y = sem("s5_y")
        s.s5_fin = sem("s5_fin")
        s.pj0 = sem("pj0")
        s.pj1 = sem("pj1")
        s.kv0 = sem("kv0")
        s.kv1 = sem("kv1")
        s.glu_in = sem("glu_in")
        s.glu_act = sem("glu_act")
        s.glu_mm = sem("glu_mm")
        s.glu_sig = sem("glu_sig")
        s.glu_y = sem("glu_y")
        s.sc_done = sem("sc_done")
        s.pl_in = sem("pl_in")
        s.pl_mm = sem("pl_mm")
        s.pl_ev = sem("pl_ev")
        s.cv_in0 = sem("cv_in0")
        s.sc_in0 = sem("sc_in0")
        s.sc_in1 = sem("sc_in1")
        s.pu0 = sem("pu0")
        s.pu1 = sem("pu1")
        s.z_in0 = sem("z_in0")
        s.z_in1 = sem("z_in1")
        s.sel_in = sem("sel_in")
        s.cst2_in = sem("cst2_in")
        s.cv_in1 = sem("cv_in1")
        s.cv_acc = sem("cv_acc")
        s.cv_act = sem("cv_act")
        s.dt_ask = sem("dt_ask")
        s.dt_act = sem("dt_act")
        s.dt_done = sem("dt_done")
        s.tm_tr = sem("tm_tr")
        s.tm_ev = sem("tm_ev")
        s.tb_tr = sem("tb_tr")
        s.tb_ev = sem("tb_ev")
        s.xt_tr = sem("xt_tr")
        s.xt_ev = sem("xt_ev")
        s.sc_mm = sem("sc_mm")
        s.sm_ev = sem("sm_ev")
        s.ea_mm = sem("ea_mm")
        s.ea_act = sem("ea_act")
        s.cj_ev = sem("cj_ev")
        s.cs_mm = sem("cs_mm")
        s.h_ev = sem("h_ev")
        s.z_use = sem("z_use")
        s.y_fin = sem("y_fin")
        s.mx_pool = sem("mx_pool")
        s.ss_out = sem("ss_out")
        s.mixn = sem("mixn")
        s.oh_hi = sem("oh_hi")
        s.oh_lo = sem("oh_lo")
        s.ac_mm = sem("ac_mm")
        s.g_pre = sem("g_pre")
        s.g_exp = sem("g_exp")
        s.g_ev = sem("g_ev")
        s.y_mm = sem("y_mm")
        s.y_ev = sem("y_ev")
        s.z_act = sem("z_act")
        s.ps_tr = sem("ps_tr")
        s.ps_ev = sem("ps_ev")
        s.ss_st = sem("ss_st")
        s.ss_in = sem("ss_in")
        s.ss_s = sem("ss_s")
        s.ss_y = sem("ss_y")
        s.ss_yst = sem("ss_yst")
        s.ss_yin = sem("ss_yin")
        s.out_st = sem("out_st")
        s.h_in = sem("h_in")
        s.kh_in = sem("kh_in")
        s.vh_in = sem("vh_in")
        s.kt_tr = sem("kt_tr")
        s.kt_ev = sem("kt_ev")
        s.sc2 = sem("sc2")
        s.p_ask = sem("p_ask")
        s.p_exp = sem("p_exp")
        s.p_ev = sem("p_ev")
        s.p_tr = sem("p_tr")
        s.pt_ev = sem("pt_ev")
        s.pv = sem("pv")
        s.o_ev = sem("o_ev")
        s.qb = sem("qb")
        s.ss_ev = sem("ss_ev")
        s.pc0 = sem("pc0")
        s.pc1 = sem("pc1")
        s.pc2 = sem("pc2")
        s.pc3 = sem("pc3")
        s.sp_tr = sem("sp_tr")
        s.sp_ask = sem("sp_ask")
        s.sp_exp = sem("sp_exp")
        s.sp_ev = sem("sp_ev")
        s.sp_tb = sem("sp_tb")
        s.sp_tev = sem("sp_tev")
        s.spv = sem("spv")
        s.po_ev = sem("po_ev")
        s.so_tr = sem("so_tr")
        s.so_ev = sem("so_ev")
        s.up_sq = sem("up_sq")
        s.hid_hi = sem("hid_hi")
        s.hid_lo = sem("hid_lo")
        s.f_ev = sem("f_ev")
        s.f_tr = sem("f_tr")
        s.f_nat = sem("f_nat")
        s.pe_own = sem("pe_own")
        s.act_own = sem("act_own")
        s.dve_own = sem("dve_own")
        s.pool_own = sem("pool_own")

        raw_rdy = (s.raw0, s.raw1)
        x_in = (s.x_in0, s.x_in1, s.x_in2, s.x_in3, s.x_in4)
        pj = (s.pj0, s.pj1)
        kv_out = (s.kv0, s.kv1)
        cv_in = (s.cv_in0, s.cv_in1)
        sc_in = (s.sc_in0, s.sc_in1)
        pu_in = (s.pu0, s.pu1)
        z_in = (s.z_in0, s.z_in1)
        pc_in = (s.pc0, s.pc1, s.pc2, s.pc3)

        def halves(t):
            return t.rearrange("p (a b) -> p a b", a=2)

        def flat(t):
            return t[:].rearrange("p k n -> p (k n)")

        def lin_tile(b):
            return lin[:, 2 * b:2 * b + 2, 0:HALF]

        def kp(w):
            return w.rearrange("(k p) n -> p k n", p=P)

        def copied(k):
            return k + 1 + (k + 1) // 4

        def in_row(t):
            return C_U5 + P * t if t < 20 else P * (t - 20)

        ctx.enter_context(nc.allow_non_contiguous_dma(reason="small parameters and states"))
        block = ctx.enter_context(nc.Block())

        @block.sync
        def _(sp):
            def load_tokens(c):
                sp.dma_start(xnat[:, 0:4, 512 * c:512 * c + 512],
                             io["x_prompt"].rearrange("(t p) n -> p t n", p=P)[:, :, 512 * c:512 * c + 512]).then_inc(x_in[c], 16)

            load_tokens(0)
            sp.dma_start(xnat[0:NS, 4, :], io["x_sample"]).then_inc(x_in[4], 16)

            def load_first(pos):
                if pos >= 2:
                    sp.wait_ge(s.w_hi, pos - 1)
                    sp.wait_ge(s.w_lo, pos - 1)
                slot = FIRST[pos]
                sp.dma_start(raw[:, pos % 2, :].rearrange("p (k n) -> p k n", n=P),
                             kp(io["w_in"])[:, 8 * (slot % 2):8 * (slot % 2) + 8,
                                            C_U5 + P * (slot // 2):C_U5 + P * (slot // 2) + P]).then_inc(raw_rdy[pos % 2], 16)

            def load(T, slot, src, shape):
                sp.wait_ge(s.w_hi, 4 * T + (slot - 1))
                sp.wait_ge(s.w_lo, 4 * T + (slot - 1))
                dst = raw[:, slot % 2, :].rearrange("p (k n) -> p k n", n=shape)
                sp.dma_start(dst, src).then_inc(raw_rdy[slot % 2], 16)

            def load_pair(T, w, col, k0=0, turned=0):
                load_slots(T, w, col, range(4), k0, turned)

            def load_slots(T, w, col, slots, k0=0, turned=0):
                for slot in slots:
                    load(T, slot, kp(w)[:, bass.ds(k0 + 8 * ((slot + turned) % 2), 8), bass.ds(col + P * (slot // 2), P)], P)

            def dma(out, in_, sm):
                sp.dma_start(out, in_).then_inc(sm, 16)

            load_first(0)
            load_first(1)
            load_tokens(1)
            load_first(2)
            load_first(3)
            load_tokens(2)
            load_tokens(3)
            dma(dwt[:], kp(io["w_in"])[:, :, C_DT:C_DT + NH], s.par_in)
            for j in range(4):
                dma(cvw[:, :, j], io["ssd_conv_w"][j].rearrange("(k p) -> p k", p=P), s.par_in)
            dma(cvb[:], io["ssd_conv_b"].rearrange("(k p) -> p k", p=P), s.par_in)
            for j in range(3):
                dma(scw[:, :, j], io["sc_conv_w"][j].rearrange("(k p) -> p k", p=P), s.par_in)
            for i, g in enumerate(("s5_d", "s5_b_glu", "pool_scale")):
                dma(c4[:, i + 1, :], io[g].rearrange("(k p) -> p k", p=P), s.par_in)
            for hh in range(2):
                dma(c4[64 * hh:64 * hh + 64, 0, :],
                    io["ssd_d"].rearrange("(a i h) -> a h i", a=1, h=2)[:, hh, :].to_broadcast([64, 4]), s.par_in)
            dma(dtb[:, 0:1], io["ssd_dt_bias"].rearrange("(h a) -> h a", a=1), s.par_in)
            dma(dtb[:, 1:2], io["ssd_a_log"].rearrange("(h a) -> h a", a=1), s.par_in)
            for i, g in enumerate(("s5_lam_re", "s5_lam_im")):
                for hh in range(2):
                    dma(s5p[64 * hh:64 * hh + 64, 3 + i, :], io[g].rearrange("(i h) n -> h n i", h=2)[hh], s.par_in)
            for hh in range(2):
                dma(s5p[64 * hh:64 * hh + 64, 5, :],
                    io["s5_log_dt"].rearrange("(a i h) -> a h i", a=1, h=2)[:, hh, :].to_broadcast([64, NST]), s.par_in)
            for i in range(2):
                sp.dma_start(mnat[:, i, :], io["mem"][P * i:P * i + P, :]).then_inc(s.mem_in, 16)
            with sp.Fori(1, 10) as p:
                load_pair(p, io["w_in"], 256 * p + C_U5)
            with sp.Fori(0, 5) as p:
                load_pair(p + 10, io["w_in"], 256 * p)
            for m, w in enumerate(("w_v", "w_k")):
                with sp.Fori(0, 4) as b:
                    for u in range(8):
                        load(2 * b + (T_KV + 8 * m + u // 4), u % 4,
                             kp(io[w])[:, 2 * u:2 * u + 2, bass.ds(512 * b, 512)], 512)
            for p in range(8):
                load_pair(p + T_OUT, io["w_out"], 256 * p, 0, 1)

            def load_piece(hd, i):
                n = 16 * hd + i
                kv, b = i // NS, i % NS
                if n >= 4:
                    j = n - 4
                    if (j % 16) < NS:
                        sp.wait_ge(s.ss_ev, NS * (j // 16) + j % 16 + 1)
                    else:
                        sp.wait_ge(s.spv, NS * (j // 16) + j % 16 - NS + 1)
                else:
                    sp.wait_ge(s.split_lo, 32 + 16)
                src = io["cache_k" if kv == 0 else "cache_v"][b].rearrange("(m p) n -> p m n", p=P)
                sp.dma_start(piece[:, n % 4, :, :], src[:, :, XAD * hd:XAD * hd + XAD]).then_inc(pc_in[n % 4], 16)

            load_pair(T_Q, io["w_q"], 0)
            load_pair(T_Q + 1, io["w_q"], 256)
            load_pair(T_Q + 2, io["w_q"], 512)
            for hd in range(XAH):
                for i in range(4):
                    load_piece(hd, i)
                if hd < XAH - 1:
                    T, w, c0 = T_Q + 2 * hd + 3, io["w_q"], 512 * hd + 768
                    load_slots(T, w, c0, (0, 1))
                    load_piece(hd, 4)
                    load_piece(hd, 5)
                    load_slots(T, w, c0, (2,))
                    load_piece(hd, 6)
                    load_piece(hd, 7)
                    load_slots(T, w, c0, (3,))
                else:
                    for i in range(4, 8):
                        load_piece(hd, i)
                for i in range(8, 12):
                    load_piece(hd, i)
                if hd < XAH - 2:
                    load_pair(T_Q + 2 * hd + 4, io["w_q"], 512 * hd + 1024)
                elif hd == XAH - 2:
                    load_pair(T_O, io["w_o"], 0)
                for i in range(12, 16):
                    load_piece(hd, i)
            with sp.Fori(1, 8) as p:
                load_pair(p + T_O, io["w_o"], 256 * p)
            with sp.Fori(0, N_CHUNK) as c:
                with sp.Fori(0, 8) as p:
                    load_pair(16 * c + p + T_MLP, io["w_up"], 2048 * c + 256 * p)
                with sp.Fori(0, 8) as p:
                    load_pair(16 * c + p + (T_MLP + 8), io["w_down"], 256 * p, 16 * c)
            for c in range(4):
                sp.wait_ge(s.f_nat, copied(4 * c + 3))
                w = slice(512 * c, 512 * c + 512)
                dma(outs["y_prompt"].rearrange("(t p) n -> p t n", p=P)[:, :, w], ynat[:, 0:4, w], s.out_st)
                dma(outs["y_sample"][:, w], ynat[0:NS, 4, w], s.out_st)
            sp.wait_ge(s.out_st, 16 * N_OUT)

        @block.gpsimd
        def _(pool):
            step = Steps(pool, s.pool_own)

            def lo_unit(T, slot):
                pool.wait_ge(s.w_hi, 4 * T + slot + 1)
                pool.tensor_tensor(wlo[:, slot, :], raw[:, slot % 2, :], whi[:, slot, :].bitcast(F32),
                                   ALU.subtract).then_inc(s.w_lo, 1)

            def lo_first(pos):
                pool.wait_ge(s.w_hi, pos + 1)
                pool.tensor_tensor(wlo[:, FIRST[pos], :], raw[:, pos % 2, :], whi[:, FIRST[pos], :].bitcast(F32),
                                   ALU.subtract).then_inc(s.w_lo, 1)

            def lo_turn(T):
                for slot in range(4):
                    lo_unit(T, slot)

            def table(st):
                if st == 0:
                    pool.wait_ge(s.s5_ev, 1)
                    pool.wait_ge(s.mem_lo, KT)
                if st >= 2:
                    pool.wait_ge(s.s5_h, st - 1)
                c, sn = (tab[:, st % 2, i, :].rearrange("p (m r) -> p m r", r=32) for i in range(2))
                t = ptmp[:, :].rearrange("p (m r) -> p m r", r=32)
                hc, hs = (ehi[:, i, st, :].unsqueeze(2).to_broadcast([P, 16, 32]) for i in range(2))
                lc, ls = (elo[:, i, st, :].unsqueeze(1).to_broadcast([P, 16, 32]) for i in range(2))
                step(pool.tensor_tensor(c, hc, lc, ALU.mult))
                step(pool.tensor_tensor(t, hs, ls, ALU.mult))
                step(pool.tensor_tensor(c, c, t, ALU.subtract))
                step(pool.tensor_tensor(sn, hs, lc, ALU.mult))
                step(pool.tensor_tensor(t, hc, ls, ALU.mult))
                step(pool.tensor_tensor(sn, sn, t, ALU.add), s.tab_rdy)

            step(pool.memset(ssq[:], 0.0))
            lo_first(0)
            lo_first(1)
            for k in range(KT):
                pool.wait_ge(s.sq_done, k + 1)
                step(pool.tensor_tensor(ssq[:], ssq[:], sqt[:], ALU.add), s.ss_done)
                if k < 2:
                    lo_first(2 + k)
            for T in range(1, 4):
                lo_turn(T)
            table(0)
            table(1)
            for n in range(8, 52):
                lo_unit(2 + n // 4, n % 4)
                if n - 4 in S5_AT and S5_AT.index(n - 4) + 2 < NST:
                    table(S5_AT.index(n - 4) + 2)
            with pool.Fori(T_KV, T_END) as T:
                lo_turn(T)

        @block.scalar
        def _(act):
            step = Steps(act, s.act_own)

            def hi_units(first, last, T0=T_KV):
                for g in range(first, last):
                    slot, n = g % 4, 4 * T0 + g
                    act.wait_ge(raw_rdy[slot % 2], 16 * (n // 2 + 1))
                    act.wait_ge(s.pe_unit, n - 3)
                    act.activation(whi[:, slot, :], raw[:, slot % 2, :], ACT.Copy).then_inc(s.w_hi, 1)

            def hi_first(pos):
                act.wait_ge(raw_rdy[pos % 2], 16 * (pos // 2 + 1))
                act.activation(whi[:, FIRST[pos], :], raw[:, pos % 2, :], ACT.Copy).then_inc(s.w_hi, 1)

            def hi_turn(T):
                hi_slots(T, range(4))

            def hi_slots(T, slots):
                for slot in slots:
                    act.wait_ge(raw_rdy[slot % 2], 32 * T + 16 * (slot // 2 + 1))
                    act.wait_ge(s.pe_unit, 4 * T + (slot - 3))
                    act.activation(whi[:, slot, :], raw[:, slot % 2, :], ACT.Copy).then_inc(s.w_hi, 1)

            def dma(out, in_, sm):
                act.dma_start(out, in_).then_inc(sm, 16)

            dma(idn[:], consts_ap[:, 0:128], s.cst_in)
            for i, g in enumerate(("norm_mix_g", "mix_out_g", "norm_xa_g", "norm_mem_g", "norm_mlp_g", "final_norm_g")):
                dma(gains[:, i, :], io[g].rearrange("(k p) -> p k", p=P), s.gain_in if i else s.gmix_in)
            dma(ones[:], consts_ap[:, 128:256], s.cst2_in)
            dma(causal[:], consts_ap[:, 256:384], s.cst2_in)
            dma(mks[:], consts_ap[:, 384:496], s.cst2_in)

            def split_tile(n, k, src, g):
                act.activation(mov[n // KT][:, k, :], src, ACT.Copy, scale=gains[:, g, k:k + 1]).then_inc(s.split_hi, 1)
                if n >= 1:
                    act.wait_ge(s.ss_done, n)
                act.activation(sqt[:], src, ACT.Square).then_inc(s.sq_done, 1)

            mov = {0: xh}
            act.wait_ge(s.gmix_in, 16)
            for k in range(KT):
                for pos in ((0, 1), (2,), (3,))[k] if k < 3 else ():
                    hi_first(pos)
                if k == 12:
                    act.wait_ge(s.par_in, 16 * N_PAR)
                    act.activation(dwh[:], dwt[:], ACT.Copy).then_inc(s.dt_hi, 1)
                act.wait_ge(s.x_ev, k + 1)
                split_tile(k, k, xT[:, k, :], 0)
            act.wait_ge(s.x_ev, KT)
            dma(xscr, xT[:], s.xs_st)

            def root(n):
                act.wait_ge(s.inv_done, n + 1)
                act.activation(rB[:], rB[:], ACT.Sqrt).then_inc(s.r_ready, 1)

            act.wait_ge(s.gain_in, 16 * 5)
            hi_slots(1, (0,))
            root(0)
            hi_slots(1, (1, 2, 3))
            act.wait_ge(s.x_tr, KT)
            for i, g in enumerate(("s5_b_re", "s5_b_im")):
                dma(bnat[:, i, :, :], io[g].rearrange("(i h) n k -> (h n) i k", h=2), s.s5_in)
            for i, g in enumerate(("s5_c_re", "s5_c_im")):
                dma(cnat[:, i, :, :], io[g].rearrange("(f g) k n -> (g k) f n", f=4), s.s5_in)
            act.wait_ge(s.xs_st, 16)
            act.wait_ge(s.ss_done, KT)
            act.wait_ge(s.split_lo, KT)
            for i, g in enumerate(("state_s5_re", "state_s5_im")):
                dma(s5nat[:, i, :], io[g], s.st_in)
            dma(cvnat[:], io["state_ssd_conv"], s.st_in)
            dma(scnat[:], io["state_sconv"], s.st_in)
            dma(plnat[:], io["state_pool"], s.st_in)
            act.wait_ge(s.s5_ask, 1)
            act.activation(s5p[:, 5, :], s5p[:, 5, :], ACT.Exp).then_inc(s.s5_act, 1)
            act.wait_ge(s.s5_ask, 2)
            act.activation(s5p[:, 0, :], sm[:, 0, :], ACT.Exp).then_inc(s.s5_act, 1)
            act.wait_ge(s.s5_ask, 3)
            act.activation(ang[:, 1, :, :], ang[:, 0, :, :], ACT.Sin).then_inc(s.s5_act, 1)
            act.activation(ang[:, 2, :, :], ang[:, 0, :, :], ACT.Sin, scale=0.5).then_inc(s.s5_act, 1)
            hi_turn(2)
            act.wait_ge(s.mem_in, 32)
            for i in range(2):
                step(act.activation(xnat[:, 4, :], mnat[:, i, :], ACT.Square, accum_out=rmem[:, i:i + 1]), s.mem_sq)
            act.wait_ge(s.mem_inv, 1)
            act.activation(rmem[:, 2:4], rmem[:, 2:4], ACT.Sqrt).then_inc(s.mem_r, 1)
            hi_slots(3, (0,))
            act.wait_ge(s.s5_ev, 1)
            for k in range(KT):
                if k in (4, 8, 12):
                    hi_slots(3, (k // 4,))
                act.wait_ge(s.mem_tr, k + 1)
                act.activation(memh[:, k, :], aux[:, k % 2, 0:NMEM], ACT.Copy,
                               scale=gains[:, 3, k:k + 1]).then_inc(s.mem_hi, 1)

            def store_u(T):
                for t in (2 * T, 2 * T + 1):
                    act.wait_ge(s.tile_free, t + 1)
                    src = stg[:, t % 2, :] if t >= 6 else (sqt[:], ssq[:])[t % 2]
                    dma(uscr[in_row(t):in_row(t) + P, :], src, pj[t % 2])

            def kv_store(b):
                act.wait_ge(s.tile_free, O_KV + b + 1)
                dst = outs["p_mem_v" if b < 4 else "p_mem_k"].rearrange("(m p) n -> p m n", p=P)
                dma(dst[:, :, 512 * (b % 4):512 * (b % 4) + 512], kvst[:, b % 2, :, :], kv_out[b % 2])

            for T in range(3, T_KV + 1):
                if T > 3:
                    hi_turn(T)
                store_u(T - 1)
                if T == 5:
                    act.wait_ge(s.dt_ask, 1)
                    act.activation(dte[:, 1, :], dte[:, 1, :], ACT.Exp).then_inc(s.dt_act, 1)
                    act.activation(dtb[:, 2:3], dtb[:, 1:2], ACT.Exp).then_inc(s.dt_act, 1)
            for i in range(2):
                act.wait_ge(pj[i], 16 * 13)

            def load_conv(i):
                dma(xb[:, i, 3:3 + TOK], uscr[C_XBC + P * i:C_XBC + P * i + P, :], cv_in[i // 3])

            def load_short(i):
                for j, c0 in enumerate((C_C, C_HV, C_B)):
                    o = 2 if j == 0 else 0
                    dma(scb[:, i % 2, j, o:o + TOK], uscr[c0 + P * i:c0 + P * i + P, :], sc_in[i % 2])

            def load_pool(i):
                dma(pu[:, i % 2, PH:PH + TOK], uscr[C_POOL + P * i:C_POOL + P * i + P, :], pu_in[i % 2])

            def load_z(i):
                dma(zt[:, i % 2, :], uscr[C_Z + P * i:C_Z + P * i + P, :], z_in[i % 2])

            for i in range(6):
                load_conv(i)
            load_short(0)
            load_short(1)
            hi_units(4, 6)
            act.wait_ge(s.s5_y, 4)
            for i in range(4):
                act.activation(y[:, 4 + i, :], y[:, 4 + i, :], ACT.Gelu_apprx_tanh).then_inc(s.glu_act, 1)
            act.wait_ge(s.s5_fin, 1)
            dma(wglu[:], kp(io["s5_w_glu"]), s.glu_in)
            dma(selG[:], consts_ap[0:8, 512:1024].rearrange("k (j m) -> k j m", j=4), s.sel_in)
            act.wait_ge(s.dt_ask, 2)
            for c in range(NC):
                act.activation(dtw[:, 4, CH * c:CH * c + CH], dtw[:, 3, CH * c:CH * c + CH], ACT.Exp, scale=-1.0,
                               bias=dtw[:, 3, CH * c + CH - 1:CH * c + CH]).then_inc(s.dt_act, 1)
            act.activation(sde[:, 0:8], sde[:, 0:8], ACT.Exp).then_inc(s.dt_act, 1)
            dma(plw[:], io["pool_w"].rearrange("g c d -> c g d"), s.pl_in)
            load_pool(0)
            load_pool(1)
            hi_units(6, 7)
            for i in range(6):
                act.wait_ge(s.cv_acc, i + 1)
                act.activation(xc[:, i, :], xc[:, i, :], ACT.Silu).then_inc(s.cv_act, 1)
                if 1 <= i <= 4:
                    act.wait_ge(s.glu_mm, i)
                    act.activation(halves(sig[:, i - 1, :]), aux[:, 2 * ((i - 1) % 2):2 * ((i - 1) % 2) + 2, 0:HALF],
                                   ACT.Sigmoid, bias=c4[:, 2, i - 1:i]).then_inc(s.glu_sig, 1)
                hi_units(7 + i, 8 + i)
            act.wait_ge(s.cv_act, 6)
            for k in range(4):
                dma(zscr[:, P * k:P * k + P].rearrange("b p -> p b"), xc[:, k, SEQ:TOK], s.ss_st)
            for k in range(2):
                dma(bscr[:, k, :].rearrange("b p -> p b"), xc[:, 4 + k, SEQ:TOK], s.ss_st)
            act.wait_ge(s.dt_done, 1)
            for j, rows in enumerate((sde[:, 0:8], dtw[:, 2, SEQ:TOK])):
                dma(dscr[64 * j:64 * j + 64].rearrange("(b h) -> h b", h=8), rows, s.ss_st)
            hi_units(13, 14)
            act.wait_ge(s.sc_done, 1)
            load_short(2)
            hi_units(14, 16)
            act.wait_ge(s.sc_done, 2)
            load_short(3)
            hi_units(16, 17)
            hi_units(17, 18)

            def load_rows(first, last):
                for n in range(first, last):
                    f, hd = n // NH, n % NH
                    g = hd // 4
                    dma(r64[64 * f + hd:64 * f + 64:NH, 32:160].rearrange("b (j n) -> b j n", j=2),
                        bscr[:, :, 64 * g:64 * g + 64], s.ss_in)

            for j in range(4):
                act.wait_ge(s.ea_mm, j + 1)
                if j >= 2:
                    act.wait_ge(s.cj_ev, j - 1)
                act.activation(gm[:, j % 2, :], aux[:, 2 + j % 2, :], ACT.Exp).then_inc(s.ea_act, 1)
                if j >= 1:
                    hi_units(17 + j, 18 + j)
            kv_store(0)
            act.wait_ge(s.glu_y, 1)
            act.wait_ge(s.ss_st, 16 * 8)
            for f in range(2):
                rows = slice(64 * f, 64 * f + 64)
                dma(hs[rows, :, :], io["state_ssd"].rearrange("b h (p n) -> (b h) p n", n=64)[:, 32 * f:32 * f + 32, :],
                    s.ss_s)
                dma(r64[rows, 0:32], zscr.rearrange("b (h p) -> (b h) p", h=NH)[:, 32 * f:32 * f + 32], s.ss_in)
                for j in range(2):
                    dma(s64[rows, j:j + 1], dscr[64 * j:64 * j + 64].rearrange("(p a) -> p a", a=1), s.ss_in)
            hi_units(21, 23)
            kv_store(1)
            load_rows(0, 5)
            for i in (2, 3):
                act.wait_ge(s.mx_pool, i - 1)
                load_pool(i)
                hi_units(19 + 2 * i, 21 + 2 * i)
            hi_units(27, 28)
            load_rows(5, 11)
            hi_units(28, 30)
            load_rows(11, 16)
            act.wait_ge(s.pl_ev, 4)
            load_z(0)
            load_z(1)
            kv_store(2)

            def norm_squares(j, ready, count):
                act.wait_ge(ready, count)
                for i in range(4):
                    act.wait_ge(s.ss_done, KT + 4 * j + max(i - 1, 0))
                    act.activation((sqt, hsq)[i % 2][:], y[:, 4 * NORM_ORDER[j] + i, :], ACT.Square).then_inc(s.sq_done, 1)

            norm_squares(0, s.glu_y, 1)
            hi_units(30, 33)
            root(1)
            hi_units(33, 34)
            norm_squares(1, s.sc_done, 4)
            hi_units(34, 36)
            root(2)
            hi_units(36, 37)
            norm_squares(2, s.pl_ev, 4)
            hi_units(37, 39)
            root(3)
            kv_store(3)
            hi_units(39, 47)
            kv_store(4)
            hi_units(47, 49)

            def sample_rows(step_):
                if step_ == 0:
                    act.wait_ge(s.ss_y, 1)
                    for f in range(2):
                        dma(yscr.rearrange("b h p -> (b h) p")[:, 32 * f:32 * f + 32], y64[64 * f:64 * f + 64, :], s.ss_yst)
                elif step_ == 1:
                    for f in range(2):
                        dma(outs["s_ssd"].rearrange("b h (p n) -> (b h) p n", n=64)[:, 32 * f:32 * f + 32, :],
                            hs[64 * f:64 * f + 64, :, :], s.ss_out)
                else:
                    act.wait_ge(s.ss_yst, 32)
                    for k in (2 * step_ - 4, 2 * step_ - 3):
                        for hh in range(2):
                            dma(y[64 * hh:64 * hh + 64, k, SEQ:TOK], yscr[:, 2 * k + hh, :].rearrange("b p -> p b"), s.ss_yin)

            for hd in range(NH):
                act.wait_ge(s.g_pre, hd + 1)
                act.activation(gm[:, hd % 2, :], gm[:, hd % 2, :], ACT.Exp).then_inc(s.g_exp, 1)
                if hd % 2 == 0:
                    i = hd // 2
                    if i >= 2:
                        act.wait_ge(s.z_use, i - 1)
                        load_z(i)
                    act.wait_ge(z_in[i % 2], 16 * (i // 2 + 1))
                    act.activation(zt[:, i % 2, :], zt[:, i % 2, :], ACT.Silu).then_inc(s.z_act, 1)
                hi_units(49 + 2 * hd, 51 + 2 * hd - (hd == 7))
                if 1 <= hd <= 4:
                    sample_rows(hd - 1)
                if hd == 3:
                    kv_store(5)
            norm_squares(3, s.y_fin, 1)
            hi_units(64, 65)

            def mix_hi(k):
                act.activation(mixh[:, k, :], y[:, k, :], ACT.Copy).then_inc(s.split_hi, 1)

            for k in OUT_ORDER[0:4]:
                mix_hi(k)
            hi_units(65, 67)
            root(4)
            for k in OUT_ORDER[4:8]:
                mix_hi(k)
            kv_store(6)
            kv_store(7)
            for k in OUT_ORDER[8:12]:
                mix_hi(k)
            hi_units(67, 68)
            for i in range(2):
                act.wait_ge(kv_out[i], 16 * 4)
            for i in range(4):
                act.wait_ge(s.mixn, 12 + i + 1)
                mix_hi(i)
            act.wait_ge(s.split_lo, KT + 8)
            dma(h[:, 8:16, :], xscr[:, 8:16, :], s.h_in)
            act.wait_ge(s.split_lo, KT + 12)
            dma(h[:, 4:8, :], xscr[:, 4:8, :], s.h_in)
            act.wait_ge(s.ps_ev, 1)
            dma(outs["p_ssd"].rearrange("(i q) n -> q i n", q=P), pst[:], s.ss_out)
            act.wait_ge(s.split_lo, 2 * KT)
            dma(h[:, 0:4, :], xscr[:, 0:4, :], s.h_in)
            act.wait_ge(s.ss_out, 16 * 3)

            def residual_pair(m, n, t, mo, g):
                for i in range(2):
                    act.wait_ge(s.tile_free, t + (i + 1))
                    act.wait_ge(s.ss_done, n + i)
                    src = flat(h)[:, bass.ds(TOK * (m + i), TOK)]
                    act.activation(flat(mo)[:, bass.ds(TOK * (m + i), TOK)], src, ACT.Copy,
                                   scale=gains[:, g, bass.ds(m + i, 1)]).then_inc(s.split_hi, 1)
                    act.activation(sqt[:], src, ACT.Square).then_inc(s.sq_done, 1)

            with act.Fori(0, 8) as p:
                hi_turn(p + (T_OUT + 1))
                residual_pair(2 * p, 2 * p + 2 * KT, 2 * p + O_OUT, ah, 2)
            def load_keys(hd):
                dma(kNh[:], outs["p_mem_k"].rearrange("(m p) n -> p m n", p=P)[:, :, XAD * hd:XAD * hd + XAD], s.kh_in)

            def load_values(hd):
                dma(vNh[:], outs["p_mem_v"].rearrange("(m p) n -> p m n", p=P)[:, :, XAD * hd:XAD * hd + XAD], s.vh_in)

            root(5)
            hi_turn(T_Q + 1)
            load_keys(0)
            load_values(0)
            hi_turn(T_Q + 2)
            def o_hi(first, last):
                for k in range(first, last):
                    act.activation(oh[:, k, :], q[:, k, :], ACT.Copy).then_inc(s.oh_hi, 1)

            def store_states(part):
                if part == 0:
                    for i in range(3):
                        dma(outs["p_ssd_conv"][i:i + 1, :],
                            uscr[C_XBC:C_XBC + 768, SEQ - 3 + i:SEQ - 2 + i].rearrange("f a -> a f"), s.out_st)
                    for b in range(NS):
                        dma(outs["s_ssd_conv"][3 * b + 2:3 * b + 3, :],
                            uscr[C_XBC:C_XBC + 768, SEQ + b:SEQ + b + 1].rearrange("f a -> a f"), s.out_st)
                        dma(outs["s_ssd_conv"][3 * b:3 * b + 2, :], io["state_ssd_conv"][3 * b + 1:3 * b + 3, :], s.out_st)
                elif part == 1:
                    for b in range(NS):
                        dma(outs["s_pool"][PH * b + PH - 1:PH * b + PH, :],
                            uscr[C_POOL:C_POOL + GW, SEQ + b:SEQ + b + 1].rearrange("f a -> a f"), s.out_st)
                        dma(outs["s_pool"][PH * b:PH * b + PH - 1, :], io["state_pool"][PH * b + 1:PH * b + PH, :], s.out_st)
                    for i in range(PH):
                        dma(outs["p_pool"][i:i + 1, :],
                            uscr[C_POOL:C_POOL + GW, SEQ - PH + i:SEQ - PH + i + 1].rearrange("f a -> a f"), s.out_st)
                elif part == 2:
                    for i, n in enumerate(("s5_re", "s5_im")):
                        for hh in range(2):
                            for j in range(NS + 1):
                                dst = outs["p_" + n][:, :] if j == NS else outs["s_" + n][32 * j:32 * j + 32, :]
                                dma(dst.rearrange("(i h) n -> h n i", h=2)[hh], s5o[64 * hh:64 * hh + 64, i, :, j], s.out_st)
                else:
                    for j in range(10):
                        dst = outs["p_sconv"][j:j + 1, :] if j < 2 else outs["s_sconv"][2 * j - 3:2 * j - 2, :]
                        dma(dst.rearrange("a (k p) -> p k a", p=P), scn[:, :, j:j + 1], s.out_st)
                    for b in range(NS):
                        dma(outs["s_sconv"][2 * b:2 * b + 1, :], io["state_sconv"][2 * b + 1:2 * b + 2, :], s.out_st)

            for hd in range(XAH):
                last = hd == XAH - 1
                W = 8 * hd + 12
                if last:
                    act.wait_ge(s.pe_unit, 4 * T_O)
                for tt in range(4):
                    n = 4 * hd + tt
                    if not last:
                        hi_units(W + tt, W + tt + 1, T_Q)
                    act.wait_ge(s.p_ask, n + 1)
                    act.activation(pr[:], aux[:, 2, 0:NMEM], ACT.Exp, scale=SCALE,
                                   bias=smx[:, 1:2], accum_out=smx[:, 2:3]).then_inc(s.p_exp, 1)
                    if tt == 0 and not last:
                        act.wait_ge(s.kt_tr, hd + 1)
                        load_keys(hd + 1)
                    if last:
                        o_hi(3 * tt, 3 * tt + 3)
                store_states(hd)
                if not last:
                    hi_units(W + 4, W + 6, T_Q)
                act.wait_ge(s.sp_ask, hd + 1)
                act.activation(prs[:], aux[0:NS, 2, 0:NMEM], ACT.Exp, scale=SCALE, bias=smx[0:NS, 5:6],
                               accum_out=smx[0:NS, 6:7]).then_inc(s.sp_exp, 1)
                if not last:
                    act.wait_ge(s.pv, 4 * hd + 4)
                    load_values(hd + 1)
                    hi_units(W + 6, W + 8, T_Q)
            act.wait_ge(s.so_ev, XAH)
            o_hi(12, KT)
            with act.Fori(0, 8) as p:
                hi_turn(p + (T_O + 1))
                residual_pair(2 * p, 2 * p + 3 * KT, 2 * p + O_O, mh, 4)
            root(6)

            def up_pair(c, p):
                hi_turn(16 * c + p + (T_MLP + 1))
                for i in range(2):
                    act.wait_ge(s.tile_free, 32 * c + 2 * p + (O_MLP + i + 1))
                    step(act.activation(hsq[:], upr[:], ACT.Square), s.up_sq)
                    act.activation(fh[:, bass.ds(2 * p + i, 1), :], hsq[:], ACT.Copy).then_inc(s.hid_hi, 1)

            with act.Fori(0, N_CHUNK - 1) as c:
                step.enter(c, [(s.up_sq, 16)])
                with act.Fori(0, 8) as p:
                    step.enter(p, [(s.up_sq, 2)])
                    up_pair(c, p)
                step.leave(8)
                with act.Fori(0, 8) as p:
                    hi_turn(16 * c + p + (T_MLP + 9))
            step.leave(N_CHUNK - 1)
            with act.Fori(0, 8) as p:
                step.enter(p, [(s.up_sq, 2)])
                up_pair(N_CHUNK - 1, p)
            step.leave(8)
            L = 16 * (N_CHUNK - 1)

            def last_pair(p):
                for i in range(2):
                    act.wait_ge(s.tile_free, 2 * p + (O_MLP + 32 * (N_CHUNK - 1) + 16 + i + 1))
                    act.wait_ge(s.ss_done, 2 * p + (4 * KT + i))
                    act.activation(sqt[:], flat(h)[:, bass.ds(TOK * (2 * p + i), TOK)], ACT.Square).then_inc(s.sq_done, 1)

            with act.Fori(0, 7) as p:
                hi_turn(p + (T_MLP + L + 9))
                last_pair(p)
            last_pair(7)
            root(7)
            for k in range(KT):
                act.wait_ge(s.f_tr, k + 1)
                step(act.activation(ynat[:, 0:4, P * k:P * k + P],
                                    aux[:, 2 * (k % 2), :].rearrange("p (t n) -> p t n", t=4), ACT.Copy), s.f_nat)
                if k % 4 == 3:
                    c0 = P * (k - 3)
                    step(act.activation(ynat[0:NS, 4, c0:c0 + 512], aux[0:NS, 1 + 2 * (k // 4 % 2), :], ACT.Copy), s.f_nat)

        @block.tensor
        def _(pe):
            step = Steps(pe, s.pe_own)

            def out_unit(T, i, half, t, hi, lo, ready, order):
                if half == 0 and not (isinstance(t, int) and t < 2):
                    pe.wait_ge(s.tile_free, t - 1)
                slot = 2 * i + half
                pe.wait_ge(s.w_lo, 4 * T + slot + 1)
                for n in range(8 * half, 8 * half + 8):
                    k = order[n]
                    if ready is not None and i == 0:
                        pe.wait_ge(ready[0], ready[1] + (n + 1))
                    wh = whi[:, slot, P * (k % 8):P * (k % 8) + P]
                    wl = wlo[:, slot, P * (k % 8):P * (k % 8) + P]
                    for part, (w, m) in enumerate(((wh, hi), (wh, lo), (wl, hi))):
                        for f in range(2):
                            mm = pe.matmul(lin[:, 2 * i + f, 0:HALF], w, m[:, k, HALF * f:HALF * f + HALF],
                                           start=(n == 0 and part == 0), stop=(n == KT - 1 and part == 2))
                mm.then_inc(s.pe_unit, 1)

            def out_tile(T, i, t, hi, lo, ready, order=range(KT)):
                for half in range(2):
                    out_unit(T, i, half, t, hi, lo, ready, order)

            def pair(T, t, hi, lo, ready=None, order=range(KT)):
                out_tile(T, 0, t, hi, lo, ready, order)
                out_tile(T, 1, t + 1, hi, lo, ready, order)

            def statistics(n, count, bank):
                pe.wait_ge(s.ss_done, count)
                for f in range(2):
                    mm = pe.matmul(aux[:, bank + f, 0:HALF], ones[:], ssq[:, HALF * f:HALF * f + HALF],
                                   start=True, stop=True)
                mm.then_inc(s.stat_mm, 1)

            pe.wait_ge(s.cst_in, 16)
            pe.wait_ge(x_in[4], 16)
            for k in range(KT + 2):
                if k < KT:
                    if k % 4 == 0:
                        pe.wait_ge(x_in[k // 4], 16)
                    if k >= 2:
                        pe.wait_ge(s.x_ev, k - 1)
                    b = 2 * (k % 2)
                    for i in range(4):
                        pe.transpose(aux[:, b, P * i:P * i + P], xnat[:, i, P * k:P * k + P], idn[:])
                    pe.transpose(aux[:, b + 1, 0:NS], xnat[0:NS, 4, P * k:P * k + P], idn[0:NS, 0:NS]).then_inc(s.x_tr, 1)
                kk = k - 2
                if kk == 0:
                    pe.wait_ge(s.w_lo, 2)
                if kk == 8:
                    pe.wait_ge(s.w_lo, 4)
                if kk >= 0:
                    pe.wait_ge(s.split_lo, kk + 1)
                    for i in range(2):
                        slot = 2 * i + kk // 8
                        wh = whi[:, slot, P * (kk % 8):P * (kk % 8) + P]
                        wl = wlo[:, slot, P * (kk % 8):P * (kk % 8) + P]
                        for part, (w, m) in enumerate(((wh, xh), (wh, xl), (wl, xh))):
                            for f in range(2):
                                mm = pe.matmul(lin[:, 2 * i + f, 0:HALF], w, m[:, kk, HALF * f:HALF * f + HALF],
                                               start=(kk == 0 and part == 0), stop=(kk == KT - 1 and part == 2))
                        if kk == 7 and i == 0:
                            mm.then_inc(s.pe_unit, 1)
                        if kk == 15:
                            mm.then_inc(s.pe_unit, i + 1)
            pe.wait_ge(s.cst2_in, 48)
            statistics(0, KT, 2)
            pe.wait_ge(s.dt_lo, 1)
            for kk in range(KT):
                for n, (w, m) in enumerate(((dwh, xh), (dwh, xl), (dwl, xh))):
                    for f in range(2):
                        mm = pe.matmul(aux[0:NH, f, 0:HALF], w[:, kk, :], m[:, kk, HALF * f:HALF * f + HALF],
                                       start=(kk == 0 and n == 0), stop=(kk == KT - 1 and n == 2))
            mm.then_inc(s.dt_mm, 1)
            pair(1, 2, xh, xl)

            def s5_in(st):
                f, r = st // 4, 32 * (st % 4)
                if st == 0:
                    pe.wait_ge(s.mem_lo, KT)
                    pe.wait_ge(s.tile_free, 4)
                else:
                    pe.wait_ge(s.s5_rot, st)
                for c in range(2):
                    pe.matmul(aux[:, c, :], bT[r:r + 32, c, f, :], u5[r:r + 32, f, 0:SEQ], start=True, stop=True)
                    mm = pe.matmul(aux[:, 3, 8 * c:8 * c + 8], bT[r:r + 32, c, f, :], u5[r:r + 32, f, SEQ:TOK],
                                   start=True, stop=True)
                mm.then_inc(s.s5_bu, 1)

            def s5_out(st):
                f, r = st // 4, 32 * (st % 4)
                pe.wait_ge(s.s5_h, st + 1)
                for c in range(2):
                    pe.matmul(aux[r:r + 32, 2, :], cT[:, c, f, r:r + 32], rot[:, 3 + c, :], start=(c == 0), stop=(c == 1))
                for c in range(2):
                    mm = pe.matmul(aux[r:r + 32, 3, 32:40], cT[:, c, f, r:r + 32], s5o[:, c, st, 0:NS],
                                   start=(c == 0), stop=(c == 1))
                mm.then_inc(s.s5_c, 1)

            def kv_units(first, last):
                for g in range(first, last):
                    b, u = g // 8, g % 8
                    if u == 0:
                        pe.wait_ge(s.tile_free, O_KV + b - 1)
                    slot = u % 4
                    pe.wait_ge(s.w_lo, 4 * T_KV + g + 1)
                    for j in range(2):
                        kk = 2 * u + j
                        wh, wl = whi[:, slot, 512 * j:512 * j + 512], wlo[:, slot, 512 * j:512 * j + 512]
                        for m in range(2):
                            for n, (a, w) in enumerate(((memh, wh), (meml, wh), (memh, wl))):
                                mm = pe.matmul(lin[:, 2 * (b % 2) + m, :], a[:, kk, P * m:P * m + P], w,
                                               start=(kk == 0 and n == 0), stop=(kk == KT - 1 and n == 2))
                    mm.then_inc(s.pe_unit, 1)

            def keys(hd):
                pe.wait_ge(s.kh_in, 16 * hd + 16)
                if hd == 0:
                    pe.wait_ge(s.inv_done, 6)
                else:
                    pe.wait_ge(s.o_ev, 4 * hd)
                for d in range(4):
                    for m in range(2):
                        mm = pe.transpose(aux[:, d // 2, NMEM * (d % 2) + P * m:NMEM * (d % 2) + P * m + P],
                                          kNh[:, m, P * d:P * d + P], idn[:])
                mm.then_inc(s.kt_tr, 1)

            def attention(hd):
                f0 = 4 * hd

                def unit(w):
                    if hd < XAH - 1:
                        out_unit(T_Q + 2 * hd + 2 + w // 4, w // 2 % 2, w % 2, O_Q + 4 * hd + 4 + w // 2,
                                 ah, al, None, range(KT))

                unit(0)
                pe.wait_ge(s.kt_ev, hd + 1)
                pe.wait_ge(s.tile_free, O_Q + 4 * hd + 4)

                def prob_t(tt):
                    n = 4 * hd + tt
                    pe.wait_ge(s.p_ev, n + 1)
                    if n >= 1:
                        pe.wait_ge(s.pt_ev, n)
                    for m in range(2):
                        mm = pe.transpose(aux[:, 3, P * m:P * m + P], pr[:, P * m:P * m + P], idn[:])
                    mm.then_inc(s.p_tr, 1)

                def query_rows(b):
                    if b >= 2:
                        pe.wait_ge(s.ss_ev, 8 * hd + b - 1)
                    for d in range(4):
                        mm = pe.matmul(aux[:, b % 2, P * d:P * d + P],
                                       q[:, f0 + d, SEQ + b:SEQ + b + 1].to_broadcast([P, P]), idn[:],
                                       start=True, stop=True)
                    mm.then_inc(s.qb, 1)

                for tt in range(4):
                    if tt >= 1:
                        pe.wait_ge(s.p_exp, 4 * hd + tt)
                    for d in range(4):
                        mm = pe.matmul(aux[:, 2, 0:NMEM], q[:, f0 + d, P * tt:P * tt + P],
                                       kTh[:, d, :], start=(d == 0), stop=(d == 3))
                    mm.then_inc(s.sc2, 1)
                    for b in (2 * tt, 2 * tt + 1):
                        query_rows(b)
                    unit(1 + tt)
                    if tt == 0 and hd >= 1:
                        pe.wait_ge(s.so_ev, hd)
                    prob_t(tt)
                unit(5)
                pe.wait_ge(s.pt_ev, 4 * hd + 4)
                pe.wait_ge(s.vh_in, 16 * hd + 16)
                for d in range(4):
                    k = 4 * hd + d
                    if d < 2:
                        pe.wait_ge(s.ss_ev, 8 * hd + 8)
                    else:
                        pe.wait_ge(s.o_ev, k - 1)
                    for m in range(2):
                        mm = pe.matmul(aux[:, d % 2, :], vNh[:, m, P * d:P * d + P], pT[:, m, :],
                                       start=(m == 0), stop=(m == 1))
                    mm.then_inc(s.pv, 1)
                    if d == 1:
                        pe.wait_ge(s.p_exp, 4 * hd + 4)
                        for m in range(2):
                            mm = pe.transpose(aux[0:NS, 2, P * m:P * m + P], ssc[:, m, :], idn[:])
                        mm.then_inc(s.sp_tr, 1)
                unit(6)
                pe.wait_ge(s.sp_ev, hd + 1)
                for m in range(2):
                    mm = pe.transpose(aux[:, 3, 256 + 8 * m:264 + 8 * m], prs[:, P * m:P * m + P], idn[0:NS, 0:NS])
                mm.then_inc(s.sp_tb, 1)
                unit(7)
                if hd < XAH - 1:
                    keys(hd + 1)
                pe.wait_ge(s.sp_tev, hd + 1)
                for b in range(NS):
                    n = 16 * hd + 8 + b
                    pe.wait_ge(pc_in[n % 4], 16 * (n // 4 + 1))
                    for m in range(2):
                        mm = pe.matmul(aux[0:NS, 2, :], pTd[:, m, b, :], piece[:, n % 4, m, :],
                                       start=(b == 0 and m == 0), stop=(b == NS - 1 and m == 1))
                    mm.then_inc(s.spv, 1)
                pe.wait_ge(s.po_ev, hd + 1)
                for d in range(4):
                    mm = pe.transpose(aux[:, 3, 288 + 8 * d:296 + 8 * d], po[:, P * d:P * d + P], idn[0:NS, 0:NS])
                mm.then_inc(s.so_tr, 1)

            def w_in_unit(n):
                out_unit(2 + n // 4, n // 2 % 2, n % 2, 4 + n // 2, xh, xl, None, range(KT))

            for n in range(4):
                w_in_unit(n)
            pe.wait_ge(s.st_in, 80)
            pe.wait_ge(s.dt_ev, 1)
            for i in range(6):
                pe.transpose(aux[:, 0, 24 * i:24 * i + 24], cvnat[:, P * i:P * i + P], idn[0:24, 0:24])
            for i in range(4):
                pe.transpose(aux[:, 0, 144 + 16 * i:160 + 16 * i], scnat[:, P * i:P * i + P], idn[0:16, 0:16])
            for i in range(4):
                pe.matmul(aux[:, 0, 208 + 8 * i:216 + 8 * i], plnat[:, P * i:P * i + P],
                          mks[0:NS * PH, 16 + 8 * i:24 + 8 * i], start=True, stop=True)
            for c in range(2):
                for st in range(NST):
                    mm = pe.transpose(aux[:, 1, 128 * c + 8 * st:128 * c + 8 * st + 8],
                                      s5nat[:, c, P * st:P * st + P], idn[0:NS, 0:NS])
            mm.then_inc(s.st_tr, 1)
            pe.wait_ge(s.s5_ask, 4)
            pe.wait_ge(s.inv_done, 1)
            pe.wait_ge(s.st_ev, 1)
            for c in range(2):
                for f in range(4):
                    pe.transpose(aux[:, 2 + c, P * f:P * f + P],
                                 bexp[:, c, 4 * f:4 * f + 4, :, :].rearrange("p a b c -> p (a b c)"), idn[:])
                    mm = pe.transpose(aux[:, c, P * f:P * f + P], cexp[:, c, f, :, :].rearrange("p a b -> p (a b)"), idn[:])
            mm.then_inc(s.s5_tr, 1)
            pe.wait_ge(s.mem_in, 32)
            pe.wait_ge(s.s5_ev, 1)
            for k in range(KT):
                if k >= 2:
                    pe.wait_ge(s.mem_lo, k - 1)
                for i in range(2):
                    mm = pe.transpose(aux[:, k % 2, P * i:P * i + P], mnat[:, i, P * k:P * k + P], idn[:])
                mm.then_inc(s.mem_tr, 1)

            for n in range(4, 52):
                if n in S5_AT:
                    st = S5_AT.index(n)
                    if st > 0:
                        s5_out(st - 1)
                        if st % 4 == 0:
                            pe.wait_ge(s.s5_y, st // 4)
                    s5_in(st)
                w_in_unit(n)
            s5_out(NST - 1)

            kv_units(0, 6)
            pe.wait_ge(s.glu_act, 4)
            pe.wait_ge(s.glu_in, 16)
            for i in range(4):
                if i == 2:
                    kv_units(6, 7)
                if i >= 2:
                    pe.wait_ge(s.glu_sig, i - 1)
                for f in range(2):
                    for k in range(4):
                        mm = pe.matmul(aux[:, 2 * (i % 2) + f, 0:HALF], wglu[:, k, P * i:P * i + P],
                                       y[:, 4 + k, HALF * f:HALF * f + HALF], start=(k == 0), stop=(k == 3))
                mm.then_inc(s.glu_mm, 1)
            kv_units(7, 14)
            pe.wait_ge(s.glu_sig, 4)
            pe.wait_ge(s.dt_done, 1)
            for c in range(NC):
                for j, row in enumerate((2, 5, 3)):
                    mm = pe.transpose(aux[:, 0, 32 * c + 8 * j:32 * c + 8 * j + 8],
                                      dtw[:, row, CH * c:CH * c + CH], idn[0:NH, 0:NH])
            mm.then_inc(s.tm_tr, 1)
            pe.wait_ge(s.cv_act, 6)
            for c in range(NC):
                mm = pe.transpose(aux[:, 1, P * c:P * c + P], xc[:, 4, CH * c:CH * c + CH], idn[:])
            mm.then_inc(s.tb_tr, 1)
            for g in range(2):
                r = 64 * g
                for c in range(NC):
                    mm = pe.matmul(aux[:, 2 + g, P * c:P * c + P], xc[r:r + 64, 4, CH * c:CH * c + CH],
                                   xc[r:r + 64, 5, CH * c:CH * c + CH], start=True, stop=True)
                mm.then_inc(s.sc_mm, 1)
            kv_units(14, 15)
            pe.wait_ge(s.sel_in, 16)
            for j in range(4):
                if j >= 2:
                    kv_units(13 + j, 14 + j)
                if j < 2:
                    pe.wait_ge(s.sm_ev, j + 1)
                else:
                    pe.wait_ge(s.ea_act, j - 1)
                pe.matmul(aux[:, 2 + j % 2, :], selG[:, j, :], dtw[:, 3, 0:SEQ], start=True, stop=True).then_inc(s.ea_mm, 1)
            kv_units(17, 20)
            pe.wait_ge(s.tm_ev, 1)
            pe.wait_ge(s.tb_ev, 1)
            pe.wait_ge(s.pl_in, 16)
            for i in range(4):
                pe.wait_ge(s.mx_pool, i + 1)
                if i >= 1:
                    pe.wait_ge(s.pl_ev, i)
                for f in range(2):
                    mm = pe.matmul(aux[:, f, 0:HALF], plw[:, i, :], halves(pt[:, i % 2, 0:TOK])[:, f, :],
                                   start=True, stop=True)
                mm.then_inc(s.pl_mm, 1)
                kv_units(20 + 2 * i, 22 + 2 * i)
            kv_units(28, 30)
            pe.wait_ge(s.ea_act, 4)
            statistics(1, KT + 4, 2)
            kv_units(30, 33)
            statistics(2, KT + 8, 2)
            kv_units(33, 36)
            statistics(3, KT + 12, 2)
            for c in range(NC):
                if c == 0:
                    pe.wait_ge(s.pl_ev, 4)
                for i in range(4):
                    mm = pe.transpose(aux[:, 0, P * i:P * i + P], xc[:, i, CH * c:CH * c + CH], idn[:])
                mm.then_inc(s.xt_tr, 1)
                kv_units(36 + 2 * c, 37 + 2 * c)
                pe.wait_ge(s.xt_ev, c + 1)
                if c > 0:
                    pe.wait_ge(s.h_ev, c)
                pe.matmul(aux[:, 1, :], tb[:, c, :], xde[:], start=True, stop=True).then_inc(s.cs_mm, 1)
                kv_units(37 + 2 * c, 38 + 2 * c)

            def running_sums(hd):
                if hd >= 2:
                    pe.wait_ge(s.g_pre, hd - 1)
                pe.matmul(aux[:, hd % 2, :], idn[0:NH, hd:hd + 1].to_broadcast([NH, P]), dtw[:, 3, 0:SEQ],
                          start=True, stop=True).then_inc(s.ac_mm, 1)

            pe.wait_ge(s.h_ev, 4)
            pe.wait_ge(s.cj_ev, 4)
            pe.wait_ge(s.inv_done, 4)
            running_sums(0)
            running_sums(1)
            kv_units(44, 46)
            for hd in range(NH):
                j, i, hh = hd % 4, hd // 2, hd % 2
                if 1 <= hd < NH - 1:
                    running_sums(hd + 1)
                kv_units(46 + 2 * hd - (hd == 7), 48 + 2 * hd - max(0, hd - 5))
                if hh == 0 and i >= 2:
                    pe.wait_ge(s.y_ev, i - 1)
                pe.wait_ge(s.g_ev, hd + 1)
                for c in range(NC):
                    o = aux[64 * hh:64 * hh + 64, 2 + i % 2, CH * c:CH * c + CH]
                    mm = pe.matmul(o, xdt[:, c, HD * hd:HD * hd + HD], gm[:, hd % 2, CH * c:CH * c + CH],
                                   start=True, stop=(c == 0))
                    if c > 0:
                        mm = pe.matmul(o, hst[:, c, HD * hd:HD * hd + HD], cj[:, j, CH * c:CH * c + CH],
                                       start=False, stop=True)
                mm.then_inc(s.y_mm, 1)
            kv_units(60, 63)
            pe.wait_ge(s.g_pre, 8)
            for i in range(4):
                mm = pe.transpose(aux[:, 0, P * i:P * i + P], hst[:, NC, P * i:P * i + P], idn[:])
            mm.then_inc(s.ps_tr, 1)
            pe.wait_ge(s.y_ev, 4)
            statistics(4, KT + 16, 2)
            kv_units(63, 64)

            pair(T_OUT, O_OUT, mixh, mixl, (s.split_lo, KT), OUT_ORDER)
            with pe.Fori(1, 8) as p:
                pair(p + T_OUT, 2 * p + O_OUT, mixh, mixl, None, OUT_ORDER)
            out_tile(T_Q, 0, O_Q, ah, al, (s.split_lo, 2 * KT))
            statistics(5, 3 * KT, 2)
            out_tile(T_Q, 1, O_Q + 1, ah, al, None)
            pair(T_Q + 1, O_Q + 2, ah, al)
            keys(0)
            for hd in range(XAH):
                attention(hd)
            pair(T_O, O_O, oh, ol, (s.oh_lo, 0))
            with pe.Fori(1, 8) as p:
                pair(p + T_O, 2 * p + O_O, oh, ol)
            out_tile(T_MLP, 0, O_MLP, mh, ml, (s.split_lo, 3 * KT))
            statistics(6, 4 * KT, 2)
            out_tile(T_MLP, 1, O_MLP + 1, mh, ml, None)
            with pe.Fori(1, 8) as p:
                pair(p + T_MLP, 2 * p + O_MLP, mh, ml)
            with pe.Fori(0, 8) as p:
                pair(p + (T_MLP + 8), 2 * p + (O_MLP + 16), fh, fl, (s.hid_lo, 0))
            with pe.Fori(1, N_CHUNK) as c:
                with pe.Fori(0, 8) as p:
                    pair(16 * c + p + T_MLP, 32 * c + 2 * p + O_MLP, mh, ml)
                with pe.Fori(0, 8) as p:
                    pair(16 * c + p + (T_MLP + 8), 32 * c + 2 * p + (O_MLP + 16), fh, fl, (s.hid_lo, 16 * c))
            statistics(7, 5 * KT, 2)
            for k in range(KT):
                pe.wait_ge(s.f_ev, k + 1)
                if k >= 2:
                    pe.wait_ge(s.f_nat, copied(k - 2))
                b = 2 * (k % 2)
                for i in range(4):
                    pe.transpose(aux[:, b, P * i:P * i + P], h[:, k, P * i:P * i + P], idn[:])
                pe.transpose(aux[0:NS, 1 + 2 * (k // 4 % 2), P * (k % 4):P * (k % 4) + P], h[:, k, SEQ:TOK],
                             idn[:]).then_inc(s.f_tr, 1)

        @block.vector
        def _(v):
            step = Steps(v, s.dve_own)

            def tt(out, a, b, op, sm=None):
                step(v.tensor_tensor(out, a, b, op), sm)

            def ts(out, a, s1, s2=None, op0=ALU.mult, op1=None, sm=None):
                if op1 is None:
                    step(v.tensor_scalar(out, a, s1, None, op0), sm)
                else:
                    step(v.tensor_scalar(out, a, s1, s2, op0, op1), sm)

            def stt(out, a, sc, b, op0, op1, sm=None):
                step(v.scalar_tensor_tensor(out=out, in0=a, scalar=sc, in1=b, op0=op0, op1=op1), sm)

            def cp(out, a, sm=None):
                step(v.tensor_copy(out, a), sm)

            def inverse(n, width, bank):
                v.wait_ge(s.stat_mm, n + 1)
                ts(halves(rB[:]), aux[:, bank:bank + 2, 0:HALF], 1.0 / width, EPS, ALU.mult, ALU.add)
                step(v.reciprocal(rB[:], rB[:]), s.inv_done)

            for k in range(KT + 1):
                if k == 1:
                    v.wait_ge(s.gmix_in, 16)
                if k < KT:
                    v.wait_ge(s.x_tr, k + 1)
                    cp(xT[:, k, 0:SEQ], aux[:, 2 * (k % 2), :])
                    cp(xT[:, k, SEQ:TOK], aux[:, 2 * (k % 2) + 1, 0:NS], s.x_ev)
                if k >= 1:
                    v.wait_ge(s.split_hi, k)
                    stt(xl[:, k - 1, :], xT[:, k - 1, :], gains[:, 0, k - 1:k], xh[:, k - 1, :].bitcast(F32),
                        ALU.mult, ALU.subtract, s.split_lo)
            step.n[s.ss_done] = KT
            v.wait_ge(s.par_in, 16 * N_PAR)
            v.wait_ge(s.dt_hi, 1)
            tt(dwl[:], dwt[:], dwh[:].bitcast(F32), ALU.subtract, s.dt_lo)
            inverse(0, D, 2)
            v.wait_ge(s.r_ready, 1)

            def evict_u(t):
                v.wait_ge(s.pe_unit, 2 * t + 2)
                if t < 4:
                    out = u5[:, t, :]
                elif t < 6:
                    out = (sqt[:], ssq[:])[t % 2]
                else:
                    if t >= 8:
                        v.wait_ge(pj[t % 2], 16 * ((t - 4) // 2))
                    out = stg[:, t % 2, :]
                tt(halves(out), lin_tile(t % 2), halves(rB[:]), ALU.mult, s.tile_free)

            evict_u(0)
            evict_u(1)

            v.wait_ge(s.cst2_in, 48)
            v.wait_ge(s.gain_in, 16 * 5)
            v.wait_ge(s.xs_st, 16)
            step(v.tensor_copy(sm[:, 23, :], s5p[:, 5, :]), s.s5_ask)
            v.wait_ge(s.s5_act, 1)
            tt(sm[:, 0, :], s5p[:, 3, :], s5p[:, 5, :], ALU.mult, s.s5_ask)
            tt(sm[:, 1, :], s5p[:, 4, :], s5p[:, 5, :], ALU.mult)
            for k in range(9):
                ts(ang[:, 3, k, :], sm[:, 1, :], float(2 ** k))
            a0, a3 = ang[:, 0, :, :], ang[:, 3, :, :]
            ts(a0, a3, float(1 / (2 * np.pi)), ROUND, ALU.mult, ALU.add)
            ts(a0, a0, -ROUND, None, ALU.add)
            for c in (PI2_A, PI2_B, PI2_C):
                stt(a3, a0, -c, a3, ALU.mult, ALU.add)
            ts(a0, a3, PI_IN, -PI_IN, ALU.min, ALU.max, s.s5_ask)
            v.wait_ge(s.s5_act, 4)
            tt(ang[:, 2, :, :], ang[:, 2, :, :], ang[:, 2, :, :], ALU.mult)
            ts(ang[:, 2, :, :], ang[:, 2, :, :], -2.0, 1.0, ALU.mult, ALU.add)
            tt(s5p[:, 1, :], s5p[:, 0, :], ang[:, 2, 0, :], ALU.mult)
            tt(s5p[:, 2, :], s5p[:, 0, :], ang[:, 1, 0, :], ALU.mult)
            lr, li = s5p[:, 3, :], s5p[:, 4, :]
            tt(sm[:, 2, :], lr, lr, ALU.mult)
            tt(sm[:, 3, :], li, li, ALU.mult)
            tt(sm[:, 2, :], sm[:, 2, :], sm[:, 3, :], ALU.add)
            step(v.reciprocal(sm[:, 2, :], sm[:, 2, :]))
            ts(sm[:, 4, :], s5p[:, 1, :], -1.0, None, ALU.add)
            tt(sm[:, 5, :], sm[:, 4, :], lr, ALU.mult)
            tt(sm[:, 6, :], s5p[:, 2, :], li, ALU.mult)
            tt(sm[:, 5, :], sm[:, 5, :], sm[:, 6, :], ALU.add)
            tt(sm[:, 5, :], sm[:, 5, :], sm[:, 2, :], ALU.mult)
            tt(sm[:, 6, :], s5p[:, 2, :], lr, ALU.mult)
            tt(sm[:, 7, :], sm[:, 4, :], li, ALU.mult)
            tt(sm[:, 6, :], sm[:, 6, :], sm[:, 7, :], ALU.subtract)
            tt(sm[:, 6, :], sm[:, 6, :], sm[:, 2, :], ALU.mult)
            v.wait_ge(s.s5_in, 64)
            fr, fi = (sm[:, i, :].unsqueeze(2).to_broadcast([P, NST, 16]) for i in (5, 6))
            br, bi = bnat[:, 0, :, :], bnat[:, 1, :, :]
            for (x1, x2, op), out in (((fr, fi, ALU.subtract), 0), ((fi, fr, ALU.add), 1)):
                tt(btmp[:, 0, :, :], br, x1, ALU.mult)
                tt(btmp[:, 1, :, :], bi, x2, ALU.mult)
                tt(btmp[:, 0, :, :], btmp[:, 0, :, :], btmp[:, 1, :, :], op)
                for hh in range(2):
                    ts(bexp[:, out, :, hh, :], btmp[:, 0, :, :], mks[:, 2 + hh:3 + hh])
            for c in range(2):
                for hh in range(2):
                    ts(cexp[:, c, :, hh, :], cnat[:, c, :, :], mks[:, hh:hh + 1], -1.0 if c else 1.0,
                       ALU.mult, ALU.mult, s.s5_ask if (c, hh) == (1, 1) else None)
            evict_u(2)
            evict_u(3)
            v.wait_ge(s.dt_mm, 1)
            tt(halves(dtr[:]), aux[0:NH, 0:2, 0:HALF], halves(rB[0:NH, :]), ALU.mult, s.dt_ev)

            def doubling(tabl, k0, steps):
                step(v.memset(tabl[:, 0, :, 0:1], 1.0))
                step(v.memset(tabl[:, 1, :, 0:1], 0.0))
                for k in range(steps):
                    n = 1 << k
                    c = ang[:, 2, k0 + k, :].unsqueeze(2).to_broadcast([P, NST, n])
                    sn = ang[:, 1, k0 + k, :].unsqueeze(2).to_broadcast([P, NST, n])
                    r, i = tabl[:, 0, :, 0:n], tabl[:, 1, :, 0:n]
                    t = etmp[:, 0, :, 0:n]
                    tt(tabl[:, 0, :, n:2 * n], r, c, ALU.mult)
                    tt(t, i, sn, ALU.mult)
                    tt(tabl[:, 0, :, n:2 * n], tabl[:, 0, :, n:2 * n], t, ALU.subtract)
                    tt(tabl[:, 1, :, n:2 * n], r, sn, ALU.mult)
                    tt(t, i, c, ALU.mult)
                    tt(tabl[:, 1, :, n:2 * n], tabl[:, 1, :, n:2 * n], t, ALU.add)

            doubling(elo, 0, 5)
            doubling(ehi, 5, 4)
            evict_u(4)
            evict_u(5)
            v.wait_ge(s.st_tr, 1)
            cp(convS[:].rearrange("p a b -> p (a b)"), aux[:, 0, 0:144])
            cp(scS[:].rearrange("p a b -> p (a b)"), aux[:, 0, 144:208])
            cp(plS[:].rearrange("p a b -> p (a b)"), aux[:, 0, 208:240])
            cp(h0[:].rearrange("p c a b -> p (c a b)"), aux[:, 1, 0:256], s.st_ev)
            v.wait_ge(s.s5_tr, 1)
            cp(bT[:].rearrange("p c a b -> p c (a b)"), aux[:, 2:4, :])
            cp(cT[:].rearrange("p c a b -> p c (a b)"), aux[:, 0:2, :], s.s5_ev)
            v.wait_ge(s.mem_sq, 2)
            ts(rmem[:, 2:4], rmem[:, 0:2], 1.0 / D, EPS, ALU.mult, ALU.add)
            step(v.reciprocal(rmem[:, 2:4], rmem[:, 2:4]), s.mem_inv)
            for k in range(KT):
                v.wait_ge(s.mem_hi, k + 1)
                stt(meml[:, k, :], aux[:, k % 2, 0:NMEM], gains[:, 3, k:k + 1], memh[:, k, :].bitcast(F32),
                    ALU.mult, ALU.subtract, s.mem_lo)
            v.wait_ge(s.mem_r, 1)

            def s5_states(st):
                c, sn = tab[:, st % 2, 0, :], tab[:, st % 2, 1, :]
                vr, vi, t, hr, hi = (rot[:, i, :] for i in (0, 1, 2, 3, 4))
                bur, bui = aux[:, 0, :], aux[:, 1, :]
                v.wait_ge(s.s5_bu, st + 1)
                v.wait_ge(s.tab_rdy, st + 1)
                tt(vr, bur, c, ALU.mult)
                tt(t, bui, sn, ALU.mult)
                tt(vr, vr, t, ALU.add)
                tt(vi, bui, c, ALU.mult)
                tt(t, bur, sn, ALU.mult)
                tt(vi, vi, t, ALU.subtract)
                a_r, a_i = s5p[:, 1, st:st + 1], s5p[:, 2, st:st + 1]
                so = s5o[:, :, st, :]
                stt(so[:, 0, 0:NS], h0[:, 0, st, :], a_r, aux[:, 3, 0:NS], ALU.mult, ALU.add)
                stt(so[:, 1, 0:NS], h0[:, 1, st, :], a_r, aux[:, 3, NS:2 * NS], ALU.mult, ALU.add, s.s5_rot)
                ts(t[:, 0:NS], h0[:, 1, st, :], a_i)
                tt(so[:, 0, 0:NS], so[:, 0, 0:NS], t[:, 0:NS], ALU.subtract)
                stt(so[:, 1, 0:NS], h0[:, 0, st, :], a_i, so[:, 1, 0:NS], ALU.mult, ALU.add)
                rho = s5p[:, 0, st:st + 1].to_broadcast([P, SEQ])
                step(v.tensor_tensor_scan(vr, rho, vr, 0.0, ALU.mult, ALU.add))
                step(v.tensor_tensor_scan(vi, rho, vi, 0.0, ALU.mult, ALU.add))
                if st >= 1:
                    v.wait_ge(s.s5_c, st)
                tt(hr, vr, c, ALU.mult)
                tt(t, vi, sn, ALU.mult)
                tt(hr, hr, t, ALU.subtract)
                tt(hi, vr, sn, ALU.mult)
                tt(t, vi, c, ALU.mult)
                tt(hi, hi, t, ALU.add)
                cp(so[:, 0, NS:NS + 1], hr[:, SEQ - 1:SEQ])
                cp(so[:, 1, NS:NS + 1], hi[:, SEQ - 1:SEQ], s.s5_h)

            def s5_y(f):
                v.wait_ge(s.s5_c, 4 * f + 4)
                stt(y[:, 4 + f, 0:SEQ], u5[:, f, 0:SEQ], c4[:, 1, f:f + 1], aux[:, 2, :], ALU.mult, ALU.add)
                stt(y[:, 4 + f, SEQ:TOK], u5[:, f, SEQ:TOK], c4[:, 1, f:f + 1], aux[:, 3, 32:40],
                    ALU.mult, ALU.add, s.s5_y)

            def evict_kv(b):
                v.wait_ge(s.pe_unit, 4 * (T_KV + 2 * b) + 8)
                if b >= 2:
                    v.wait_ge(kv_out[b % 2], 16 * (b // 2))
                ts(kvst[:, b % 2, 0, :], lin[:, 2 * (b % 2), :], rmem[:, 2:3])
                ts(kvst[:, b % 2, 1, :], lin[:, 2 * (b % 2) + 1, :], rmem[:, 3:4], sm=s.tile_free)

            def soft_ask():
                ts(dtr[:], dtr[:], dtb[:, 0:1], None, ALU.add)
                stt(dte[:, 1, :], dtr[:], -1.0, dtr[:], ALU.mult, ALU.max)
                ts(dte[:, 1, :], dte[:, 1, :], -1.0, sm=s.dt_ask)

            def softplus(part):
                z, e, z2, dt = dte[:, 0, :], dte[:, 1, :], dte[:, 2, :], dte[:, 1, :]
                if part == 0:
                    v.wait_ge(s.dt_act, 2)
                    ts(z, e, 2.0, None, ALU.add)
                    step(v.reciprocal(z, z))
                if part == 1:
                    tt(z, z, e, ALU.mult)
                    tt(z2, z, z, ALU.mult)
                    ts(dt, z2, 1.0 / 17, 1.0 / 15, ALU.mult, ALU.add)
                if part >= 1:
                    for k in ((13, 11), (9, 7, 5), (3, 1))[part - 1]:
                        tt(dt, dt, z2, ALU.mult)
                        ts(dt, dt, 1.0 / k, None, ALU.add)
                if part == 3:
                    tt(dt, dt, z, ALU.mult)
                    ts(dtr[:], dtr[:], 0.0, None, ALU.max)
                    stt(dtr[:], dt, 2.0, dtr[:], ALU.mult, ALU.add)

            for n in range(4, 52):
                if n in S5_AT:
                    st = S5_AT.index(n)
                    if st > 0 and st % 4 == 0:
                        s5_y(st // 4 - 1)
                    s5_states(st)
                if n % 2 == 1:
                    evict_u(4 + n // 2)
                if n == 11:
                    soft_ask()
                if n in (20, 24, 28, 32):
                    softplus(n // 4 - 5)
            s5_y(3)
            step(v.memset(smx[:, 15:16], 0.0), s.s5_fin)

            ts(dtb[:, 2:3], dtb[:, 2:3], -1.0)
            ts(dtw[:, 1, :], dtr[:], dtb[:, 2:3])
            cp(sde[:, 0:8], dtw[:, 1, SEQ:TOK])
            one = ones[0:NH, 0:CH]
            for c in range(NC):
                w = slice(CH * c, CH * c + CH)
                step(v.tensor_tensor_scan(dtw[:, 3, w], one, dtw[:, 1, w], 0.0, ALU.mult, ALU.add),
                     s.dt_ask if c == 3 else None)
            cp(dtw[:, 2, :], dtr[:])
            for i in range(6):
                v.wait_ge(cv_in[i // 3], 48)
                x, o = xb[:, i, :], xc[:, i, :]
                step(v.memset(x[:, 0:3], 0.0))
                ts(o, x[:, 3:3 + TOK], cvw[:, i, 3:4], cvb[:, i:i + 1], ALU.mult, ALU.add)
                for r in (2, 1, 0):
                    stt(o[:, SEQ:TOK], convS[:, i, r:24:3], cvw[:, i, r:r + 1], o[:, SEQ:TOK], ALU.mult, ALU.add)
                    stt(o[:, 0:SEQ], x[:, r:r + SEQ], cvw[:, i, r:r + 1], o[:, 0:SEQ], ALU.mult, ALU.add,
                        s.cv_acc if r == 0 else None)
                if i == 1:
                    v.wait_ge(s.dt_act, 7)
                    tt(dtw[:, 5, 0:SEQ], dtw[:, 4, 0:SEQ], dtw[:, 2, 0:SEQ], ALU.mult, s.dt_done)
            def short_conv(i):
                v.wait_ge(sc_in[i % 2], 48 * (i // 2 + 1))
                c, hv, b, pr_ = (scb[:, i % 2, j, :] for j in range(4))
                step(v.memset(pr_[:, 0:2], 0.0))
                tt(pr_[:, 2:2 + TOK], c[:, 2:2 + TOK], hv[:, 0:TOK], ALU.mult)
                cp(scn[:, i, :], pr_[:, SEQ:SEQ + 10])
                o = y[:, 8 + i, :]
                ts(o[:, 0:SEQ], pr_[:, 2:2 + SEQ], scw[:, i, 2:3])
                stt(o[:, 0:SEQ], pr_[:, 1:1 + SEQ], scw[:, i, 1:2], o[:, 0:SEQ], ALU.mult, ALU.add)
                stt(o[:, 0:SEQ], pr_[:, 0:SEQ], scw[:, i, 0:1], o[:, 0:SEQ], ALU.mult, ALU.add)
                ts(o[:, SEQ:TOK], pr_[:, 2 + SEQ:2 + TOK], scw[:, i, 2:3])
                for r in (1, 0):
                    stt(o[:, SEQ:TOK], scS[:, i, r:16:2], scw[:, i, r:r + 1], o[:, SEQ:TOK], ALU.mult, ALU.add)
                tt(o, o, b[:, 0:TOK], ALU.mult, s.sc_done)

            for i in range(4):
                v.wait_ge(s.glu_sig, i + 1)
            for i in range(4):
                tt(y[:, 4 + i, :], y[:, 4 + i, :], sig[:, i, :], ALU.mult, s.glu_y if i == 3 else None)
            short_conv(0)
            short_conv(1)
            evict_kv(0)
            v.wait_ge(s.tm_tr, 1)
            src = aux[:, 0, 0:128].rearrange("p (c j h) -> p c j h", c=NC, j=4)
            for j in range(3):
                ts(tm[:, j, :, :], src[:, :, j, :], -1.0 if j == 2 else 1.0, sm=s.tm_ev if j == 2 else None)
            v.wait_ge(s.tb_tr, 1)
            cp(tb[:].rearrange("p a b -> p (a b)"), aux[:, 1, :], s.tb_ev)
            for g in range(2):
                v.wait_ge(s.sc_mm, g + 1)
                tt(smk[:, g, :, :], aux[:, 2 + g, :].rearrange("p (a b) -> p a b", a=NC),
                   causal[:].unsqueeze(1).to_broadcast([P, NC, CH]), ALU.mult, s.sm_ev)
            short_conv(2)
            short_conv(3)
            for j in range(4):
                v.wait_ge(s.ea_act, j + 1)
                cp(decs[:, j, :], gm[:, j % 2, CH - 1:SEQ:CH])
                tt(cj[:, j, :], xc[:, 5, 0:SEQ], gm[:, j % 2, :], ALU.mult, s.cj_ev)
            evict_kv(1)

            def pool_rows(i, w):
                v.wait_ge(pu_in[i % 2], 16 * (i // 2 + 1))
                u = pu[:, i % 2, :]
                step(v.memset(u[:, 0:PH], 0.0))
                a, b = pt2[:, 0, :], pt2[:, 1, :]
                n = PH + SEQ
                src, dst = u, a
                for d in range(i + 1):
                    sh, lo = 1 << d, PH - (w - (2 << d))
                    tt(dst[:, lo:n], src[:, lo:n], src[:, lo - sh:n - sh], ALU.add)
                    src, dst = dst, (b if dst is a else a)
                if i >= 2:
                    v.wait_ge(s.pl_mm, i - 1)
                o = pt[:, i % 2, :]
                stt(o[:, 0:SEQ], src[:, PH:n], 1.0 / w, u[:, PH:n], ALU.mult, ALU.subtract)
                tt(o[:, 0:16], src[:, PH:PH + 16], mks[:, 48 + 16 * i:64 + 16 * i], ALU.mult)
                tt(o[:, 0:16], o[:, 0:16], u[:, PH:PH + 16], ALU.subtract)
                tt(o[:, SEQ:TOK], plS[:, i, :], u[:, n:n + NS], ALU.add)
                stt(o[:, SEQ:TOK], o[:, SEQ:TOK], 1.0 / w, u[:, n:n + NS], ALU.mult, ALU.subtract, s.mx_pool)

            for i in range(5):
                if i < 4:
                    pool_rows(i, POOL_W[i])
                if i >= 1:
                    v.wait_ge(s.pl_mm, i)
                    ts(halves(y[:, 11 + i, :]), aux[:, 0:2, 0:HALF], c4[:, 3, i - 1:i], sm=s.pl_ev)
            step(v.memset(hst[:].rearrange("p a b -> p (a b)"), 0.0))
            evict_kv(2)

            def norm_sum(j):
                if j > 0:
                    v.wait_ge(s.stat_mm, j + 1)
                for i in range(4):
                    v.wait_ge(s.sq_done, KT + 4 * j + i + 1)
                    if i == 0:
                        cp(ssq[:], sqt[:], s.ss_done)
                    else:
                        tt(ssq[:], ssq[:], (sqt, hsq)[i % 2][:], ALU.add, s.ss_done)

            def norm_apply(j):
                v.wait_ge(s.r_ready, 2 + j)
                for i in range(4):
                    k = 4 * NORM_ORDER[j] + i
                    stt(y[:, k, :], y[:, k, :], gains[:, 1, k:k + 1], rB[:], ALU.mult, ALU.mult, s.mixn)

            def chunk_inputs(c):
                v.wait_ge(s.xt_tr, c + 1)
                xv = aux[:, 0, :].rearrange("p (h n) -> p h n", h=NH)
                if c > 0:
                    v.wait_ge(s.cs_mm, c)
                tt(xde[:].rearrange("p (h n) -> p h n", h=NH), xv,
                   tm[:, 1, c, :].unsqueeze(2).to_broadcast([P, NH, HD]), ALU.mult)
                tt(xdt[:, c, :].rearrange("p (h n) -> p h n", h=NH), xv,
                   tm[:, 0, c, :].unsqueeze(2).to_broadcast([P, NH, HD]), ALU.mult, s.xt_ev)

            norm_sum(0)
            for j in range(3):
                inverse(1 + j, GW, 2)
                if j < 2:
                    norm_sum(j + 1)
                else:
                    chunk_inputs(0)
                norm_apply(j)
            evict_kv(3)
            for c in range(NC):
                if c > 0:
                    chunk_inputs(c)
                v.wait_ge(s.cs_mm, c + 1)
                for g in range(2):
                    r, w = slice(64 * g, 64 * g + 64), slice(256 * g, 256 * g + 256)
                    o = hst[r, c + 1, w]
                    if c > 0:
                        tt(o.rearrange("p (h n) -> p h n", h=4), hst[r, c, w].rearrange("p (h n) -> p h n", h=4),
                           decs[r, :, c:c + 1].to_broadcast([64, 4, HD]), ALU.mult)
                        tt(o, o, aux[r, 1, w], ALU.add, s.h_ev if g else None)
                    else:
                        cp(o, aux[r, 1, w], s.h_ev if g else None)
            evict_kv(4)

            def g_pre(hd):
                v.wait_ge(s.ac_mm, hd + 1)
                if hd >= 2:
                    v.wait_ge(s.y_mm, hd - 1)
                for c in range(NC):
                    w = slice(CH * c, CH * c + CH)
                    ts(gm[:, hd % 2, w], aux[:, hd % 2, w], tm[:, 2, c, hd:hd + 1], 0.0, ALU.add, ALU.min,
                       s.g_pre if c == 3 else None)

            g_pre(0)
            g_pre(1)
            v.wait_ge(s.ss_in, 16 * 22)
            v.wait_ge(s.ss_s, 16 * 2)
            ts(r64[:, 0:32], r64[:, 0:32], s64[:, 1:2])
            tt(ht[:], r64[:, 0:32].unsqueeze(2).to_broadcast([P, 32, 64]),
               r64[:, 32:96].unsqueeze(1).to_broadcast([P, 32, 64]), ALU.mult)
            stt(hs[:].rearrange("p a b -> p (a b)"), hs[:].rearrange("p a b -> p (a b)"), s64[:, 0:1],
                ht[:].rearrange("p a b -> p (a b)"), ALU.mult, ALU.add)
            tt(ht[:], hs[:], r64[:, 96:160].unsqueeze(1).to_broadcast([P, 32, 64]), ALU.mult)
            step(v.tensor_reduce(y64[:], ht[:], AX.X, ALU.add), s.ss_y)

            for hd in range(NH):
                if 1 <= hd < NH - 1:
                    g_pre(hd + 1)
                v.wait_ge(s.g_exp, hd + 1)
                g_ = gm[:, hd % 2, :].rearrange("p (a b) -> p a b", a=NC)
                tt(g_, g_, smk[:, hd // 4, :, :], ALU.mult, s.g_ev)
                if hd in (2, 6):
                    evict_kv(5 if hd == 2 else 6)
                if hd % 2 == 1:
                    i = hd // 2
                    v.wait_ge(s.y_mm, hd + 1)
                    stt(y[:, i, 0:SEQ], xc[:, i, 0:SEQ], c4[:, 0, i:i + 1], aux[:, 2 + i % 2, :], ALU.mult, ALU.add, s.y_ev)
                    v.wait_ge(s.z_act, i + 1)
                    tt(y[:, i, 0:SEQ], y[:, i, 0:SEQ], zt[:, i % 2, 0:SEQ], ALU.mult)
                    cp(zs[:, i, :], zt[:, i % 2, SEQ:TOK], s.z_use)
            v.wait_ge(s.ss_yin, 16 * 8)
            for i in range(4):
                o = y[:, i, SEQ:TOK]
                stt(o, xc[:, i, SEQ:TOK], c4[:, 0, i:i + 1], o, ALU.mult, ALU.add)
                tt(o, o, zs[:, i, :], ALU.mult, s.y_fin if i == 3 else None)
            norm_sum(3)

            def mix_lo(n):
                k = OUT_ORDER[n]
                v.wait_ge(s.split_hi, KT + n + 1)
                tt(mixl[:, k, :], y[:, k, :], mixh[:, k, :].bitcast(F32), ALU.subtract, s.split_lo)

            for n in range(4):
                mix_lo(n)
            inverse(4, GW, 2)
            evict_kv(7)
            for n in range(4, 8):
                mix_lo(n)
            norm_apply(3)
            for n in range(8, KT):
                mix_lo(n)
            v.wait_ge(s.ps_tr, 1)
            for g in range(2):
                for i in (2 * g, 2 * g + 1):
                    cp(pst[:, i, :], aux[:, 0, P * i + 64 * g:P * i + 64 * g + 64], s.ps_ev if i == 3 else None)
            v.wait_ge(s.h_in, 48)

            def residual_pair(T, m, n, lo, g):
                for i in range(2):
                    v.wait_ge(s.pe_unit, 4 * T + (2 * i + 2))
                    w = bass.ds(TOK * (m + i), TOK)
                    ht = flat(h)[:, w]
                    tt(halves(ht), lin_tile(i), halves(ht), ALU.add, s.tile_free)
                    if lo is not None:
                        v.wait_ge(s.split_hi, n + (i + 1))
                        stt(flat(lo[0])[:, w], ht, gains[:, g, bass.ds(m + i, 1)], flat(lo[1])[:, w].bitcast(F32),
                            ALU.mult, ALU.subtract, s.split_lo)
                    if n is not None:
                        v.wait_ge(s.sq_done, (4 * KT if lo is None else 0) + n + (i + 1))
                        tt(ssq[:], ssq[:], sqt[:], ALU.add, s.ss_done)

            def residual(T0, n0, lo, g):
                step(v.memset(ssq[:], 0.0))
                with v.Fori(0, 8) as p:
                    step.enter(p, [(s.tile_free, 2), (s.ss_done, 2)] + ([(s.split_lo, 2)] if lo else []))
                    residual_pair(p + T0, 2 * p, 2 * p + n0, lo, g)
                    step.leave(8)

            residual(T_OUT, 2 * KT, (al, ah), 2)
            inverse(5, D, 2)

            def evict_q(t):
                v.wait_ge(s.pe_unit, 4 * T_Q + 2 * t + 2)
                if t == 0:
                    v.wait_ge(s.r_ready, 6)
                tt(halves(q[:, t, :]), lin_tile(t % 2), halves(rB[:]), ALU.mult, s.tile_free)

            def o_lo(first, last):
                for k in range(first, last):
                    v.wait_ge(s.oh_hi, k + 1)
                    tt(ol[:, k, :], q[:, k, :], oh[:, k, :].bitcast(F32), ALU.subtract, s.oh_lo)

            step(v.memset(pTd[:].rearrange("p m a b -> p (m a b)"), 0.0))
            for t in range(4):
                evict_q(t)
            for hd in range(XAH):
                last = hd == XAH - 1
                v.wait_ge(s.kt_tr, hd + 1)
                cp(kTh[:].rearrange("p (a d) m -> p a (d m)", a=2), aux[:, 0:2, :], s.kt_ev)
                for t4 in range(4):
                    n = 4 * hd + t4
                    v.wait_ge(s.sc2, n + 1)
                    sc = aux[:, 2, 0:NMEM]
                    step(v.tensor_reduce(smx[:, 0:1], sc, AX.X, ALU.max))
                    if n >= 1:
                        v.wait_ge(s.p_tr, n)
                    ts(smx[:, 1:2], smx[:, 0:1], -SCALE, sm=s.p_ask)
                    for b in (2 * t4, 2 * t4 + 1):
                        m = 8 * hd + b
                        i = 16 * hd + b
                        v.wait_ge(s.qb, m + 1)
                        v.wait_ge(pc_in[i % 4], 16 * (i // 4 + 1))
                        for mt in range(2):
                            step(v.tensor_tensor_reduce(piece[:, i % 4, mt, :], piece[:, i % 4, mt, :], aux[:, b % 2, :],
                                                        1.0, 0.0, ALU.mult, ALU.add, ssc[:, mt, b:b + 1]),
                                 s.ss_ev if mt else None)
                    v.wait_ge(s.p_exp, n + 1)
                    step(v.reciprocal(smx[:, 3:4], smx[:, 2:3]))
                    ts(pr[:], pr[:], smx[:, 3:4], sm=s.p_ev)
                    if last and t4 >= 1:
                        o_lo(3 * t4 - 3, 3 * t4)
                    v.wait_ge(s.p_tr, n + 1)
                    if n >= 4:
                        v.wait_ge(s.pv, 4 * hd)
                    cp(pT[:, :, P * t4:P * t4 + P], aux[:, 3, 0:NMEM].rearrange("p (m t) -> p m t", m=2), s.pt_ev)
                    if not last and t4 in (0, 2):
                        evict_q(4 * hd + 4 + t4 // 2)
                if last:
                    o_lo(9, 12)
                else:
                    evict_q(4 * hd + 6)
                for d in range(4):
                    k = 4 * hd + d
                    v.wait_ge(s.pv, k + 1)
                    cp(q[:, k, 0:SEQ], aux[:, d % 2, :], s.o_ev)
                    if d == 1:
                        v.wait_ge(s.sp_tr, hd + 1)
                        sc = aux[0:NS, 2, 0:NMEM]
                        step(v.tensor_reduce(smx[0:NS, 4:5], sc, AX.X, ALU.max))
                        ts(smx[0:NS, 5:6], smx[0:NS, 4:5], -SCALE, sm=s.sp_ask)
                v.wait_ge(s.sp_exp, hd + 1)
                step(v.reciprocal(smx[0:NS, 7:8], smx[0:NS, 6:7]))
                ts(prs[:], prs[:], smx[0:NS, 7:8], sm=s.sp_ev)
                v.wait_ge(s.sp_tb, hd + 1)
                cp(pTd[:].rearrange("p m a b -> p m (a b)")[:, :, 0:NS * NS:NS + 1],
                   aux[:, 3, 256:272].rearrange("p (m b) -> p m b", m=2), s.sp_tev)
                if not last:
                    evict_q(4 * hd + 7)
                v.wait_ge(s.spv, 8 * hd + 8)
                cp(po[:], aux[0:NS, 2, :], s.po_ev)
                v.wait_ge(s.so_tr, hd + 1)
                cp(q[:, 4 * hd:4 * hd + 4, SEQ:TOK], aux[:, 3, 288:320].rearrange("p (d b) -> p d b", d=4), s.so_ev)
            o_lo(12, KT)
            residual(T_O, 3 * KT, (ml, mh), 4)
            inverse(6, D, 2)
            v.wait_ge(s.r_ready, 7)

            def up_pair(T, c, p):
                for i in range(2):
                    v.wait_ge(s.pe_unit, 4 * T + (2 * i + 2))
                    n = 16 * c + 2 * p
                    stt(halves(upr[:]), lin_tile(i), 0.0, halves(rB[:]), ALU.max, ALU.mult, s.tile_free)
                    v.wait_ge(s.hid_hi, n + (i + 1))
                    w = bass.ds(TOK * (2 * p + i), TOK)
                    tt(flat(fl)[:, w], hsq[:], flat(fh)[:, w].bitcast(F32), ALU.subtract, s.hid_lo)

            per_up = [(s.tile_free, 2), (s.hid_lo, 2)]
            with v.Fori(0, N_CHUNK - 1) as c:
                step.enter(c, [(s.hid_lo, 16), (s.tile_free, 32)])
                with v.Fori(0, 8) as p:
                    step.enter(p, per_up)
                    up_pair(16 * c + p + T_MLP, c, p)
                    step.leave(8)
                with v.Fori(0, 8) as p:
                    step.enter(p, [(s.tile_free, 2)])
                    residual_pair(16 * c + p + (T_MLP + 8), 2 * p, None, None, None)
                    step.leave(8)
                step.leave(N_CHUNK - 1)
            L = N_CHUNK - 1
            with v.Fori(0, 8) as p:
                step.enter(p, per_up)
                up_pair(p + (T_MLP + 16 * L), L, p)
                step.leave(8)
            step(v.memset(ssq[:], 0.0))
            with v.Fori(0, 8) as p:
                step.enter(p, [(s.tile_free, 2), (s.ss_done, 2)])
                residual_pair(p + (T_MLP + 16 * L + 8), 2 * p, 2 * p, None, None)
                step.leave(8)
            inverse(7, D, 2)
            v.wait_ge(s.r_ready, 8)
            for k in range(KT):
                stt(h[:, k, :], h[:, k, :], gains[:, 5, k:k + 1], rB[:], ALU.mult, ALU.mult, s.f_ev)


N_PAR = 22
N_OUT = 112

_IN = {
    "x_prompt": (SEQ, D), "x_sample": (NS, D), "mem_prompt": (NMEM, D), "state_ssd_conv": (24, 768),
    "state_ssd": (NS, NH, 4096), "state_s5_re": (NS, D), "state_s5_im": (NS, D), "state_sconv": (16, GW),
    "state_pool": (NS * PH, GW), "cache_mem_k": (NS, NMEM, D), "cache_mem_v": (NS, NMEM, D),
    "norm_mix_g": (D,), "w_in": (D, IN_W), "ssd_conv_w": (4, 768), "ssd_conv_b": (768,), "ssd_dt_bias": (NH,),
    "ssd_a_log": (NH,), "ssd_d": (NH,), "s5_lam_re": (32, 64), "s5_lam_im": (32, 64), "s5_log_dt": (32,),
    "s5_b_re": (32, 64, 16), "s5_b_im": (32, 64, 16), "s5_c_re": (32, 16, 64), "s5_c_im": (32, 16, 64),
    "s5_d": (GW,), "s5_w_glu": (GW, GW), "s5_b_glu": (GW,), "sc_conv_w": (3, GW), "pool_w": (4, P, P),
    "pool_scale": (GW,), "mix_out_g": (D,), "w_out": (D, D), "norm_xa_g": (D,), "norm_mem_g": (D,),
    "w_q": (D, D), "w_k": (D, D), "w_v": (D, D), "w_o": (D, D), "norm_mlp_g": (D,), "w_up": (D, DFF),
    "w_down": (DFF, D), "final_norm_g": (D,),
}
_SHORT = {"mem_prompt": "mem", "cache_mem_k": "cache_k", "cache_mem_v": "cache_v"}
_OUT = [
    ("y_prompt", (SEQ, D), (1, SEQ, D)), ("y_sample", (NS, D), (NS, 1, D)),
    ("p_ssd_conv", (3, 768), (1, 1, 3, 768)), ("p_ssd", (512, 64), (1, 1, 8, 64, 64)),
    ("p_s5_re", (32, 64), (1, 1, 32, 64)), ("p_s5_im", (32, 64), (1, 1, 32, 64)),
    ("p_sconv", (2, GW), (1, 1, 2, GW)), ("p_pool", (PH, GW), (1, 1, PH, GW)),
    ("p_mem_k", (NMEM, D), (1, 1, NMEM, XAH, XAD)), ("p_mem_v", (NMEM, D), (1, 1, NMEM, XAH, XAD)),
    ("s_ssd_conv", (24, 768), (1, NS, 3, 768)), ("s_ssd", (NS, NH, 4096), (1, NS, 8, 64, 64)),
    ("s_s5_re", (256, 64), (1, NS, 32, 64)), ("s_s5_im", (256, 64), (1, NS, 32, 64)),
    ("s_sconv", (16, GW), (1, NS, 2, GW)), ("s_pool", (NS * PH, GW), (1, NS, PH, GW)),
]


def kernel(**inputs):
    import concourse.bacc as bacc
    from concourse.bass_utils import run_bass_kernel_spmd

    nc = bacc.Bacc("TRN2", target_bir_lowering=False, num_devices=1, dynamic_dma_scratch_size=1024)
    arrays, io = {}, {}
    for name, shape in _IN.items():
        a = np.ascontiguousarray(inputs[name]).reshape(shape)
        arrays["in_" + name] = a
        io[_SHORT.get(name, name)] = nc.dram_tensor("in_" + name, shape, mybir.dt.from_np(a.dtype), kind="ExternalInput").ap()
    arrays["consts"] = constants()
    cst = nc.dram_tensor("consts", arrays["consts"].shape, F32, kind="ExternalInput").ap()
    outs = {n: nc.dram_tensor("out_" + n, shape, F32, kind="ExternalOutput").ap() for n, shape, _ in _OUT}
    build(nc, io, cst, outs)
    r = run_bass_kernel_spmd(nc, [arrays], core_ids=[0])
    return tuple(r.results[0]["out_" + n].reshape(shape) for n, _, shape in _OUT)
```
